# Optimizing a Trainium2 kernel written in Bass

```python
import math
import jax, jax.numpy as jnp
from jax import lax
import numpy as np
import jax
import jax.numpy as jnp

D_MODEL = 1024
BATCH = 1
SEQ = 256
DEPTH = 2

N_HEADS = 16
HEAD_DIM = D_MODEL // N_HEADS
MOBA_BLOCK = 256
MOBA_TOPK = 3
Q_CHUNK = 32
ROPE_THETA = 10000.0
RWKV_HEAD = 64
RWKV_HEADS = D_MODEL // RWKV_HEAD
DECAY_LORA = 64
AAA_LORA = 64
GATE_LORA = 128
LNX_EPS = 64e-5
D_FF = ((8 * D_MODEL // 3 + 127) // 128) * 128
CONV_WIDTH = 3
N_MIXERS = 2
N_ATTN_LAYERS = (DEPTH + N_MIXERS - 1) // N_MIXERS
N_RWKV_LAYERS = DEPTH // N_MIXERS
RMS_EPS = 1e-6


def rms_norm(x, g):
    xf = x.astype(jnp.float32)
    y = xf * lax.rsqrt(jnp.mean(xf * xf, axis=-1, keepdims=True) + RMS_EPS)
    return (y * g.astype(jnp.float32)).astype(x.dtype)

def rope_tables(seq):
    inv = 1.0 / (ROPE_THETA ** (jnp.arange(0, HEAD_DIM, 2, dtype=jnp.float32) / HEAD_DIM))
    ang = jnp.arange(seq, dtype=jnp.float32)[:, None] * inv[None, :]
    ang = jnp.concatenate([ang, ang], axis=-1)
    return jnp.cos(ang), jnp.sin(ang)

def apply_rope(t, cos, sin):
    half = HEAD_DIM // 2
    rot = jnp.concatenate([-t[..., half:], t[..., :half]], axis=-1)
    return t * cos.astype(t.dtype) + rot * sin.astype(t.dtype)

def moba_attention(x, w_qkv, w_o, cos, sin):
    B, S, D = x.shape
    H, Dh = N_HEADS, HEAD_DIM
    qkv = x @ w_qkv
    q, k, v = jnp.split(qkv, 3, axis=-1)
    to_heads = lambda t: t.reshape(B, S, H, Dh).transpose(0, 2, 1, 3)
    q = apply_rope(to_heads(q), cos, sin)
    k = apply_rope(to_heads(k), cos, sin)
    v = to_heads(v)
    scale = 1.0 / math.sqrt(Dh)

    nb = -(-S // MOBA_BLOCK)
    pad = nb * MOBA_BLOCK - S
    kb = jnp.pad(k, ((0, 0), (0, 0), (0, pad), (0, 0))).reshape(B, H, nb, MOBA_BLOCK, Dh)
    vb = jnp.pad(v, ((0, 0), (0, 0), (0, pad), (0, 0))).reshape(B, H, nb, MOBA_BLOCK, Dh)

    kmean = jnp.mean(kb.astype(jnp.float32), axis=3)
    gate = jnp.einsum('bhsd,bhnd->bhsn', q.astype(jnp.float32), kmean)
    qblk = jnp.arange(S) // MOBA_BLOCK
    past = jnp.arange(nb)[None, :] < qblk[:, None]
    gate = jnp.where(past, gate, -jnp.inf)
    k_sel = min(MOBA_TOPK, nb)
    _, gidx = lax.top_k(gate, k_sel)
    gvalid = gidx < qblk[:, None]

    bi = jnp.arange(B)[:, None, None, None]
    hi = jnp.arange(H)[None, :, None, None]

    def chunk(c):
        s0 = c * Q_CHUNK
        qc = lax.dynamic_slice_in_dim(q, s0, Q_CHUNK, axis=2)
        idc = lax.dynamic_slice_in_dim(gidx, s0, Q_CHUNK, axis=2)
        vdc = lax.dynamic_slice_in_dim(gvalid, s0, Q_CHUNK, axis=2)
        kg = kb[bi, hi, idc]
        vg = vb[bi, hi, idc]
        s_sel = jnp.einsum('bhqd,bhqjtd->bhqjt', qc, kg) * scale
        s_sel = jnp.where(vdc[..., None], s_sel, -jnp.inf)
        s_sel = s_sel.reshape(B, H, Q_CHUNK, k_sel * MOBA_BLOCK)
        own = s0 // MOBA_BLOCK
        ko = lax.dynamic_index_in_dim(kb, own, axis=2, keepdims=False)
        vo = lax.dynamic_index_in_dim(vb, own, axis=2, keepdims=False)
        s_own = jnp.einsum('bhqd,bhtd->bhqt', qc, ko) * scale
        qpos = s0 + jnp.arange(Q_CHUNK)
        kpos = own * MOBA_BLOCK + jnp.arange(MOBA_BLOCK)
        s_own = jnp.where(kpos[None, :] <= qpos[:, None], s_own, -jnp.inf)
        s_all = jnp.concatenate([s_sel, s_own], axis=-1).astype(jnp.float32)
        p = jax.nn.softmax(s_all, axis=-1).astype(v.dtype)
        p_sel = p[..., :k_sel * MOBA_BLOCK].reshape(B, H, Q_CHUNK, k_sel, MOBA_BLOCK)
        p_own = p[..., k_sel * MOBA_BLOCK:]
        return (jnp.einsum('bhqjt,bhqjtd->bhqd', p_sel, vg)
                + jnp.einsum('bhqt,bhtd->bhqd', p_own, vo))

    out = lax.map(chunk, jnp.arange(S // Q_CHUNK))
    out = out.transpose(1, 0, 3, 2, 4).reshape(B, S, D)
    return out @ w_o

def rwkv7_time_mix(x, mu, w_rkv, w0, w1, w2, a0, a1, a2, g1, g2, k_k, k_a, r_k,
                   lnx_w, lnx_b, w_o):
    B, S, D = x.shape
    H, N = RWKV_HEADS, RWKV_HEAD
    f32 = jnp.float32
    x_prev = jnp.pad(x[:, :-1], ((0, 0), (1, 0), (0, 0)))
    xx = x_prev - x
    xr, xw, xk, xv, xa, xg = [x + xx * mu[n] for n in range(6)]
    rkv = jnp.einsum('nbsd,nde->nbse', jnp.stack([xr, xk, xv]), w_rkv)
    r, k, v = rkv[0], rkv[1], rkv[2]
    w = -jax.nn.softplus(-(w0 + jnp.tanh(xw @ w1) @ w2).astype(f32)) - 0.5
    decay = jnp.exp(-jnp.exp(w))
    a = jax.nn.sigmoid((a0 + (xa @ a1) @ a2).astype(f32))
    g = jax.nn.sigmoid(xg @ g1) @ g2

    heads = lambda t: t.astype(f32).reshape(B, S, H, N)
    r, k, v, decay, a = heads(r), heads(k), heads(v), heads(decay), heads(a)
    kk = k * k_k.astype(f32).reshape(H, N)
    kk = kk / jnp.maximum(jnp.sqrt(jnp.sum(kk * kk, axis=-1, keepdims=True)), 1e-12)
    k = k * (1.0 + (a - 1.0) * k_a.astype(f32).reshape(H, N))

    def step(state, inp):
        r_t, w_t, k_t, v_t, kk_t, a_t = inp
        sa = jnp.einsum('bhvk,bhk->bhv', state, -kk_t)
        state = (state * w_t[:, :, None, :]
                 + sa[..., None] * (kk_t * a_t)[:, :, None, :]
                 + v_t[..., None] * k_t[:, :, None, :])
        y = jnp.einsum('bhvk,bhk->bhv', state, r_t)
        return state, y

    tm = lambda t: jnp.swapaxes(t, 0, 1)
    _, y = lax.scan(step, jnp.zeros((B, H, N, N), f32),
                    (tm(r), tm(decay), tm(k), tm(v), tm(kk), tm(a)))
    y = jnp.swapaxes(y, 0, 1)
    mean = jnp.mean(y, axis=-1, keepdims=True)
    var = jnp.mean(jnp.square(y - mean), axis=-1, keepdims=True)
    yn = ((y - mean) * lax.rsqrt(var + LNX_EPS)).reshape(B, S, D)
    yn = yn * lnx_w.astype(f32) + lnx_b.astype(f32)
    bonus = (jnp.sum(r * k * r_k.astype(f32), axis=-1, keepdims=True) * v).reshape(B, S, D)
    return ((yn + bonus).astype(x.dtype) * g) @ w_o

def conv_ffn(x, w_gate, w_up, conv_w, conv_b, w_down):
    gt = x @ w_gate
    gt = lax.conv_general_dilated(
        gt, conv_w[:, None, :].astype(gt.dtype), window_strides=(1,),
        padding=[(CONV_WIDTH - 1, 0)], dimension_numbers=('NWC', 'WIO', 'NWC'),
        feature_group_count=gt.shape[-1]) + conv_b
    return (jax.nn.silu(gt) * (x @ w_up)) @ w_down

def first_inputs(seed: int = 0) -> dict:
    key = jax.random.key(seed)
    ks = iter(jax.random.split(key, 40))
    nrm = lambda shape, s: jax.random.normal(next(ks), shape, jnp.float32) * s
    D, F, H, N = D_MODEL, D_FF, RWKV_HEADS, RWKV_HEAD
    NA, NR = N_ATTN_LAYERS, N_RWKV_LAYERS
    return {
        'x': nrm((BATCH, SEQ, D), 1.0),
        'norm_mix': 1.0 + nrm((DEPTH, D), 0.02),
        'norm_ffn': 1.0 + nrm((DEPTH, D), 0.02),
        'norm_final': 1.0 + nrm((D,), 0.02),
        'attn_w_qkv': nrm((NA, D, 3 * D), D ** -0.5),
        'attn_w_o': nrm((NA, D, D), D ** -0.5),
        'rwkv_mu': jax.random.uniform(next(ks), (NR, 6, D), jnp.float32),
        'rwkv_w_rkv': nrm((NR, 3, D, D), D ** -0.5),
        'rwkv_w0': -1.0 + nrm((NR, D), 0.5),
        'rwkv_w1': nrm((NR, D, DECAY_LORA), D ** -0.5),
        'rwkv_w2': nrm((NR, DECAY_LORA, D), 0.5 * DECAY_LORA ** -0.5),
        'rwkv_a0': nrm((NR, D), 0.1),
        'rwkv_a1': nrm((NR, D, AAA_LORA), D ** -0.5),
        'rwkv_a2': nrm((NR, AAA_LORA, D), 0.5 * AAA_LORA ** -0.5),
        'rwkv_g1': nrm((NR, D, GATE_LORA), D ** -0.5),
        'rwkv_g2': nrm((NR, GATE_LORA, D), GATE_LORA ** -0.5),
        'rwkv_k_k': 0.85 + nrm((NR, D), 0.05),
        'rwkv_k_a': 1.0 + nrm((NR, D), 0.05),
        'rwkv_r_k': nrm((NR, H, N), 0.1),
        'rwkv_lnx_w': 1.0 + nrm((NR, D), 0.02),
        'rwkv_lnx_b': nrm((NR, D), 0.02),
        'rwkv_w_o': nrm((NR, D, D), D ** -0.5),
        'ffn_w_gate': nrm((DEPTH, D, F), D ** -0.5),
        'ffn_w_up': nrm((DEPTH, D, F), D ** -0.5),
        'ffn_conv_w': nrm((DEPTH, CONV_WIDTH, F), CONV_WIDTH ** -0.5),
        'ffn_conv_b': nrm((DEPTH, F), 0.02),
        'ffn_w_down': nrm((DEPTH, F, D), F ** -0.5),
    }

def first_block(x, norm_mix, norm_ffn, norm_final, attn_w_qkv, attn_w_o,
              rwkv_mu, rwkv_w_rkv, rwkv_w0, rwkv_w1, rwkv_w2, rwkv_a0, rwkv_a1,
              rwkv_a2, rwkv_g1, rwkv_g2, rwkv_k_k, rwkv_k_a, rwkv_r_k,
              rwkv_lnx_w, rwkv_lnx_b, rwkv_w_o,
              ffn_w_gate, ffn_w_up, ffn_conv_w, ffn_conv_b, ffn_w_down):
    S = x.shape[1]
    cos, sin = rope_tables(S)
    h = x
    for i in range(DEPTH):
        xn = rms_norm(h, norm_mix[i])
        j = i // N_MIXERS
        if i % N_MIXERS == 0:
            h = h + moba_attention(xn, attn_w_qkv[j], attn_w_o[j], cos, sin)
        else:
            h = h + rwkv7_time_mix(
                xn, rwkv_mu[j], rwkv_w_rkv[j], rwkv_w0[j], rwkv_w1[j], rwkv_w2[j],
                rwkv_a0[j], rwkv_a1[j], rwkv_a2[j], rwkv_g1[j], rwkv_g2[j],
                rwkv_k_k[j], rwkv_k_a[j], rwkv_r_k[j], rwkv_lnx_w[j], rwkv_lnx_b[j],
                rwkv_w_o[j])
        h = h + conv_ffn(rms_norm(h, norm_ffn[i]), ffn_w_gate[i], ffn_w_up[i],
                         ffn_conv_w[i], ffn_conv_b[i], ffn_w_down[i])
    return rms_norm(h, norm_final)


_first_inputs = first_inputs


def first_inputs(seed=0):
    import zlib

    import numpy as np

    out = dict(_first_inputs(seed))
    spreads = {}
    factors = {'norm_mix': 2.684,
     'norm_final': 9.023,
     'rwkv_k_k': 37.85,
     'rwkv_lnx_w': 25.426,
     'rwkv_lnx_b': 25.843,
     'ffn_conv_b': 3.569,
     'norm_ffn': 4.052}
    for name, (base, spread) in spreads.items():
        noise = np.random.default_rng([zlib.crc32(name.encode()), seed]).standard_normal(out[name].shape)
        drawn = base * np.exp(spread * noise) if base else spread * noise
        out[name] = __import__('jax').numpy.asarray(drawn.astype(out[name].dtype))
    for name, factor in factors.items():
        out[name] = (out[name] * factor).astype(out[name].dtype)
    return out


_narrow_inputs = first_inputs


def first_inputs(seed=0):

    out = dict(_narrow_inputs(seed))
    wider = {'norm_final': 3.38, 'rwkv_k_k': 4.82, 'rwkv_lnx_w': 3.63, 'rwkv_lnx_b': 3.68}
    for name, times in wider.items():
        mean = out[name].mean()
        out[name] = (mean + times * (out[name] - mean)).astype(out[name].dtype)
    return out


CHUNK = 64
Q_BLOCK = 128
MEM_LEN = 256
ROPE_THETA_2 = 500000.0
LN_EPS = 1e-5
DEEPNORM_ALPHA = (2.0 * DEPTH) ** 0.25
DEEPNORM_BETA = (8.0 * DEPTH) ** -0.25

DIFF_HEADS = 8
DIFF_HEAD_DIM = 64
DIFF_ROPE_DIM = DIFF_HEAD_DIM // 4

MLA_HEADS = 8
MLA_Q_RANK = 256
MLA_KV_RANK = 256
MLA_ROPE_DIM = 32
MLA_NOPE_DIM = 96
MLA_V_DIM = 128
IDX_HEADS = 16
IDX_DIM = 64
IDX_ROPE_DIM = IDX_DIM // 4
IDX_TOPK_MAX = 256

MEM_HEADS = 4
MEM_HEAD_DIM = D_MODEL // MEM_HEADS

N_GROUPS = 4
EXPERTS_PER_GROUP = 4
N_EXPERTS = N_GROUPS * EXPERTS_PER_GROUP
EXPERT_TOP_K = 2
EXPERT_FF = 512

N_DIFF_LAYERS = (DEPTH + 1) // 2
N_DSA_LAYERS = DEPTH // 2


def layer_norm(x, g, b):
    xf = x.astype(jnp.float32)
    mu = jnp.mean(xf, axis=-1, keepdims=True)
    xc = xf - mu
    var = jnp.mean(xc * xc, axis=-1, keepdims=True)
    y = xc * lax.rsqrt(var + LN_EPS) * g.astype(jnp.float32) + b.astype(jnp.float32)
    return y.astype(x.dtype)

def rms_norm_2(x, g):
    xf = x.astype(jnp.float32)
    y = xf * lax.rsqrt(jnp.mean(xf * xf, axis=-1, keepdims=True) + LN_EPS) * g.astype(jnp.float32)
    return y.astype(x.dtype)

def rope_tables_2(positions, rot_dim):
    inv_freq = ROPE_THETA_2 ** (-jnp.arange(0, rot_dim, 2, dtype=jnp.float32) / rot_dim)
    ang = positions.astype(jnp.float32)[..., None] * inv_freq
    return jnp.cos(ang), jnp.sin(ang)

def apply_partial_rope(x, cos, sin):
    half = cos.shape[-1]
    c = cos[:, :, None, :].astype(x.dtype)
    s = sin[:, :, None, :].astype(x.dtype)
    x1 = x[..., :half]
    x2 = x[..., half:2 * half]
    return jnp.concatenate([x1 * c - x2 * s, x2 * c + x1 * s, x[..., 2 * half:]], axis=-1)

def to_blocks(a, blk):
    b, s = a.shape[0], a.shape[1]
    return jnp.moveaxis(a.reshape((b, s // blk, blk) + a.shape[2:]), 1, 0)

def from_blocks(a):
    nb, b, blk = a.shape[0], a.shape[1], a.shape[2]
    return jnp.moveaxis(a, 0, 1).reshape((b, nb * blk) + a.shape[3:])

def diff_lambda_init(layer_idx):
    return 0.8 - 0.6 * math.exp(-0.3 * layer_idx)

def differential_attention(x, cos, sin, w_in, lam, subln_g, w_out, lambda_init):
    bsz, seq, _ = x.shape
    h, d = DIFF_HEADS, DIFF_HEAD_DIM
    q, k, v = jnp.split(x @ w_in, 3, axis=-1)
    q = apply_partial_rope(q.reshape(bsz, seq, 2 * h, d), cos, sin) * (d ** -0.5)
    k = apply_partial_rope(k.reshape(bsz, seq, 2 * h, d), cos, sin)
    q = q.reshape(bsz, seq, h, 2, d)
    k = k.reshape(bsz, seq, h, 2, d)
    v = v.reshape(bsz, seq, h, 2 * d)
    lamf = lam.astype(jnp.float32)
    lam_full = jnp.exp(jnp.sum(lamf[0] * lamf[1])) - jnp.exp(jnp.sum(lamf[2] * lamf[3])) + lambda_init
    key_chunk = jnp.arange(seq) // CHUNK

    def block(args):
        q_blk, blk_idx = args
        q_chunk = (blk_idx * Q_BLOCK + jnp.arange(Q_BLOCK)) // CHUNK
        allowed = key_chunk[None, :] <= q_chunk[:, None]
        s = jnp.einsum('bqhcd,bkhcd->bhcqk', q_blk, k).astype(jnp.float32)
        p = jax.nn.softmax(jnp.where(allowed, s, -jnp.inf), axis=-1)
        p_diff = p[:, :, 0] - lam_full * p[:, :, 1]
        return jnp.einsum('bhqk,bkhe->bqhe', p_diff.astype(v.dtype), v)

    o = from_blocks(lax.map(block, (to_blocks(q, Q_BLOCK), jnp.arange(seq // Q_BLOCK))))
    o = rms_norm_2(o, subln_g) * (1.0 - lambda_init)
    return o.reshape(bsz, seq, h * 2 * d) @ w_out

def dsa_sparse_mla(x, cos_r, sin_r, cos_i, sin_i, w_in, q_norm_g, kv_norm_g, w_uq, w_qidx, w_uk, w_uv, w_out):
    bsz, seq, _ = x.shape
    h = MLA_HEADS
    splits = [MLA_Q_RANK,
              MLA_Q_RANK + MLA_KV_RANK,
              MLA_Q_RANK + MLA_KV_RANK + MLA_ROPE_DIM,
              MLA_Q_RANK + MLA_KV_RANK + MLA_ROPE_DIM + IDX_DIM]
    c_q, c_kv, k_rope, k_idx, w_idx = jnp.split(x @ w_in, splits, axis=-1)
    c_q = rms_norm_2(c_q, q_norm_g)
    c_kv = rms_norm_2(c_kv, kv_norm_g)
    q = (c_q @ w_uq).reshape(bsz, seq, h, MLA_ROPE_DIM + MLA_NOPE_DIM)
    q_rope = apply_partial_rope(q[..., :MLA_ROPE_DIM], cos_r, sin_r)
    q_lat = jnp.einsum('bshn,hrn->bshr', q[..., MLA_ROPE_DIM:], w_uk)
    q_full = jnp.concatenate([q_lat, q_rope], axis=-1) * ((MLA_ROPE_DIM + MLA_NOPE_DIM) ** -0.5)
    k_rope = apply_partial_rope(k_rope[:, :, None, :], cos_r, sin_r)[:, :, 0]
    kv_lat = jnp.concatenate([c_kv, k_rope], axis=-1)
    q_idx = apply_partial_rope((c_q @ w_qidx).reshape(bsz, seq, IDX_HEADS, IDX_DIM), cos_i, sin_i)
    k_idx = apply_partial_rope(k_idx[:, :, None, :], cos_i, sin_i)[:, :, 0]
    w_idx = w_idx * ((IDX_HEADS * IDX_DIM) ** -0.5)
    top_k = min(IDX_TOPK_MAX, seq // 4)
    key_chunk = jnp.arange(seq) // CHUNK
    gather = jax.vmap(lambda table, idx: table[idx])

    def block(args):
        qf, qi, wi, chunk_idx = args
        logits = jnp.einsum('bqhd,bkd->bqhk', qi, k_idx)
        score = jnp.einsum('bqh,bqhk->bqk', wi, jax.nn.relu(logits)).astype(jnp.float32)
        score = jnp.where((key_chunk <= chunk_idx)[None, None, :], score, -jnp.inf)
        top_score, top_idx = lax.top_k(score, top_k)
        valid = jnp.isfinite(top_score)
        sel = gather(kv_lat, top_idx)
        s = jnp.einsum('bqhd,bqkd->bhqk', qf, sel).astype(jnp.float32)
        p = jax.nn.softmax(jnp.where(valid[:, None], s, -jnp.inf), axis=-1)
        return jnp.einsum('bhqk,bqkr->bqhr', p.astype(sel.dtype), sel[..., :MLA_KV_RANK])

    o_lat = from_blocks(lax.map(block, (to_blocks(q_full, CHUNK), to_blocks(q_idx, CHUNK),
                                        to_blocks(w_idx, CHUNK), jnp.arange(seq // CHUNK))))
    o = jnp.einsum('bshr,hrv->bshv', o_lat, w_uv).reshape(bsz, seq, h * MLA_V_DIM)
    return o @ w_out

def memory_cross_attention(x, mem_k, mem_v, w_q, w_out):
    bsz, seq, _ = x.shape
    q = (x @ w_q).reshape(bsz, seq, MEM_HEADS, MEM_HEAD_DIM) * (MEM_HEAD_DIM ** -0.5)
    s = jnp.einsum('bshd,bmhd->bhsm', q, mem_k).astype(jnp.float32)
    p = jax.nn.softmax(s, axis=-1)
    o = jnp.einsum('bhsm,bmhd->bshd', p.astype(mem_v.dtype), mem_v).reshape(bsz, seq, MEM_HEADS * MEM_HEAD_DIM)
    return o @ w_out

def hierarchical_moe(x, w_group, b_group, w_expert, b_expert, w_gate, w_up, w_down):
    bsz, seq, dm = x.shape
    n_tok = bsz * seq
    t = x.reshape(n_tok, dm)
    g_logits = (t @ w_group + b_group).astype(jnp.float32)
    g_sel = jnp.argmax(g_logits, axis=-1)
    g_gate = jnp.max(jax.nn.softmax(g_logits, axis=-1), axis=-1, keepdims=True)
    e_logits = (t @ w_expert + b_expert).astype(jnp.float32).reshape(n_tok, N_GROUPS, EXPERTS_PER_GROUP)
    e_logits = e_logits[jnp.arange(n_tok), g_sel]
    top_val, top_idx = lax.top_k(e_logits, EXPERT_TOP_K)
    top_w = jax.nn.softmax(top_val, axis=-1) * g_gate
    expert_id = g_sel[:, None] * EXPERTS_PER_GROUP + top_idx
    combine = jnp.sum(jax.nn.one_hot(expert_id, N_EXPERTS, dtype=jnp.float32) * top_w[..., None], axis=1).astype(t.dtype)
    y = jnp.zeros_like(t)
    for e in range(N_EXPERTS):
        hid = jax.nn.silu(t @ w_gate[e]) * (t @ w_up[e])
        y = y + combine[:, e:e + 1] * (hid @ w_down[e])
    return y.reshape(bsz, seq, dm)

def second_inputs(seed: int = 0) -> dict:
    key = jax.random.key(seed)
    ks = iter(jax.random.split(key, 40))
    beta = DEEPNORM_BETA
    d = D_MODEL

    def nrm(shape, scale):
        return jax.random.normal(next(ks), shape, jnp.float32) * scale

    x = nrm((BATCH, SEQ, d), 1.0)
    mem = nrm((BATCH, MEM_LEN, d), 1.0)
    offsets = jax.random.randint(next(ks), (BATCH, 1), 0, 1024) * CHUNK
    positions = (offsets + jnp.arange(SEQ)[None, :]).astype(jnp.int32)

    diff_w = DIFF_HEADS * 2 * DIFF_HEAD_DIM
    a_w_in = jnp.concatenate([nrm((N_DIFF_LAYERS, d, 2 * diff_w), d ** -0.5),
                              nrm((N_DIFF_LAYERS, d, diff_w), beta * d ** -0.5)], axis=-1)
    a_lambda = nrm((N_DIFF_LAYERS, 4, DIFF_HEAD_DIM), 0.1)
    a_subln_g = 1.0 + nrm((N_DIFF_LAYERS, 2 * DIFF_HEAD_DIM), 0.02)
    a_w_out = nrm((N_DIFF_LAYERS, diff_w, d), beta * diff_w ** -0.5)

    b_in_w = MLA_Q_RANK + MLA_KV_RANK + MLA_ROPE_DIM + IDX_DIM + IDX_HEADS
    b_w_in = nrm((N_DSA_LAYERS, d, b_in_w), d ** -0.5)
    b_q_norm_g = 1.0 + nrm((N_DSA_LAYERS, MLA_Q_RANK), 0.02)
    b_kv_norm_g = 1.0 + nrm((N_DSA_LAYERS, MLA_KV_RANK), 0.02)
    b_w_uq = nrm((N_DSA_LAYERS, MLA_Q_RANK, MLA_HEADS * (MLA_ROPE_DIM + MLA_NOPE_DIM)), MLA_Q_RANK ** -0.5)
    b_w_qidx = nrm((N_DSA_LAYERS, MLA_Q_RANK, IDX_HEADS * IDX_DIM), MLA_Q_RANK ** -0.5)
    b_w_uk = nrm((N_DSA_LAYERS, MLA_HEADS, MLA_KV_RANK, MLA_NOPE_DIM), MLA_KV_RANK ** -0.5)
    b_w_uv = nrm((N_DSA_LAYERS, MLA_HEADS, MLA_KV_RANK, MLA_V_DIM), beta * MLA_KV_RANK ** -0.5)
    b_w_out = nrm((N_DSA_LAYERS, MLA_HEADS * MLA_V_DIM, d), beta * (MLA_HEADS * MLA_V_DIM) ** -0.5)

    mem_w = MEM_HEADS * MEM_HEAD_DIM
    mem_w_kv = jnp.concatenate([nrm((d, mem_w), d ** -0.5), nrm((d, mem_w), beta * d ** -0.5)], axis=-1)
    xa_w_q = nrm((DEPTH, d, mem_w), d ** -0.5)
    xa_w_out = nrm((DEPTH, mem_w, d), beta * mem_w ** -0.5)

    moe_w_group = nrm((DEPTH, d, N_GROUPS), d ** -0.5)
    moe_b_group = nrm((DEPTH, N_GROUPS), 0.01)
    moe_w_expert = nrm((DEPTH, d, N_EXPERTS), d ** -0.5)
    moe_b_expert = nrm((DEPTH, N_EXPERTS), 0.01)
    moe_w_gate = nrm((DEPTH, N_EXPERTS, d, EXPERT_FF), d ** -0.5)
    moe_w_up = nrm((DEPTH, N_EXPERTS, d, EXPERT_FF), beta * d ** -0.5)
    moe_w_down = nrm((DEPTH, N_EXPERTS, EXPERT_FF, d), beta * EXPERT_FF ** -0.5)

    ln_g = 1.0 + nrm((DEPTH, 3, d), 0.02)
    ln_b = nrm((DEPTH, 3, d), 0.02)

    return {"x": x, "mem": mem, "positions": positions,
            "a_w_in": a_w_in, "a_lambda": a_lambda, "a_subln_g": a_subln_g, "a_w_out": a_w_out,
            "b_w_in": b_w_in, "b_q_norm_g": b_q_norm_g, "b_kv_norm_g": b_kv_norm_g,
            "b_w_uq": b_w_uq, "b_w_qidx": b_w_qidx, "b_w_uk": b_w_uk, "b_w_uv": b_w_uv, "b_w_out": b_w_out,
            "mem_w_kv": mem_w_kv, "xa_w_q": xa_w_q, "xa_w_out": xa_w_out,
            "moe_w_group": moe_w_group, "moe_b_group": moe_b_group,
            "moe_w_expert": moe_w_expert, "moe_b_expert": moe_b_expert,
            "moe_w_gate": moe_w_gate, "moe_w_up": moe_w_up, "moe_w_down": moe_w_down,
            "ln_g": ln_g, "ln_b": ln_b}

def second_block(x, mem, positions, a_w_in, a_lambda, a_subln_g, a_w_out,
              b_w_in, b_q_norm_g, b_kv_norm_g, b_w_uq, b_w_qidx, b_w_uk, b_w_uv, b_w_out,
              mem_w_kv, xa_w_q, xa_w_out,
              moe_w_group, moe_b_group, moe_w_expert, moe_b_expert, moe_w_gate, moe_w_up, moe_w_down,
              ln_g, ln_b):
    bsz = x.shape[0]
    n_mem = mem.shape[1]
    cos_d, sin_d = rope_tables_2(positions, DIFF_ROPE_DIM)
    cos_r, sin_r = rope_tables_2(positions, MLA_ROPE_DIM)
    cos_i, sin_i = rope_tables_2(positions, IDX_ROPE_DIM)
    mem_k, mem_v = jnp.split(mem @ mem_w_kv, 2, axis=-1)
    mem_k = mem_k.reshape(bsz, n_mem, MEM_HEADS, MEM_HEAD_DIM)
    mem_v = mem_v.reshape(bsz, n_mem, MEM_HEADS, MEM_HEAD_DIM)
    alpha = DEEPNORM_ALPHA
    h = x
    for i in range(DEPTH):
        j = i // N_MIXERS
        if i % N_MIXERS == 0:
            mix = differential_attention(h, cos_d, sin_d, a_w_in[j], a_lambda[j], a_subln_g[j], a_w_out[j],
                                         diff_lambda_init(i))
        else:
            mix = dsa_sparse_mla(h, cos_r, sin_r, cos_i, sin_i, b_w_in[j], b_q_norm_g[j], b_kv_norm_g[j],
                                 b_w_uq[j], b_w_qidx[j], b_w_uk[j], b_w_uv[j], b_w_out[j])
        h = layer_norm(alpha * h + mix, ln_g[i, 0], ln_b[i, 0])
        h = layer_norm(alpha * h + memory_cross_attention(h, mem_k, mem_v, xa_w_q[i], xa_w_out[i]),
                       ln_g[i, 1], ln_b[i, 1])
        h = layer_norm(alpha * h + hierarchical_moe(h, moe_w_group[i], moe_b_group[i], moe_w_expert[i],
                                                    moe_b_expert[i], moe_w_gate[i], moe_w_up[i], moe_w_down[i]),
                       ln_g[i, 2], ln_b[i, 2])
    return h


def setup_inputs(seed=0):
    out = dict(first_inputs(seed))
    for name, value in second_inputs(seed + 1).items():
        if name != "x":
            out[name + "_2"] = value
    return out


def reference(
    x, norm_mix, norm_ffn, norm_final, attn_w_qkv, attn_w_o, rwkv_mu, rwkv_w_rkv, rwkv_w0,
    rwkv_w1, rwkv_w2, rwkv_a0, rwkv_a1, rwkv_a2, rwkv_g1, rwkv_g2, rwkv_k_k, rwkv_k_a, rwkv_r_k,
    rwkv_lnx_w, rwkv_lnx_b, rwkv_w_o, ffn_w_gate, ffn_w_up, ffn_conv_w, ffn_conv_b, ffn_w_down,
    mem_2, positions_2, a_w_in_2, a_lambda_2, a_subln_g_2, a_w_out_2, b_w_in_2, b_q_norm_g_2,
    b_kv_norm_g_2, b_w_uq_2, b_w_qidx_2, b_w_uk_2, b_w_uv_2, b_w_out_2, mem_w_kv_2, xa_w_q_2,
    xa_w_out_2, moe_w_group_2, moe_b_group_2, moe_w_expert_2, moe_b_expert_2, moe_w_gate_2,
    moe_w_up_2, moe_w_down_2, ln_g_2, ln_b_2,
):
    x = first_block(
        x, norm_mix, norm_ffn, norm_final, attn_w_qkv, attn_w_o, rwkv_mu, rwkv_w_rkv, rwkv_w0,
        rwkv_w1, rwkv_w2, rwkv_a0, rwkv_a1, rwkv_a2, rwkv_g1, rwkv_g2, rwkv_k_k, rwkv_k_a,
        rwkv_r_k, rwkv_lnx_w, rwkv_lnx_b, rwkv_w_o, ffn_w_gate, ffn_w_up, ffn_conv_w,
        ffn_conv_b, ffn_w_down,
    )
    return second_block(
        x, mem_2, positions_2, a_w_in_2, a_lambda_2, a_subln_g_2, a_w_out_2, b_w_in_2,
        b_q_norm_g_2, b_kv_norm_g_2, b_w_uq_2, b_w_qidx_2, b_w_uk_2, b_w_uv_2, b_w_out_2,
        mem_w_kv_2, xa_w_q_2, xa_w_out_2, moe_w_group_2, moe_b_group_2, moe_w_expert_2,
        moe_b_expert_2, moe_w_gate_2, moe_w_up_2, moe_w_down_2, ln_g_2, ln_b_2,
    )


_drawn_inputs = setup_inputs


def setup_inputs(seed=0):
    import zlib

    import numpy as np

    out = dict(_drawn_inputs(seed))
    spreads = {}
    factors = {'a_lambda_2': 8.0,
     'a_subln_g_2': 8.0,
     'b_q_norm_g_2': 8.0,
     'b_kv_norm_g_2': 8.0,
     'moe_b_group_2': 8.0,
     'moe_b_expert_2': 8.0}
    for name, (base, spread) in spreads.items():
        noise = np.random.default_rng([zlib.crc32(name.encode()), seed]).standard_normal(out[name].shape)
        drawn = base * np.exp(spread * noise) if base else spread * noise
        out[name] = jnp.asarray(drawn.astype(out[name].dtype))
    for name, factor in factors.items():
        out[name] = (out[name] * factor).astype(out[name].dtype)
    return out
```

```python
import math
from contextlib import ExitStack

import numpy as np
import concourse.bass as bass
from concourse import mybir

F32 = mybir.dt.float32
I32 = mybir.dt.int32
ALU = mybir.AluOpType
ACT = mybir.ActivationFunctionType
AX = mybir.AxisListType.X

P = 128
SEQ = 256
D = 1024
T = SEQ // P
KD = D // P
COLS = 512
F_FF = ((8 * D // 3 + 127) // 128) * 128
FT = F_FF // P
FU = FT // 2
N_EXPERTS, N_GROUPS, PER_GROUP, EXPERT_FF = 16, 4, 4, 512
EU = N_EXPERTS * EXPERT_FF // (2 * P)
UNIT = 2 * KD * 2 * P + 2 * D
SLOTS = 4
CHUNK = 64
NCH = SEQ // CHUNK
HEADS, HD = 16, 64
ALPHA = 4.0 ** 0.25
LN_EPS, RMS_EPS, LNX_EPS = 1e-5, 1e-6, 64e-5
DECAY = -math.exp(-0.5)
LAMBDA_INIT = 0.8 - 0.6 * math.exp(-0.3 * 0)
MASKED = -1e30
TAKEN = -3e38
TOPK = min(256, SEQ // 4)
Q_RANK, KV_RANK, MLA_ROPE, MLA_NOPE, IDX_DIM, IDX_HEADS = 256, 256, 32, 96, 64, 16
B_IN = Q_RANK + KV_RANK + MLA_ROPE + IDX_DIM + IDX_HEADS
DIFF_ROPE = 16
ROUTE = N_GROUPS + N_EXPERTS
BLK = 2048

_COLS = [("norm_mix", 2 * KD), ("norm_ffn", 2 * KD), ("mu", 6 * KD), ("w0", KD), ("a0", KD), ("k_k", KD),
         ("k_a", KD), ("r_k", KD), ("conv_w", 2 * 3 * FT), ("conv_b", 2 * FT), ("subln", 1),
         ("q_norm", 2), ("kv_norm", 2), ("route", 2 * KD * ROUTE)]
COL, _at = {}, 0
for _n, _w in _COLS:
    COL[_n] = _at
    _at += _w
N_COLS = _at


class Signal:

    def __init__(self, sem):
        self.sem, self.base, self.count = sem, 0, 0

    def up(self, step=1, runs=1):
        self.count += step * runs
        return self.sem

    def at(self, n):
        return self.base + n


def build_program(nc, d, out):
    with ExitStack() as ctx:
        def sb(name, shape, dt=F32):
            return ctx.enter_context(nc.sbuf_tensor(name, shape, dt))

        ring = sb("ring", [P, SLOTS, UNIT])
        arena = sb("arena", [P, 10, BLK])
        h = sb("h", [P, T, D])
        xT = sb("xT", [P, KD, SEQ])
        rows = sb("rows", [P, 2, D])
        ident = sb("ident", [P, P])
        cols = sb("cols", [P, N_COLS])
        mask = sb("mask", [P, T, SEQ])
        cos0, sin0 = sb("cos0", [P, T, HD]), sb("sin0", [P, T, HD])
        cosd, sind = sb("cosd", [P, T, DIFF_ROPE]), sb("sind", [P, T, DIFF_ROPE])
        cosr, sinr = sb("cosr", [P, T, MLA_ROPE]), sb("sinr", [P, T, MLA_ROPE])
        stat = sb("stat", [P, 128])
        nlam = sb("nlam", [P, 1])
        ps = ctx.enter_context(nc.psum_tensor("ps", [P, 8, 512], F32))

        def bank(b):
            return ps[:, b, :]

        def blk(i):
            return arena[:, i, :]

        def tok(i):
            return arena[:, i, :].rearrange("p (t f) -> p t f", t=T)

        def fm(i):
            return arena[:, i, :].rearrange("p (k s) -> p k s", k=KD)

        def col(name, i, n=1):
            return cols[:, COL[name] + i:COL[name] + i + n]

        signals = {}

        def sig(name):
            if name not in signals:
                signals[name] = Signal(ctx.enter_context(nc.semaphore(name)))
            return signals[name]

        def new_block():
            for s in signals.values():
                s.base = s.count
            return nc.Block(no_gpsimd_drain=True)

        def link(eng, name, ins, step=1):
            s = sig(name)
            ins.then_inc(s.up(step), step)
            eng.wait_ge(s.sem, s.count)

        proj, ffn, moe = d["w_proj"], d["w_ffn"], d["w_moe"]
        n_proj = [0]

        def take(n):
            n_proj[0] += n
            return [proj[n_proj[0] - n + i] for i in range(n)]

        loads = take(6) + take(2)
        loads += [ffn[i] for i in range(FU)]
        loads += take(6) + [d["w_lora"]] + take(2)
        loads += [ffn[FU + i] for i in range(FU)]
        loads += take(4) + take(6) + take(2)
        loads += take(4)
        moe_at = [len(loads)]
        loads += [moe[i] for i in range(EU)]
        loads += [d["w_b_in"], d["w_uq"], d["w_ukv"]] + take(2) + take(4)
        moe_at.append(len(loads))
        loads += [moe[EU + i] for i in range(EU)]
        loaded = [sig(f"weights_loaded{s}") for s in range(SLOTS)]
        pos = {"issued": 0, "unit": 0}
        release = {}

        def load(sp, j):
            if j >= SLOTS:
                sem, value = release[j - SLOTS]
                sp.wait_ge(sem, value)
            w = loads[j].shape[-1]
            sp.dma_start(ring[:, j % SLOTS, 0:w], loads[j]).then_inc(loaded[j % SLOTS].up(16), 16)

        def stream(block, n):
            first = pos["issued"]
            last = min(first + n, len(loads))
            pos["issued"] = last

            @block.sync
            def _(sp):
                for j in range(first, last):
                    load(sp, j)

        def arrived(pe, j):
            pe.wait_ge(loaded[j % SLOTS].sem, 16 * (j // SLOTS + 1))

        def unit_done(j, signal):
            release[j] = signal.sem, signal.count

        def next_unit(n=1):
            pos["unit"] += n
            return pos["unit"] - n

        def norm(kind, eps, xn, gains=None, store=None):
            src = xn if kind == "rms" else h
            with new_block() as block:
                sq_done, ms_ready, root, ready = sig("row_stats"), sig("mean_square"), sig("row_root"), sig("normed")
                tp, rows_in = sig("transposed"), sig("rows_loaded")
                ss, ms, std, rstd = stat[:, 0:2], stat[:, 2:4], stat[:, 4:6], stat[:, 6:8]
                bn, mv = stat[:, 8:32].rearrange("p (t c s) -> p t c s", t=T, c=2), stat[:, 32:36].rearrange("p (t s) -> p t s", t=T)

                @block.scalar
                def _(act):
                    if kind != "ln":
                        for t in range(T):
                            act.activation(xn[:, t, :], h[:, t, :], ACT.Square, accum_out=ss[:, t:t + 1]).then_inc(sq_done.up(), 1)
                    act.wait_ge(ms_ready.sem, ms_ready.at(1))
                    act.activation(std, ms, ACT.Sqrt).then_inc(root.up(), 1)
                    if gains is None:
                        for t in range(T):
                            act.wait_ge(tp.sem, tp.at(2 * t + 1))
                            act.copy(xT[:, 0:4, t * P:(t + 1) * P], bank(2 * t).rearrange("p (k s) -> p k s", k=4))

                @block.vector
                def _(dve):
                    if kind == "ln":
                        for t in range(T):
                            for c in range(2):
                                link(dve, "dve_step", dve.bn_stats(bn[:, t, c, :], h[:, t, c * 512:(c + 1) * 512]))
                            link(dve, "dve_step", dve.bn_aggr(mv[:, t, :], bn[:, t, :, :]))
                        dve.tensor_scalar(ms, mv[:, :, 1], eps, None, ALU.add).then_inc(ms_ready.up(), 1)
                    else:
                        dve.wait_ge(sq_done.sem, sq_done.at(T))
                        dve.tensor_scalar(ms, ss, 1.0 / D, eps, ALU.mult, ALU.add).then_inc(ms_ready.up(), 1)
                    dve.wait_ge(root.sem, root.at(1))
                    link(dve, "dve_step", dve.reciprocal(rstd, std))
                    for t in range(T):
                        if kind == "rms":
                            dve.tensor_scalar(xn[:, t, :], h[:, t, :], rstd[:, t:t + 1], None, ALU.mult).then_inc(ready.up(), 1)
                        elif kind == "rms_rows":
                            dve.wait_ge(rows_in.sem, rows_in.count)
                            dve.scalar_tensor_tensor(h[:, t, :], h[:, t, :], rstd[:, t:t + 1], rows[:, 0, :], ALU.mult, ALU.mult).then_inc(ready.up(), 1)
                        else:
                            dve.wait_ge(rows_in.sem, rows_in.count)
                            link(dve, "dve_step", dve.tensor_scalar(h[:, t, :], h[:, t, :], mv[:, t, 0:1], rstd[:, t:t + 1], ALU.subtract, ALU.mult))
                            link(dve, "dve_step", dve.tensor_tensor(h[:, t, :], h[:, t, :], rows[:, 0, :], ALU.mult))
                            dve.tensor_tensor(h[:, t, :], h[:, t, :], rows[:, 1, :], ALU.add).then_inc(ready.up(), 1)
                    for t in range(T):
                        for f in range(2):
                            if gains is None and f == 0:
                                continue
                            dve.wait_ge(tp.sem, tp.at(2 * t + f + 1))
                            o, i = xT[:, 4 * f:4 * f + 4, t * P:(t + 1) * P], bank(2 * t + f).rearrange("p (k s) -> p k s", k=4)
                            if gains is None:
                                dve.tensor_copy(o, i)
                            else:
                                g = gains[:, 4 * f:4 * f + 4].rearrange("p (k o) -> p k o", o=1).broadcast_to([P, 4, P])
                                dve.tensor_tensor(o, i, g, ALU.mult)

                @block.tensor
                def _(pe):
                    for t in range(T):
                        pe.wait_ge(ready.sem, ready.at(t + 1))
                        for f in range(2):
                            for k in range(4):
                                c = (4 * f + k) * P
                                last = pe.transpose(bank(2 * t + f)[:, k * P:(k + 1) * P], src[:, t, c:c + P], ident[:])
                            last.then_inc(tp.up(), 1)

                if store is not None:
                    @block.sync
                    def _(sp):
                        sp.wait_ge(ready.sem, ready.at(T))
                        stored = sig("stored")
                        sp.dma_start(store.rearrange("(t p) f -> p t f", p=P), h[:]).then_inc(stored.up(16), 16)
                        sp.wait_ge(stored.sem, stored.at(16))

        def transpose_all(pairs, scale=None):
            with new_block() as block:
                tp, free = sig("transposed"), [sig("act_evacuated"), sig("dve_evacuated")]
                jobs = [(s, o, t, f) for s, o in pairs for t in range(T) for f in range(2)]

                @block.tensor
                def _(pe):
                    for n, (s, o, t, f) in enumerate(jobs):
                        if n >= 8:
                            pe.wait_ge(free[n % 2].sem, free[n % 2].at(n // 2 - 3))
                        for k in range(4):
                            c = (4 * f + k) * P
                            last = pe.transpose(bank(n % 8)[:, k * P:(k + 1) * P], s[:, t, c:c + P], ident[:])
                        last.then_inc(tp.up(), 1)

                def evacuate(e):
                    def body(eng):
                        for n, (s, o, t, f) in enumerate(jobs):
                            if n % 2 != e:
                                continue
                            eng.wait_ge(tp.sem, tp.at(n + 1))
                            i = bank(n % 8).rearrange("p (k s) -> p k s", k=4)
                            q = o[:, 4 * f:4 * f + 4, t * P:(t + 1) * P]
                            if e == 0:
                                ins = eng.copy(q, i) if scale is None else eng.activation(q, i, ACT.Copy, scale=scale)
                            else:
                                ins = eng.tensor_copy(q, i) if scale is None else eng.tensor_scalar(q, i, scale, None, ALU.mult)
                            ins.then_inc(free[e].up(), 1)
                    return body

                block.scalar(evacuate(0))
                block.vector(evacuate(1))

        def rope(dve, x, heads, dh, at, rot, cos, sin, tmp):
            half = rot // 2
            v = x.rearrange("p (a f) -> p a f", a=heads)[:, :, at:at + rot]
            a = tmp[:, 0:heads * rot].rearrange("p (a f) -> p a f", a=heads)
            b = tmp[:, heads * rot:2 * heads * rot].rearrange("p (a f) -> p a f", a=heads)

            def wide(c):
                return c.rearrange("p (o f) -> p o f", o=1).broadcast_to([P, heads, c.shape[-1]])

            dve.tensor_tensor(a, v, wide(cos), ALU.mult)
            dve.tensor_tensor(b[:, :, 0:half], v[:, :, half:rot], wide(sin[:, 0:half]), ALU.mult)
            link(dve, "dve_step", dve.tensor_tensor(b[:, :, half:rot], v[:, :, 0:half], wide(sin[:, half:rot]), ALU.mult))
            return dve.tensor_tensor(v, a, b, ALU.add)

        def project(units, dest=None, src=None, rotary=None, residual=None, row_src=()):
            src = xT if src is None else src
            j0 = next_unit(units)
            with new_block() as block:
                mm, evac, free = sig("product_ready"), sig("act_evacuated"), sig("dve_evacuated")
                rows_in = sig("rows_loaded")

                @block.tensor
                def _(pe):
                    for u in range(units):
                        arrived(pe, j0 + u)
                        w = ring[:, (j0 + u) % SLOTS, 0:KD * COLS].rearrange("p (k n) -> p k n", k=KD)
                        for t in range(T):
                            n = T * u + t
                            if n >= 4:
                                pe.wait_ge((evac if residual is None else free).sem, (evac if residual is None else free).at(n - 3))
                            for k in range(KD):
                                last = pe.matmul(bank(n % 4), src[:, k, t * P:(t + 1) * P], w[:, k, :], start=(k == 0), stop=(k == KD - 1))
                            last.then_inc(mm.up(), 1)
                        unit_done(j0 + u, mm)
                stream(block, units)

                @block.scalar
                def _(act):
                    for i, r in enumerate(row_src):
                        act.dma_start(rows[:, i, :], r.rearrange("(o f) -> o f", o=1).broadcast_to([P, D])).then_inc(rows_in.up(16), 16)
                    if residual is None:
                        for n in range(T * units):
                            act.wait_ge(mm.sem, mm.at(n + 1))
                            act.copy(dest(n // T, n % T), bank(n % 4)).then_inc(evac.up(), 1)

                @block.vector
                def _(dve):
                    for n in range(T * units):
                        u, t = n // T, n % T
                        if residual is not None:
                            dve.wait_ge(mm.sem, mm.at(n + 1))
                            x = h[:, t, u * COLS:(u + 1) * COLS]
                            dve.scalar_tensor_tensor(x, x, residual, bank(n % 4), ALU.mult, ALU.add).then_inc(free.up(), 1)
                        elif rotary is not None and rotary(u) is not None:
                            heads, dh, at, rot, cos, sin, tmp = rotary(u)
                            dve.wait_ge(evac.sem, evac.at(n + 1))
                            link(dve, "dve_step", rope(dve, dest(u, t), heads, dh, at, rot, cos[:, t, :], sin[:, t, :], tmp))

        def project_fm(pe, w, src, n, out_bank, free):
            for m in range(4):
                if m % 2 == 0 and n + m // 2 >= 4:
                    pe.wait_ge(free.sem, free.at(n + m // 2 - 3))
                for k in range(KD):
                    last = pe.matmul(bank((n + m // 2) % 4)[:, (m % 2) * SEQ:(m % 2 + 1) * SEQ], w[:, k, m * P:(m + 1) * P],
                                     src[:, k, :], start=(k == 0), stop=(k == KD - 1))
                if m % 2:
                    last.then_inc(out_bank.up(), 1)
            return last

        def project_features(src, dst, units=2):
            j0 = next_unit(units)
            with new_block() as block:
                mm, evac = sig("product_ready"), sig("act_evacuated")

                @block.tensor
                def _(pe):
                    for u in range(units):
                        arrived(pe, j0 + u)
                        w = ring[:, (j0 + u) % SLOTS, 0:KD * COLS].rearrange("p (k n) -> p k n", k=KD)
                        project_fm(pe, w, src, 2 * u, mm, evac)
                        unit_done(j0 + u, mm)
                stream(block, units)

                @block.scalar
                def _(act):
                    for n in range(2 * units):
                        act.wait_ge(mm.sem, mm.at(n + 1))
                        act.copy(dst[:, 2 * n:2 * n + 2, :], bank(n % 4).rearrange("p (m s) -> p m s", m=2)).then_inc(evac.up(), 1)

        def attention(maps, q, k, v, dv, o, scale, use_mask, work, diff=False):
            s_sb = work[0][:, 0:1024].rearrange("p (b t s) -> p b t s", b=2, t=T)
            p_sb = work[0][:, 1024:2048].rearrange("p (b t s) -> p b t s", b=2, t=T)
            pT = work[1][:, 0:1024].rearrange("p (b c s) -> p b c s", b=2, c=4)
            nmax = stat[:, 0:4].rearrange("p (b t) -> p b t", b=2)
            sums = stat[:, 4:8].rearrange("p (b t) -> p b t", b=2)
            rs = stat[:, 8:12].rearrange("p (b t) -> p b t", b=2)
            pmax = stat[:, 12:16].rearrange("p (b t) -> p b t", b=2)
            with new_block() as block:
                s_mm, p_mm, o_mm = sig("scores_ready"), sig("transposed"), sig("product_ready")
                s_out, m_ready, p_ready = sig("scores_copied"), sig("max_ready"), sig("probs_ready")
                pT_ready, o_out = sig("act_evacuated"), sig("dve_evacuated")

                @block.tensor
                def _(pe):
                    for i in range(maps + 2):
                        if i < maps:
                            if i >= 2:
                                pe.wait_ge(s_out.sem, s_out.at(i - 1))
                            for t in range(T):
                                parts = list(zip(q(i, t), k(i)))
                                for n, (a, b) in enumerate(parts):
                                    last = pe.matmul(bank(i % 2)[:, t * SEQ:(t + 1) * SEQ], a, b, start=(n == 0), stop=(n == len(parts) - 1))
                            last.then_inc(s_mm.up(), 1)
                        if 1 <= i <= maps:
                            m = i - 1
                            pe.wait_ge(p_ready.sem, p_ready.at(T * (m + 1)))
                            if m >= 2:
                                pe.wait_ge(pT_ready.sem, pT_ready.at(m - 1))
                            for c in range(4):
                                last = pe.transpose(bank(2 + m % 2)[:, c * P:(c + 1) * P], p_sb[:, m % 2, c // 2, (c % 2) * P:(c % 2 + 1) * P], ident[:])
                            last.then_inc(p_mm.up(), 1)
                        if i >= 2:
                            m = i - 2
                            pe.wait_ge(pT_ready.sem, pT_ready.at(m + 1))
                            if m >= 2:
                                pe.wait_ge(o_out.sem, o_out.at(m - 1))
                            for t in range(T):
                                for kt in range(2):
                                    last = pe.matmul(bank(4 + m % 2)[:, t * dv:(t + 1) * dv], pT[:, m % 2, 2 * t + kt, :], v(m, kt), start=(kt == 0), stop=(kt == 1))
                            last.then_inc(o_mm.up(), 1)

                @block.vector
                def _(dve):
                    for i in range(maps + 2):
                        if i < maps:
                            b = i % 2
                            dve.wait_ge(s_mm.sem, s_mm.at(i + 1))
                            if i >= 2:
                                dve.wait_ge(p_ready.sem, p_ready.at(T * (i - 1)))
                            s = bank(b).rearrange("p (t s) -> p t s", t=T)
                            if use_mask:
                                ins = dve.scalar_tensor_tensor(s_sb[:, b], s, scale, mask[:], ALU.mult, ALU.add)
                            else:
                                ins = dve.tensor_scalar(s_sb[:, b], s, scale, None, ALU.mult)
                            ins.then_inc(s_out.up(), 1)
                            dve.wait_ge(s_out.sem, s_out.at(i + 1))
                            link(dve, "dve_step", dve.tensor_reduce(pmax[:, b, :], s_sb[:, b], AX, ALU.max))
                            dve.tensor_scalar(nmax[:, b, :], pmax[:, b, :], -1.0, None, ALU.mult).then_inc(m_ready.up(), 1)
                        if i >= 2:
                            m = i - 2
                            b = m % 2
                            dve.wait_ge(p_ready.sem, p_ready.at(T * (m + 1)))
                            link(dve, "dve_step", dve.reciprocal(rs[:, b, :], sums[:, b, :]))
                            if diff and m % 2:
                                link(dve, "dve_step", dve.tensor_scalar(rs[:, b, :], rs[:, b, :], nlam[:], None, ALU.mult))
                            dve.wait_ge(o_mm.sem, o_mm.at(m + 1))
                            for t in range(T):
                                x, r = bank(4 + b)[:, t * dv:(t + 1) * dv], rs[:, b, t:t + 1]
                                if diff and m % 2:
                                    ins = dve.scalar_tensor_tensor(o(m, t), x, r, o(m, t), ALU.mult, ALU.add)
                                else:
                                    ins = dve.tensor_scalar(o(m, t), x, r, None, ALU.mult)
                            ins.then_inc(o_out.up(), 1)
                            dve.wait_ge(o_out.sem, o_out.at(m + 1))

                @block.scalar
                def _(act):
                    for i in range(maps + 1):
                        if i < maps:
                            b = i % 2
                            act.wait_ge(m_ready.sem, m_ready.at(i + 1))
                            if i >= 2:
                                act.wait_ge(p_mm.sem, p_mm.at(i - 1))
                                act.wait_ge(o_out.sem, o_out.at(i - 1))
                            for t in range(T):
                                act.activation(p_sb[:, b, t, :], s_sb[:, b, t, :], ACT.Exp, bias=nmax[:, b, t:t + 1], accum_out=sums[:, b, t:t + 1]).then_inc(p_ready.up(), 1)
                        if i >= 1:
                            m = i - 1
                            act.wait_ge(p_mm.sem, p_mm.at(m + 1))
                            if m >= 2:
                                act.wait_ge(o_mm.sem, o_mm.at(m - 1))
                            act.copy(pT[:, m % 2], bank(2 + m % 2).rearrange("p (c s) -> p c s", c=4)).then_inc(pT_ready.up(), 1)

        pos["issued"] = SLOTS
        with new_block() as block:
            const_in, small_in = sig("inputs_loaded"), sig("small_loaded")
            trig = sig("angles_ready")
            posn = sb("posn", [P, T], I32)
            inv = blk(2)[:, 0:24]
            lam = blk(2)[:, 64:64 + 4 * HD].rearrange("p (a f) -> p a f", a=4)
            posf, ang, turn = stat[:, 0:2], blk(2)[:, 512:560], blk(2)[:, 576:624]
            red = blk(2)[:, 640:736].rearrange("p (c n) -> p c n", c=2)
            trigs = blk(2)[:, 768:864].rearrange("p (c n) -> p c n", c=2)
            lsum, lexp, lprod = stat[:, 4:6], stat[:, 6:8], blk(2)[:, 1024:1024 + 2 * HD].rearrange("p (a f) -> p a f", a=2)

            @block.sync
            def _(sp):
                for n, (o, i) in enumerate([(h[:], d["x"].rearrange("(t p) f -> p t f", p=P)), (ident[:], d["ident"]), (cols[:], d["cols"]),
                                            (mask[:], d["causal"]), (cos0[:], d["cos0"]), (sin0[:], d["sin0"])]):
                    sp.dma_start(o, i).then_inc(const_in.up(16), 16)
                    if n == 0:
                        load(sp, 0)
                for j in range(1, SLOTS):
                    load(sp, j)
                sp.wait_ge(const_in.sem, const_in.at(6 * 16))

            @block.scalar
            def _(act):
                act.dma_start(posn[:], d["pos"]).then_inc(small_in.up(16), 16)
                act.dma_start(inv, d["inv"].rearrange("(o f) -> o f", o=1).broadcast_to([P, 24])).then_inc(small_in.up(16), 16)
                act.dma_start(lam.rearrange("p a f -> p (a f)"), d["lam"].rearrange("(o f) -> o f", o=1).broadcast_to([P, 4 * HD])).then_inc(small_in.up(16), 16)
                act.wait_ge(trig.sem, trig.at(1))
                for c in range(2):
                    act.activation(trigs[:, c, :], red[:, c, :], ACT.Sin).then_inc(sig("trig_ready").up(), 1)
                act.wait_ge(sig("lambda_sums").sem, sig("lambda_sums").at(1))
                act.activation(lexp, lsum, ACT.Exp).then_inc(sig("lambda_exp").up(), 1)

            @block.vector
            def _(dve):
                def step(ins):
                    link(dve, "dve_step", ins)
                dve.wait_ge(small_in.sem, small_in.at(48))
                step(dve.tensor_copy(posf, posn[:]))
                two_pi = 2 * math.pi
                c1 = 6.28125
                c2 = math.floor((two_pi - c1) * 2 ** 19) / 2 ** 19
                c3 = two_pi - c1 - c2
                big = 1.5 * 2 ** 23
                for t in range(T):
                    step(dve.tensor_scalar(ang[:, t * 24:(t + 1) * 24], inv, posf[:, t:t + 1], None, ALU.mult))
                for c in range(2):
                    step(dve.tensor_scalar(turn, ang, 1 / two_pi, 0.25 * c, ALU.mult, ALU.add))
                    step(dve.tensor_scalar(turn, turn, big, None, ALU.add))
                    step(dve.tensor_scalar(turn, turn, big, None, ALU.subtract))
                    step(dve.scalar_tensor_tensor(red[:, c, :], turn, -c1, ang, ALU.mult, ALU.add))
                    step(dve.scalar_tensor_tensor(red[:, c, :], turn, -c2, red[:, c, :], ALU.mult, ALU.add))
                    step(dve.scalar_tensor_tensor(red[:, c, :], turn, -c3, red[:, c, :], ALU.mult, ALU.add))
                    if c:
                        step(dve.tensor_scalar(red[:, c, :], red[:, c, :], math.pi / 2, None, ALU.add))
                    step(dve.tensor_scalar(red[:, c, :], red[:, c, :], 3.1415925, -3.1415925, ALU.min, ALU.max))
                dve.tensor_scalar(red[:, 0, 0:1], red[:, 0, 0:1], 1.0, None, ALU.mult).then_inc(trig.up(), 1)
                dve.wait_ge(sig("trig_ready").sem, sig("trig_ready").at(2))
                for t in range(T):
                    for n, (c, s, half) in enumerate([(cosd, sind, DIFF_ROPE // 2), (cosr, sinr, MLA_ROPE // 2)]):
                        a = t * 24 + 8 * n
                        sn, cs = trigs[:, 0, a:a + half], trigs[:, 1, a:a + half]
                        dve.tensor_copy(c[:, t, 0:half], cs)
                        dve.tensor_copy(c[:, t, half:2 * half], cs)
                        dve.tensor_scalar(s[:, t, 0:half], sn, -1.0, None, ALU.mult)
                        dve.tensor_copy(s[:, t, half:2 * half], sn)
                step(dve.tensor_tensor(lprod, lam[:, 0:4:2, :], lam[:, 1:4:2, :], ALU.mult))
                step(dve.tensor_reduce(lsum, lprod, AX, ALU.add))
                dve.tensor_scalar(lsum, lsum, 1.0, None, ALU.mult).then_inc(sig("lambda_sums").up(), 1)
                dve.wait_ge(sig("lambda_exp").sem, sig("lambda_exp").at(1))
                step(dve.tensor_tensor(nlam[:], lexp[:, 1:2], lexp[:, 0:1], ALU.subtract))
                step(dve.tensor_scalar(nlam[:], nlam[:], LAMBDA_INIT, None, ALU.subtract))

        def ffn_stage(n_units, layer, expert_rows=None, row_src=(), residual=1.0):
            j0 = next_unit(n_units)
            hid = blk(0)[:, 0:1024].rearrange("p (b f s) -> p b f s", b=2, f=2)
            act_out = blk(1)[:, 0:1024].rearrange("p (b f s) -> p b f s", b=2, f=2)
            conv = blk(2)[:, 0:1024].rearrange("p (b f s) -> p b f s", b=2, f=2)
            group = SLOTS
            with new_block() as block:
                gu, dn = sig("gate_up_ready"), sig("down_done")
                biased, conv_ready, act_ready, hid_ready = sig("gate_biased"), sig("conv_ready"), sig("gate_active"), sig("hidden_ready")
                rows_in = sig("rows_loaded")
                moe_i = None if expert_rows is None else moe_at.index(j0)
                def runs(eng, body):
                    if expert_rows is None:
                        for n in range(n_units):
                            body(0, n, n == 0, n == n_units - 1, 1)
                        return
                    for u in range(group):
                        body(0, u, u == 0, False, 1)
                    with eng.Fori(1, n_units // group - 1) as i:
                        for u in range(group):
                            body(i, u, False, False, n_units // group - 2)
                    for u in range(group):
                        body(n_units // group - 1, u, False, u == group - 1, 1)

                def at(i, u):
                    return u if isinstance(i, int) and i == 0 else i * group + u

                @block.tensor
                def _(pe):
                    def down(i, u, first, last, r):
                        s = (j0 + u) % SLOTS
                        pe.wait_ge(hid_ready.sem, hid_ready.at(at(i, u) + 1))
                        w = ring[:, s, 2 * KD * 2 * P:UNIT].rearrange("p (f n) -> p f n", f=2)
                        for t in range(T):
                            for c in range(2):
                                for f in range(2):
                                    mm = pe.matmul(bank(4 + 2 * t + c), hid[:, u % 2, f, t * P:(t + 1) * P], w[:, f, c * 512:(c + 1) * 512],
                                                   start=(first and f == 0), stop=(last and f == 1), skip_group_check=True)
                        mm.then_inc(dn.up(1, r), 1)

                    def body(i, u, first, last, r):
                        s = (j0 + u) % SLOTS
                        pe.wait_ge(loaded[s].sem, i * 16 * (group // SLOTS) + 16 * ((j0 + u) // SLOTS + 1))
                        if not (isinstance(i, int) and i == 0 and u < 2):
                            pe.wait_ge(hid_ready.sem, hid_ready.at(at(i, u) - 1))
                        w = ring[:, s, 0:2 * KD * 2 * P].rearrange("p (g k n) -> p g k n", g=2, k=KD)
                        for g in range(2):
                            for f in range(2):
                                for k in range(KD):
                                    mm = pe.matmul(bank(2 * (u % 2) + g)[:, f * SEQ:(f + 1) * SEQ], w[:, g, k, f * P:(f + 1) * P], xT[:, k, :],
                                                   start=(k == 0), stop=(k == KD - 1))
                        mm.then_inc(gu.up(1, r), 1)
                        if not first:
                            down(i, u - 1, isinstance(i, int) and i == 0 and u == 1, False, r)

                    runs(pe, body)
                    if expert_rows is None:
                        down(0, n_units - 1, False, True, 1)
                    else:
                        down(n_units // group - 1, group - 1, False, True, 1)

                @block.scalar
                def _(act):
                    for n, r in enumerate(row_src):
                        act.dma_start(rows[:, n, :], r.rearrange("(o f) -> o f", o=1).broadcast_to([P, D])).then_inc(rows_in.up(16), 16)

                    def body(i, u, first, last, r):
                        b = u % 2
                        act.wait_ge(gu.sem, gu.at(at(i, u) + 1))
                        g = bank(2 * b).rearrange("p (f s) -> p f s", f=2)
                        if not (isinstance(i, int) and i == 0 and u < 2):
                            act.wait_ge(hid_ready.sem, hid_ready.at(at(i, u) - 1))
                        if expert_rows is None:
                            for f in range(2):
                                ft = 2 * u + f
                                act.activation(conv[:, b, f, :], g[:, f, :], ACT.Identity, bias=col("conv_b", layer * FT + ft),
                                                         scale=col("conv_w", (layer * 3 + 2) * FT + ft)).then_inc(biased.up(), 1)
                            act.wait_ge(conv_ready.sem, conv_ready.at(u + 1))
                            act.activation(act_out[:, b], conv[:, b], ACT.Silu).then_inc(act_ready.up(), 1)
                        else:
                            act.activation(act_out[:, b], g, ACT.Silu).then_inc(act_ready.up(1, r), 1)
                    runs(act, body)

                @block.vector
                def _(dve):
                    def body(i, u, first, last, r):
                        b = u % 2
                        gt = bank(2 * b).rearrange("p (f s) -> p f s", f=2)
                        up = bank(2 * b + 1).rearrange("p (f s) -> p f s", f=2)
                        if expert_rows is None:
                            dve.wait_ge(biased.sem, biased.at(2 * u + 2))
                            for lag, w in ((1, 1), (2, 0)):
                                for f in range(2):
                                    ft = 2 * u + f
                                    x = conv[:, b, f, lag:SEQ]
                                    ins = dve.scalar_tensor_tensor(x, gt[:, f, 0:SEQ - lag], col("conv_w", (layer * 3 + w) * FT + ft), x, ALU.mult, ALU.add)
                                if lag == 1:
                                    link(dve, "dve_step", ins)
                            ins.then_inc(conv_ready.up(), 1)
                        dve.wait_ge(act_ready.sem, act_ready.at(at(i, u) + 1))
                        if not (isinstance(i, int) and i == 0 and u < 2):
                            dve.wait_ge(dn.sem, dn.at(at(i, u) - 1))
                        if expert_rows is None:
                            dve.tensor_tensor(hid[:, b], act_out[:, b], up, ALU.mult).then_inc(hid_ready.up(), 1)
                        else:
                            weighted = sig("gate_weighted")
                            if isinstance(i, int):
                                e = expert_rows[:, (i * group + u) // 2, :].rearrange("p (o s) -> p o s", o=1)
                            else:
                                e = expert_rows[:, bass.ds(i * (group // 2) + u // 2, 1), :]
                            dve.tensor_tensor(act_out[:, b], act_out[:, b], e.broadcast_to([P, 2, SEQ]), ALU.mult).then_inc(weighted.up(1, r), 1)
                            dve.wait_ge(weighted.sem, weighted.at(at(i, u) + 1))
                            dve.tensor_tensor(hid[:, b], act_out[:, b], up, ALU.mult).then_inc(hid_ready.up(1, r), 1)
                    runs(dve, body)
                    dve.wait_ge(dn.sem, dn.at(n_units))
                    for t in range(T):
                        for c in range(2):
                            x = h[:, t, c * 512:(c + 1) * 512]
                            dve.scalar_tensor_tensor(x, x, residual, bank(4 + 2 * t + c), ALU.mult, ALU.add)

                for n in range(n_units):
                    release[j0 + n] = dn.sem, dn.base + n + 1
                if expert_rows is None:
                    stream(block, n_units)
                else:
                    first, last = pos["issued"], min(pos["issued"] + n_units, len(loads))
                    pos["issued"] = last

                    @block.sync
                    def _(sp):
                        with sp.Fori(0, n_units // group - 1) as i:
                            for u in range(group):
                                j = first + u
                                sp.wait_ge(dn.sem, dn.at(i * group + (u + 1)))
                                src = moe[bass.ds(i * group + (moe_i * EU + group + u), 1), :, :].rearrange("a p n -> p (a n)")
                                sp.dma_start(ring[:, j % SLOTS, :], src).then_inc(loaded[j % SLOTS].up(16, n_units // group - 1), 16)
                        for j in range(first + n_units - group, last):
                            load(sp, j)

        def first_attention():
            norm("rms", RMS_EPS, tok(0), gains=col("norm_mix", 0, KD))
            project(6, dest=lambda u, t: tok(u // 2)[:, t, (u % 2) * COLS:(u % 2 + 1) * COLS],
                    rotary=lambda u: (8, HD, 0, HD, cos0, sin0, blk(3)) if u < 4 else None)
            transpose_all([(tok(0), fm(3)), (tok(1), fm(4))])

            def hs(m):
                return slice(64 * (m % 2), 64 * (m % 2) + 64)
            attention(HEADS, lambda m, t: [fm(3)[hs(m), m // 2, t * P:(t + 1) * P]], lambda m: [fm(4)[hs(m), m // 2, :]],
                      lambda m, kt: tok(2)[:, kt, m * HD:(m + 1) * HD], HD, lambda m, t: tok(5)[:, t, m * HD:(m + 1) * HD],
                      HD ** -0.5, True, (blk(6), blk(7)))
            transpose_all([(tok(5), xT)])
            project(2, residual=1.0)

        def rwkv():
            A_, R_ = 1, 7
            BKs = arena[:, 2:4, :].rearrange("p a f -> p (a f)").rearrange("p (m c w s) -> p m c w s", m=KD, c=NCH, w=2)
            UV = arena[:, 5:7, :].rearrange("p a f -> p (a f)").rearrange("p (c g m v) -> p c g m v", c=NCH, g=2, m=KD)
            gT = fm(9)
            sgm, xx = fm(3), fm(0)
            mixes = [fm(1), fm(2)]
            kx, ax, rx = fm(8), fm(4), fm(R_)
            pc = stat[:, 64:96].rearrange("p (m c) -> p m c", m=KD)
            bonus = sb("bonus", [P, NCH, HEADS])
            norm("rms", RMS_EPS, tok(0), gains=col("norm_mix", KD, KD))
            j0 = next_unit(7)
            order = [0, 2, 3, 1, 4, 5]
            hw, ha, hg = rows[0:64, 0, 0:SEQ], rows[0:64, 0, 256:512], rows[:, 0, 512:768]
            with new_block() as block:
                mix_ready, mm, evac = sig("mix_ready"), sig("product_ready"), sig("act_evacuated")
                reads = [4, 8, 12, 13]

                @block.vector
                def _(dve):
                    link(dve, "dve_step", dve.tensor_tensor(xx[:, :, 1:SEQ], xT[:, :, 0:SEQ - 1], xT[:, :, 1:SEQ], ALU.subtract))
                    link(dve, "dve_step", dve.tensor_scalar(xx[:, :, 0:1], xT[:, :, 0:1], -1.0, None, ALU.mult))
                    for n, i in enumerate(order):
                        if n >= 2:
                            dve.wait_ge(mm.sem, mm.at(reads[n - 2]))
                        for k in range(KD):
                            ins = dve.scalar_tensor_tensor(mixes[n % 2][:, k, :], xx[:, k, :], col("mu", i * KD + k), xT[:, k, :], ALU.mult, ALU.add)
                        ins.then_inc(mix_ready.up(), 1)

                @block.tensor
                def _(pe):
                    n = 0
                    for i in range(2):
                        pe.wait_ge(mix_ready.sem, mix_ready.at(i + 1))
                        for u in range(2):
                            arrived(pe, j0 + 2 * i + u)
                            w = ring[:, (j0 + 2 * i + u) % SLOTS, 0:KD * COLS].rearrange("p (k n) -> p k n", k=KD)
                            project_fm(pe, w, mixes[i], n, mm, evac)
                            unit_done(j0 + 2 * i + u, mm)
                            n += 2
                    pe.wait_ge(mix_ready.sem, mix_ready.at(3))
                    for u in range(2):
                        arrived(pe, j0 + 4 + u)
                        w = ring[:, (j0 + 4 + u) % SLOTS, 0:KD * COLS].rearrange("p (k n) -> p k n", k=KD)
                        for t in range(T):
                            pe.wait_ge(evac.sem, evac.at(n - 3))
                            for k in range(KD):
                                last = pe.matmul(bank(n % 4), mixes[0][:, k, t * P:(t + 1) * P], w[:, k, :], start=(k == 0), stop=(k == KD - 1))
                            last.then_inc(mm.up(), 1)
                            n += 1
                        unit_done(j0 + 4 + u, mm)
                    arrived(pe, j0 + 6)
                    lora = ring[:, (j0 + 6) % SLOTS, :]
                    w1, a1 = (lora[:, a:a + 512].rearrange("p (k n) -> p k n", k=KD) for a in (0, 512))
                    g1 = lora[:, 1024:2048].rearrange("p (k n) -> p k n", k=KD)
                    w2, a2, g2 = lora[0:64, 2048:3072], lora[0:64, 3072:4096], lora[:, 4096:5120]
                    for i, (wi, rank, wo, hid) in enumerate([(w1, 64, w2, hw), (a1, 64, a2, ha), (g1, 128, g2, hg)]):
                        pe.wait_ge(mix_ready.sem, mix_ready.at(4 + i))
                        pe.wait_ge(evac.sem, evac.at(n - 3))
                        for k in range(KD):
                            last = pe.matmul(bank(n % 4)[0:rank, 0:SEQ], wi[:, k, :], mixes[(3 + i) % 2][:, k, :], start=(k == 0), stop=(k == KD - 1))
                        last.then_inc(mm.up(), 1)
                        n += 1
                        pe.wait_ge(evac.sem, evac.at(n))
                        for f in range(4):
                            pe.wait_ge(evac.sem, evac.at(n - 3))
                            for m in range(2):
                                c = (2 * f + m) * P
                                last = pe.matmul(bank(n % 4)[:, m * SEQ:(m + 1) * SEQ], wo[:, c:c + P], hid, start=True, stop=True)
                            last.then_inc(mm.up(), 1)
                            n += 1
                    unit_done(j0 + 6, mm)
                stream(block, 7)

                @block.scalar
                def _(act):
                    n = 0
                    for dst in (rx, kx):
                        for f in range(4):
                            act.wait_ge(mm.sem, mm.at(n + 1))
                            act.copy(dst[:, 2 * f:2 * f + 2, :], bank(n % 4).rearrange("p (m s) -> p m s", m=2)).then_inc(evac.up(), 1)
                            n += 1
                    for u in range(2):
                        for t in range(T):
                            act.wait_ge(mm.sem, mm.at(n + 1))
                            for half in range(2):
                                o = UV[64:128, 2 * t + half, :, 4 * u:4 * u + 4, :].rearrange("p g m v -> p m g v")
                                ins = act.copy(o, bank(n % 4)[64 * half:64 * half + 64, :].rearrange("p (m g v) -> p m g v", m=4, g=2))
                            ins.then_inc(evac.up(), 1)
                            n += 1
                    for i, (hid, fn, rank, dst, fn2, bias) in enumerate([(hw, ACT.Tanh, 64, sgm, ACT.Sigmoid, "w0"), (ha, ACT.Copy, 64, ax, ACT.Sigmoid, "a0"),
                                                                         (hg, ACT.Sigmoid, 128, gT, ACT.Copy, None)]):
                        act.wait_ge(mm.sem, mm.at(n + 1))
                        act.activation(hid, bank(n % 4)[0:rank, 0:SEQ], fn).then_inc(evac.up(), 1)
                        n += 1
                        for f in range(4):
                            act.wait_ge(mm.sem, mm.at(n + 1))
                            for m in range(2):
                                k = 2 * f + m
                                src = bank(n % 4)[:, m * SEQ:(m + 1) * SEQ]
                                ins = act.activation(dst[:, k, :], src, fn2) if bias is None else act.activation(dst[:, k, :], src, fn2, bias=col(bias, k))
                            ins.then_inc(evac.up(), 1)
                            n += 1

            cum, kk, scratch = fm(0), fm(A_), fm(2)
            spread = rows[0:HEADS, 0, :].rearrange("p (m f) -> p m f", m=KD)
            heads16 = rows[:, 1, 0:KD * HEADS].rearrange("p (m a) -> p m a", m=KD)
            reset = rows[:, 1, 256:512]
            pair = rows[:, 1, 512:514]
            with new_block() as block:
                c_in, step_a = sig("small_loaded"), sig("act_step")
                kk_raw, sq, ss_mm, nrm, inv_ready, wide_mm, wide_used = (sig(x) for x in ("kk_ready", "squares_ready", "scores_ready", "row_root", "inverse_ready", "product_ready", "dve_evacuated"))
                rk_ready, bonus_mm, cum_ready, diff_ready = sig("bonus_terms"), sig("transposed"), sig("cumsum_ready"), sig("cumsum_before")
                exp_ready, exp_used = sig("exps_ready"), sig("exps_used")
                root = mask.rearrange("p t s -> p (t s)")[0:HEADS, 0:SEQ]
                rin = mask.rearrange("p t s -> p (t s)")[0:HEADS, SEQ:2 * SEQ]

                @block.sync
                def _(sp):
                    sp.dma_start(spread, d["spread"]).then_inc(c_in.up(16), 16)
                    sp.dma_start(heads16, d["heads16"]).then_inc(c_in.up(16), 16)
                    sp.dma_start(reset, d["reset"]).then_inc(c_in.up(16), 16)
                    sp.dma_start(pair, d["pair"]).then_inc(c_in.up(16), 16)

                @block.vector
                def _(dve):
                    def step(ins):
                        link(dve, "dve_step", ins)
                    for m in range(KD):
                        dve.tensor_scalar(kk[:, m, :], kx[:, m, :], col("k_k", m), None, ALU.mult).then_inc(kk_raw.up(), 1)
                    dve.wait_ge(c_in.sem, c_in.at(64))
                    for m in range(KD):
                        ins = dve.tensor_tensor_scan(cum[:, m, :], reset, sgm[:, m, :], 0.0, ALU.mult, ALU.add)
                    ins.then_inc(cum_ready.up(), 1)
                    dve.wait_ge(sq.sem, sq.at(2))
                    dve.wait_ge(ss_mm.sem, ss_mm.at(1))
                    for m in range(KD):
                        ins = dve.tensor_scalar(scratch[:, m, :], ax[:, m, :], 1.0, col("k_a", m), ALU.subtract, ALU.mult)
                    step(ins)
                    step(dve.scalar_tensor_tensor(kx, scratch, 1.0, kx, ALU.add, ALU.mult))
                    for m in range(KD):
                        ins = dve.scalar_tensor_tensor(xT[:, m, :], rx[:, m, :], col("r_k", m), kx[:, m, :], ALU.mult, ALU.mult)
                    ins.then_inc(rk_ready.up(), 1)
                    dve.wait_ge(nrm.sem, nrm.at(1))
                    step(dve.tensor_scalar(root, root, 1e-12, None, ALU.max))
                    dve.reciprocal(rin, root).then_inc(inv_ready.up(), 1)
                    for n in range(4):
                        dve.wait_ge(wide_mm.sem, wide_mm.at(n + 1))
                        x = kk[:, 2 * n:2 * n + 2, :]
                        ins = dve.tensor_tensor(x, x, bank(n + 1).rearrange("p (m s) -> p m s", m=2), ALU.mult)
                    step(ins)
                    step(dve.tensor_tensor(ax, kk, ax, ALU.mult))
                    dve.tensor_tensor(sgm, cum, sgm, ALU.subtract).then_inc(diff_ready.up(), 1)
                    dve.wait_ge(exp_ready.sem, exp_ready.at(1))
                    step(dve.tensor_copy(pc, scratch.rearrange("p m (c s) -> p m c s", c=NCH)[:, :, :, CHUNK - 1]))
                    dve.tensor_tensor(rx, rx, scratch, ALU.mult).then_inc(exp_used.up(), 1)
                    dve.wait_ge(exp_ready.sem, exp_ready.at(2))
                    dve.scalar_tensor_tensor(kk, kk, -1.0, sgm, ALU.mult, ALU.mult).then_inc(exp_used.up(), 1)
                    dve.wait_ge(exp_ready.sem, exp_ready.at(3))
                    dve.wait_ge(exp_used.sem, exp_used.at(2))
                    for w, x in enumerate((ax, kx)):
                        dve.tensor_tensor(BKs[:, :, :, w, :], x.rearrange("p m (c s) -> p m c s", c=NCH), cum.rearrange("p m (c s) -> p m c s", c=NCH), ALU.mult)
                    dve.wait_ge(bonus_mm.sem, bonus_mm.at(1))
                    dve.tensor_copy(bonus[64:128].rearrange("p c a -> p (c a)"), bank(5)[64:128, 0:NCH * HEADS])

                @block.scalar
                def _(act):
                    act.wait_ge(kk_raw.sem, kk_raw.at(KD))
                    act.activation(scratch, kk, ACT.Square).then_inc(sq.up(2), 2)
                    act.wait_ge(ss_mm.sem, ss_mm.at(1))
                    act.activation(root, bank(0)[0:HEADS, 0:SEQ], ACT.Sqrt).then_inc(nrm.up(), 1)
                    act.wait_ge(rk_ready.sem, rk_ready.at(1))
                    act.wait_ge(cum_ready.sem, cum_ready.at(1))
                    act.activation(scratch, cum, ACT.Exp, scale=DECAY).then_inc(exp_ready.up(), 1)
                    act.wait_ge(diff_ready.sem, diff_ready.at(1))
                    act.activation(sgm, sgm, ACT.Exp, scale=DECAY).then_inc(exp_ready.up(), 1)
                    act.wait_ge(exp_ready.sem, exp_ready.at(1))
                    act.activation(cum, cum, ACT.Exp, scale=-DECAY).then_inc(exp_ready.up(), 1)

                @block.tensor
                def _(pe):
                    pe.wait_ge(c_in.sem, c_in.at(64))
                    pe.wait_ge(sq.sem, sq.at(2))
                    for m in range(KD):
                        last = pe.matmul(bank(0)[0:HEADS, 0:SEQ], heads16[:, m, :], scratch[:, m, :], start=(m == 0), stop=(m == KD - 1))
                    last.then_inc(ss_mm.up(), 1)
                    pe.wait_ge(rk_ready.sem, rk_ready.at(1))
                    for c in range(NCH):
                        for m in range(KD):
                            last = pe.matmul(bank(5)[64:128, c * HEADS + 2 * m:c * HEADS + 2 * m + 2], xT[:, m, c * CHUNK:(c + 1) * CHUNK], pair, start=True, stop=True)
                    last.then_inc(bonus_mm.up(), 1)
                    pe.wait_ge(inv_ready.sem, inv_ready.at(1))
                    for m in range(KD):
                        last = pe.matmul(bank(1 + m // 2)[:, (m % 2) * SEQ:(m % 2 + 1) * SEQ], spread[:, m, :], rin, start=True, stop=True)
                        if m % 2:
                            last.then_inc(wide_mm.up(), 1)

            view = arena[:, :, :].rearrange("p b (m c s) -> p b m c s", m=KD, c=NCH)

            def AR(m, c):
                return view[:, A_:R_ + 1:R_ - A_, m, c, :]

            def BK(m, c):
                return BKs[:, m, c, :, :].rearrange("p w s -> p (w s)")

            G = blk(0).rearrange("p (g m s) -> p g m s", g=2, m=KD)
            BKt = blk(4)[:, 0:1024].rearrange("p (m s) -> p m s", m=KD)
            M = blk(4)[0:64, 1024:2048].rearrange("p (g m s) -> p g m s", g=2, m=KD)
            X = blk(8)[0:64, 0:1024].rearrange("p (g m s) -> p g m s", g=2, m=KD)
            Y = blk(4)[64:128, 1024:2048]
            Z = blk(8)[64:128, 0:1024]
            W1 = blk(8)[64:128, 1024:2048]
            lmask = stat[0:64, 0:64]
            ST = mask.rearrange("p t s -> p (t s)").rearrange("p (m v) -> p m v", m=KD)
            gm = cos0.rearrange("p t f -> p (t f)")
            ROUNDS = 5

            with new_block() as block:
                c_in = sig("small_loaded")
                n = {x: sig(x) for x in ("bk_turned", "bk_copied", "g_ready", "g_masked", "m_ready", "m_masked", "squared", "n_copied", "m_copied",
                                         "x_step", "x_added", "rhs_ready", "rhs_copied", "u_ready", "u_copied", "y_ready", "state_ready", "state_updated",
                                         "y_copied", "z_ready", "z_turned", "z_gated")}

                @block.sync
                def _(sp):
                    sp.dma_start(gm, d["gmask"]).then_inc(c_in.up(16), 16)
                    sp.dma_start(lmask, d["lmask"]).then_inc(c_in.up(16), 16)
                    sp.dma_start(rows[:, 0, :], d["lnx_w"].rearrange("(o f) -> o f", o=1).broadcast_to([P, D])).then_inc(c_in.up(16), 16)
                    sp.dma_start(rows[:, 1, :], d["lnx_b"].rearrange("(o f) -> o f", o=1).broadcast_to([P, D])).then_inc(c_in.up(16), 16)

                @block.tensor
                def _(pe):
                    def z_turn(c):
                        pe.wait_ge(n["z_ready"].sem, n["z_ready"].at(c + 1))
                        if c:
                            pe.wait_ge(n["z_gated"].sem, n["z_gated"].at(c))
                        for m in range(KD):
                            last = pe.transpose(bank(7)[:, m * CHUNK:(m + 1) * CHUNK], Z[:, m * P:(m + 1) * P], ident[64:128, 64:128])
                        last.then_inc(n["z_turned"].up(), 1)

                    for c in range(NCH):
                        if c:
                            pe.wait_ge(n["u_copied"].sem, n["u_copied"].at(2 * c))
                            pe.wait_ge(n["state_updated"].sem, n["state_updated"].at(c))
                            pe.wait_ge(n["y_copied"].sem, n["y_copied"].at(2 * c))
                        for m in range(KD):
                            last = pe.transpose(bank(m // 4)[:, (m % 4) * P:(m % 4 + 1) * P], BK(m, c), ident[:])
                            if m % 4 == 3:
                                last.then_inc(n["bk_turned"].up(), 1)
                        for m in range(KD):
                            for g in range(2):
                                hs = slice(64 * g, 64 * g + 64)
                                last = pe.matmul(bank(2 + 2 * g + m // 4)[:, (m % 4) * P:(m % 4 + 1) * P], BK(m, c)[hs], AR(m, c)[hs], start=True, stop=True)
                        last.then_inc(n["g_ready"].up(), 1)
                        if c:
                            z_turn(c - 1)
                            pe.wait_ge(n["z_gated"].sem, n["z_gated"].at(c))
                        for m in range(KD):
                            for g in range(2):
                                hs = slice(64 * g, 64 * g + 64)
                                last = pe.matmul(bank(6 + g)[0:64, m * 64:(m + 1) * 64], view[hs, A_, m, c, :], BKs[hs, m, c, 0, :], start=True, stop=True)
                        last.then_inc(n["m_ready"].up(), 1)
                        for j in range(ROUNDS):
                            r = c * ROUNDS + j
                            pe.wait_ge(n["g_masked"].sem, n["g_masked"].at(5 * (c + 1)))
                            pe.wait_ge(n["m_masked"].sem, n["m_masked"].at(c + 1))
                            if j:
                                pe.wait_ge(n["n_copied"].sem, n["n_copied"].at(c * (ROUNDS - 1) + j))
                            for g in range(2):
                                for m in range(KD):
                                    N_ = G[0:64, g, m, 0:64]
                                    if j < ROUNDS - 1:
                                        pe.matmul(bank(2 + g)[0:64, m * 64:(m + 1) * 64], M[:, g, m, :], N_, start=True, stop=True)
                                    last = pe.matmul(bank(4 + g)[0:64, m * 64:(m + 1) * 64], N_, M[:, g, m, :], start=True, stop=True)
                            last.then_inc(n["squared"].up(), 1)
                            pe.wait_ge(n["m_copied"].sem, n["m_copied"].at(r + 1))
                            if r:
                                pe.wait_ge(n["x_added"].sem, n["x_added"].at(r))
                            for g in range(2):
                                for m in range(KD):
                                    last = pe.matmul(bank(6 + g)[0:64, m * 64:(m + 1) * 64], M[:, g, m, :], X[:, g, m, :], start=True, stop=True)
                            last.then_inc(n["x_step"].up(), 1)
                        pe.wait_ge(n["bk_copied"].sem, n["bk_copied"].at(2 * c + 2))
                        if c:
                            pe.wait_ge(n["state_updated"].sem, n["state_updated"].at(c))
                            for g in range(2):
                                for m in range(KD):
                                    hs = slice(64 * g, 64 * g + 64)
                                    last = pe.matmul(bank(g)[0:64, m * 64:(m + 1) * 64], view[hs, A_, m, c, :], ST[hs, m, :], start=(m == 0), stop=False, skip_group_check=True)
                            last.then_inc(sig("from_state").up(), 1)
                            pe.wait_ge(sig("from_state").sem, sig("from_state").at(c))
                        for g in range(2):
                            for m in range(KD):
                                last = pe.matmul(bank(g)[0:64, m * 64:(m + 1) * 64], G[64:128, g, m, 0:64], UV[64:128, c, g, m, :],
                                                 start=(c == 0 and m == 0), stop=(m == KD - 1), skip_group_check=True)
                        last.then_inc(n["rhs_ready"].up(), 1)
                        pe.wait_ge(n["rhs_copied"].sem, n["rhs_copied"].at(2 * c + 2))
                        pe.wait_ge(n["x_added"].sem, n["x_added"].at((c + 1) * ROUNDS))
                        for g in range(2):
                            for m in range(KD):
                                last = pe.matmul(bank(2 + g)[0:64, m * 64:(m + 1) * 64], X[:, g, m, :], M[:, g, m, :], start=True, stop=True)
                        last.then_inc(n["u_ready"].up(), 1)
                        if c:
                            for g in range(2):
                                for m in range(KD):
                                    hs = slice(64 * g, 64 * g + 64)
                                    pe.matmul(bank(4 + g)[64:128, m * 64:(m + 1) * 64], view[hs, R_, m, c, :], ST[hs, m, :], start=(m == 0), stop=False, skip_group_check=True)
                        pe.wait_ge(n["u_copied"].sem, n["u_copied"].at(2 * c + 2))
                        for g in range(2):
                            for m in range(KD):
                                last = pe.matmul(bank(4 + g)[64:128, m * 64:(m + 1) * 64], G[:, g, m, 64:128], UV[:, c, g, m, :],
                                                 start=(c == 0 and m == 0), stop=(m == KD - 1), skip_group_check=True)
                        last.then_inc(n["y_ready"].up(), 1)
                        for g in range(2):
                            for m in range(KD):
                                last = pe.matmul(bank(6)[64 * g:64 * g + 64, m * 64:(m + 1) * 64], BKt[:, m, 64 * g:64 * g + 64], UV[:, c, g, m, :], start=True, stop=True)
                        last.then_inc(n["state_ready"].up(), 1)
                    z_turn(NCH - 1)

                @block.scalar
                def _(act):
                    def post(c):
                        act.wait_ge(sig("centred").sem, sig("centred").at(c + 1))
                        act.activation(W1, Y, ACT.Square).then_inc(sig("squares_ready").up(), 1)
                        act.wait_ge(sig("mean_square").sem, sig("mean_square").at(c + 1))
                        act.activation(stat[64:128, 32:48], stat[64:128, 16:32], ACT.Sqrt).then_inc(sig("row_root").up(), 1)

                    for c in range(NCH):
                        for f in range(2):
                            act.wait_ge(n["bk_turned"].sem, n["bk_turned"].at(2 * c + f + 1))
                            act.copy(BKt[:, 4 * f:4 * f + 4, :], bank(f).rearrange("p (m s) -> p m s", m=4)).then_inc(n["bk_copied"].up(), 1)
                        if c:
                            post(c - 1)
                        for j in range(ROUNDS - 1):
                            act.wait_ge(n["squared"].sem, n["squared"].at(c * ROUNDS + j + 1))
                            for g in range(2):
                                ins = act.copy(G[0:64, g, :, 0:64], bank(2 + g)[0:64, :].rearrange("p (m s) -> p m s", m=KD))
                            ins.then_inc(n["n_copied"].up(), 1)
                        act.wait_ge(n["rhs_ready"].sem, n["rhs_ready"].at(c + 1))
                        act.wait_ge(n["x_step"].sem, n["x_step"].at((c + 1) * ROUNDS))
                        act.copy(M[:, 0], bank(0)[0:64, :].rearrange("p (m s) -> p m s", m=KD)).then_inc(n["rhs_copied"].up(), 1)
                        act.wait_ge(n["u_ready"].sem, n["u_ready"].at(c + 1))
                        act.copy(UV[0:64, c, 0, :, :], bank(2)[0:64, :].rearrange("p (m s) -> p m s", m=KD)).then_inc(n["u_copied"].up(), 1)
                        act.wait_ge(n["y_ready"].sem, n["y_ready"].at(c + 1))
                        if c:
                            act.wait_ge(n["z_ready"].sem, n["z_ready"].at(c))
                        for g in range(2):
                            act.copy(Y.rearrange("p (m g v) -> p m g v", m=KD, g=2)[:, :, g, :], bank(4 + g)[64:128, :].rearrange("p (m v) -> p m v", m=KD)).then_inc(n["y_copied"].up(), 1)
                    post(NCH - 1)

                @block.vector
                def _(dve):
                    def step(ins):
                        link(dve, "dve_step", ins)

                    def by_head(s):
                        return s.rearrange("p (a o) -> p a o", o=1).broadcast_to([64, HEADS, HD])

                    def rows3(x):
                        return x.rearrange("p (a v) -> p a v", a=HEADS)

                    sm = stat[64:128, 0:16]

                    def post_a(c):
                        dve.wait_ge(n["y_copied"].sem, n["y_copied"].at(2 * c + 2))
                        step(dve.tensor_reduce(sm, rows3(Y), AX, ALU.add))
                        step(dve.tensor_scalar(sm, sm, 1.0 / HD, None, ALU.mult))
                        dve.tensor_tensor(rows3(Y), rows3(Y), by_head(sm), ALU.subtract).then_inc(sig("centred").up(), 1)

                    def post_b(c):
                        dve.wait_ge(sig("squares_ready").sem, sig("squares_ready").at(c + 1))
                        step(dve.tensor_reduce(sm, rows3(W1), AX, ALU.add))
                        dve.tensor_scalar(stat[64:128, 16:32], sm, 1.0 / HD, LNX_EPS, ALU.mult, ALU.add).then_inc(sig("mean_square").up(), 1)
                        v = UV[64:128, c, :, :, :]
                        for g in range(2):
                            s = bonus[64:128, c, g:HEADS:2].rearrange("p (m o) -> p m o", o=1).broadcast_to([64, KD, HD])
                            ins = dve.tensor_tensor(W1.rearrange("p (m g v) -> p m g v", m=KD, g=2)[:, :, g, :], v[:, g], s, ALU.mult)
                        step(ins)
                        step(dve.tensor_tensor(W1, W1, rows[64:128, 1, :], ALU.add))
                        dve.wait_ge(sig("row_root").sem, sig("row_root").at(c + 1))
                        step(dve.reciprocal(stat[64:128, 48:64], stat[64:128, 32:48]))
                        step(dve.tensor_tensor(rows3(Y), rows3(Y), by_head(stat[64:128, 48:64]), ALU.mult))
                        step(dve.tensor_tensor(Y, Y, rows[64:128, 0, :], ALU.mult))
                        if c:
                            dve.wait_ge(n["z_turned"].sem, n["z_turned"].at(c))
                        dve.tensor_tensor(Z, Y, W1, ALU.add).then_inc(n["z_ready"].up(), 1)

                    def post_c(c):
                        dve.wait_ge(n["z_turned"].sem, n["z_turned"].at(c + 1))
                        x = bank(7).rearrange("p (m s) -> p m s", m=KD)
                        dve.tensor_tensor(xT[:, :, c * CHUNK:(c + 1) * CHUNK], x, gT[:, :, c * CHUNK:(c + 1) * CHUNK], ALU.mult).then_inc(n["z_gated"].up(), 1)

                    dve.wait_ge(c_in.sem, c_in.at(64))
                    wide_g = gm.rearrange("p (o s) -> p o s", o=1).broadcast_to([P, 4, P])
                    wide_l = lmask.rearrange("p (o s) -> p o s", o=1).broadcast_to([64, KD, 64])
                    wide_i = ident[0:64, 0:64].rearrange("p (o s) -> p o s", o=1).broadcast_to([64, KD, 64])
                    for c in range(NCH):
                        dve.wait_ge(n["g_ready"].sem, n["g_ready"].at(c + 1))
                        for b in range(4):
                            dve.tensor_tensor(G[:, b // 2, 4 * (b % 2):4 * (b % 2) + 4, :], bank(2 + b).rearrange("p (m s) -> p m s", m=4), wide_g, ALU.mult).then_inc(n["g_masked"].up(), 1)
                        if c:
                            post_b(c - 1)
                            post_c(c - 1)
                        dve.wait_ge(n["m_ready"].sem, n["m_ready"].at(c + 1))
                        for g in range(2):
                            ins = dve.tensor_tensor(M[:, g], bank(6 + g)[0:64, :].rearrange("p (m s) -> p m s", m=KD), wide_l, ALU.mult)
                        ins.then_inc(n["m_masked"].up(), 1)
                        dve.wait_ge(n["g_masked"].sem, n["g_masked"].at(5 * c + 4))
                        for g in range(2):
                            ins = dve.tensor_tensor(X[:, g], G[0:64, g, :, 0:64], wide_i, ALU.add)
                        ins.then_inc(n["g_masked"].up(), 1)
                        for j in range(ROUNDS):
                            r = c * ROUNDS + j
                            dve.wait_ge(n["squared"].sem, n["squared"].at(r + 1))
                            for g in range(2):
                                ins = dve.tensor_copy(M[:, g], bank(4 + g)[0:64, :].rearrange("p (m s) -> p m s", m=KD))
                            ins.then_inc(n["m_copied"].up(), 1)
                            dve.wait_ge(n["x_step"].sem, n["x_step"].at(r + 1))
                            for g in range(2):
                                ins = dve.tensor_tensor(X[:, g], X[:, g], bank(6 + g)[0:64, :].rearrange("p (m s) -> p m s", m=KD), ALU.add)
                            link(dve, "x_added", ins)
                        dve.wait_ge(n["rhs_ready"].sem, n["rhs_ready"].at(c + 1))
                        dve.tensor_copy(M[:, 1], bank(1)[0:64, :].rearrange("p (m s) -> p m s", m=KD)).then_inc(n["rhs_copied"].up(), 1)
                        dve.wait_ge(n["u_ready"].sem, n["u_ready"].at(c + 1))
                        dve.tensor_copy(UV[0:64, c, 1, :, :], bank(3)[0:64, :].rearrange("p (m s) -> p m s", m=KD)).then_inc(n["u_copied"].up(), 1)
                        dve.wait_ge(n["state_ready"].sem, n["state_ready"].at(c + 1))
                        new = bank(6).rearrange("p (m v) -> p m v", m=KD)
                        decay = pc[:, :, c:c + 1].broadcast_to([P, KD, HD])
                        if c:
                            step(dve.tensor_tensor(ST, ST, new, ALU.add))
                            dve.tensor_tensor(ST, ST, decay, ALU.mult).then_inc(n["state_updated"].up(), 1)
                        else:
                            dve.tensor_tensor(ST, new, decay, ALU.mult).then_inc(n["state_updated"].up(), 1)
                        dve.wait_ge(n["state_updated"].sem, n["state_updated"].at(c + 1))
                        post_a(c)
                    post_b(NCH - 1)
                    post_c(NCH - 1)
            project(2, residual=1.0)

        memK, memV = fm(8), tok(9)

        def memory_kv():
            with new_block() as block:
                got = sig("inputs_loaded")

                @block.sync
                def _(sp):
                    sp.dma_start(tok(0), d["mem"].rearrange("(t p) f -> p t f", p=P)).then_inc(got.up(16), 16)
                    sp.dma_start(mask[:], d["chunk_mask"]).then_inc(got.up(16), 16)
                    sp.wait_ge(got.sem, got.at(32))
            transpose_all([(tok(0), fm(1))])
            project_features(fm(1), memK)
            project(2, dest=lambda u, t: memV[:, t, u * COLS:(u + 1) * COLS], src=fm(1))

        def differential():
            project(6, dest=lambda u, t: tok(u // 2)[:, t, (u % 2) * COLS:(u % 2 + 1) * COLS],
                    rotary=lambda u: (8, HD, 0, DIFF_ROPE, cosd, sind, blk(3)) if u < 4 else None)
            transpose_all([(tok(0), fm(3)), (tok(1), fm(4))])

            def hs(m):
                return slice(64 * (m % 2), 64 * (m % 2) + 64)
            o = tok(5)
            attention(16, lambda m, t: [fm(3)[hs(m), m // 2, t * P:(t + 1) * P]], lambda m: [fm(4)[hs(m), m // 2, :]],
                      lambda m, kt: tok(2)[:, kt, (m // 2) * P:(m // 2 + 1) * P], P, lambda m, t: o[:, t, (m // 2) * P:(m // 2 + 1) * P],
                      HD ** -0.5, True, (blk(6), blk(7)), diff=True)
            with new_block() as block:
                sq, ms, root = sig("squares_ready"), sig("mean_square"), sig("row_root")
                o3 = blk(5).rearrange("p (a f) -> p a f", f=P)

                @block.scalar
                def _(act):
                    act.activation(blk(0), blk(5), ACT.Square).then_inc(sq.up(), 1)
                    act.wait_ge(ms.sem, ms.at(1))
                    act.activation(stat[:, 16:32], stat[:, 0:16], ACT.Sqrt).then_inc(root.up(), 1)

                @block.vector
                def _(dve):
                    dve.wait_ge(sq.sem, sq.at(1))
                    link(dve, "dve_step", dve.tensor_reduce(stat[:, 0:16], blk(0).rearrange("p (a f) -> p a f", f=P), AX, ALU.add))
                    dve.tensor_scalar(stat[:, 0:16], stat[:, 0:16], 1.0 / P, LN_EPS, ALU.mult, ALU.add).then_inc(ms.up(), 1)
                    link(dve, "dve_step", dve.tensor_scalar(stat[:, 48:49], col("subln", 0), 1.0 - LAMBDA_INIT, None, ALU.mult))
                    dve.wait_ge(root.sem, root.at(1))
                    link(dve, "dve_step", dve.reciprocal(stat[:, 32:48], stat[:, 16:32]))
                    link(dve, "dve_step", dve.tensor_tensor(o3, o3, stat[:, 32:48].rearrange("p (a o) -> p a o", o=1).broadcast_to([P, 16, P]), ALU.mult))
            transpose_all([(o, xT)], scale=stat[:, 48:49])
            project(2, residual=ALPHA, row_src=(d["ln_g"][0], d["ln_b"][0]))
            norm("ln", LN_EPS, None)

        def cross_attention(layer):
            project_features(xT, fm(0))
            o = tok(1)
            attention(4, lambda m, t: [fm(0)[:, 2 * m + i, t * P:(t + 1) * P] for i in range(2)], lambda m: [memK[:, 2 * m + i, :] for i in range(2)],
                      lambda m, kt: memV[:, kt, m * 256:(m + 1) * 256], 256, lambda m, t: o[:, t, m * 256:(m + 1) * 256],
                      256 ** -0.5, False, (blk(6), blk(7)))
            transpose_all([(o, xT)])
            project(2, residual=ALPHA, row_src=(d["ln_g"][3 * layer + 1], d["ln_b"][3 * layer + 1]))
            norm("ln", LN_EPS, None)

        def mixture(layer, store=None):
            rowsE = arena[:, 3:5, :].rearrange("p a f -> p (a f)").rearrange("p (e s) -> p e s", e=N_EXPERTS)
            w = blk(0)
            lg, key = w[:, 0:40].rearrange("p (t n) -> p t n", t=T), w[:, 40:48].rearrange("p (t n) -> p t n", t=T)
            gsel, es = w[:, 48:56].rearrange("p (t n) -> p t n", t=T), w[:, 56:64].rearrange("p (t n) -> p t n", t=T)
            eg = w[:, 64:96].rearrange("p (t e g) -> p t e g", t=T, e=4)
            oh1, oh2 = w[:, 96:104].rearrange("p (t n) -> p t n", t=T), w[:, 104:112].rearrange("p (t n) -> p t n", t=T)
            es2, gexp = w[:, 112:120].rearrange("p (t n) -> p t n", t=T), w[:, 120:128].rearrange("p (t n) -> p t n", t=T)
            gmx, kmx, m1, m2 = w[:, 128:130], w[:, 130:132], w[:, 132:134], w[:, 134:136]
            gsum, dm, de, den = w[:, 136:138], w[:, 138:140], w[:, 140:142], w[:, 142:144]
            w1, w2, tmp = w[:, 144:146], w[:, 146:148], w[:, 148:156].rearrange("p (t n) -> p t n", t=T)
            comb = w[:, 160:192].rearrange("p (t g e) -> p t g e", t=T, g=4)
            bias, rank = w[:, 192:212], w[:, 212:216]
            with new_block() as block:
                got, mm, e_in, e_out, rt, ev = sig("small_loaded"), sig("product_ready"), sig("max_ready"), sig("exps_ready"), sig("normed"), sig("act_evacuated")

                @block.sync
                def _(sp):
                    sp.dma_start(bias, d["route_b"][layer].rearrange("(o f) -> o f", o=1).broadcast_to([P, ROUTE])).then_inc(got.up(16), 16)
                    sp.dma_start(rank, d["rank"].rearrange("(o f) -> o f", o=1).broadcast_to([P, 4])).then_inc(got.up(16), 16)

                @block.tensor
                def _(pe):
                    for t in range(T):
                        for k in range(KD):
                            last = pe.matmul(bank(0)[:, t * ROUTE:(t + 1) * ROUTE], xT[:, k, t * P:(t + 1) * P], col("route", (layer * KD + k) * ROUTE, ROUTE),
                                             start=(k == 0), stop=(k == KD - 1))
                    last.then_inc(mm.up(), 1)
                    pe.wait_ge(rt.sem, rt.at(1))
                    for e in range(N_EXPERTS):
                        b = 1 + (e // 2) % 4
                        if e >= 8 and e % 2 == 0:
                            pe.wait_ge(ev.sem, ev.at(e // 2 - 3))
                        for t in range(T):
                            c = comb[:, t, e // 4, e % 4:e % 4 + 1].broadcast_to([P, P])
                            last = pe.matmul(bank(b)[:, ((e % 2) * T + t) * P:((e % 2) * T + t + 1) * P], c, ident[:], start=True, stop=True)
                        if e % 2:
                            last.then_inc(mm.up(), 1)

                @block.scalar
                def _(act):
                    act.wait_ge(e_in.sem, e_in.at(1))
                    act.activation(gexp, gexp, ACT.Exp).then_inc(e_out.up(), 1)
                    act.wait_ge(e_in.sem, e_in.at(2))
                    act.activation(de, dm, ACT.Exp).then_inc(e_out.up(), 1)
                    for n in range(N_EXPERTS // 2):
                        act.wait_ge(mm.sem, mm.at(n + 2))
                        act.copy(rowsE[:, 2 * n:2 * n + 2, :], bank(1 + n % 4).rearrange("p (e s) -> p e s", e=2)).then_inc(ev.up(), 1)

                @block.vector
                def _(dve):
                    def step(ins):
                        link(dve, "dve_step", ins)

                    def w4(x):
                        return x.rearrange("p (t o) -> p t o", o=1).broadcast_to([P, T, 4])

                    wr = rank.rearrange("p (o n) -> p o n", o=1).broadcast_to([P, T, 4])

                    def first_max(x, m, onehot):
                        step(dve.tensor_reduce(m, x, AX, ALU.max))
                        step(dve.tensor_tensor(key, x, w4(m), ALU.is_equal))
                        step(dve.tensor_tensor(key, key, wr, ALU.mult))
                        step(dve.tensor_reduce(kmx, key, AX, ALU.max))
                        step(dve.tensor_tensor(onehot, key, w4(kmx), ALU.is_equal))

                    dve.wait_ge(mm.sem, mm.at(1))
                    dve.wait_ge(got.sem, got.at(32))
                    step(dve.tensor_tensor(lg, bank(0)[:, 0:T * ROUTE].rearrange("p (t n) -> p t n", t=T), bias.rearrange("p (o n) -> p o n", o=1).broadcast_to([P, T, ROUTE]), ALU.add))
                    first_max(lg[:, :, 0:4], gmx, gsel)
                    dve.tensor_tensor(gexp, lg[:, :, 0:4], w4(gmx), ALU.subtract).then_inc(e_in.up(), 1)
                    for t in range(T):
                        el = lg[:, t, 4:ROUTE].rearrange("p (g e) -> p e g", g=4)
                        ins = dve.tensor_tensor(eg[:, t], el, gsel[:, t:t + 1, :].broadcast_to([P, 4, 4]), ALU.mult)
                    step(ins)
                    step(dve.tensor_reduce(es, eg, AX, ALU.add))
                    first_max(es, m1, oh1)
                    step(dve.scalar_tensor_tensor(es2, oh1, MASKED, es, ALU.mult, ALU.add))
                    first_max(es2, m2, oh2)
                    dve.tensor_tensor(dm, m2, m1, ALU.subtract).then_inc(e_in.up(), 1)
                    dve.wait_ge(e_out.sem, e_out.at(2))
                    step(dve.tensor_reduce(gsum, gexp, AX, ALU.add))
                    step(dve.tensor_scalar(den, de, 1.0, None, ALU.add))
                    step(dve.tensor_tensor(den, den, gsum, ALU.mult))
                    step(dve.reciprocal(w1, den))
                    step(dve.tensor_tensor(w2, w1, de, ALU.mult))
                    step(dve.tensor_tensor(oh1, oh1, w4(w1), ALU.mult))
                    step(dve.tensor_tensor(oh2, oh2, w4(w2), ALU.mult))
                    step(dve.tensor_tensor(tmp, oh1, oh2, ALU.add))
                    for t in range(T):
                        g = gsel[:, t, :].rearrange("p (g o) -> p g o", o=1).broadcast_to([P, 4, 4])
                        ins = dve.tensor_tensor(comb[:, t], tmp[:, t:t + 1, :].broadcast_to([P, 4, 4]), g, ALU.mult)
                    ins.then_inc(rt.up(), 1)
            ffn_stage(EU, layer, expert_rows=rowsE, row_src=(d["ln_g"][3 * layer + 2], d["ln_b"][3 * layer + 2]), residual=ALPHA)
            norm("ln", LN_EPS, None, store=store)

        def sparse_mla():
            cin = arena[:, 0:2, :].rearrange("p a f -> p (a f)")[:, 0:T * 640].rearrange("p (t f) -> p t f", t=T)
            kpad = blk(1)[:, 1024:2048].rearrange("p (t a f) -> p t a f", t=T, a=4)
            cT = blk(2)[:, 0:1024].rearrange("p (k s) -> p k s", k=4)
            kiT = blk(2)[:, 1024:1280]
            q_tok, qi_tok, v_tok = tok(3), tok(4), tok(5)
            qT, kT, qiT = fm(6), fm(7), xT
            j0 = next_unit(1)
            with new_block() as block:
                mm, ev, dv = sig("product_ready"), sig("act_evacuated"), sig("dve_evacuated")
                sq, ms, root, ready, tp = sig("row_stats"), sig("mean_square"), sig("row_root"), sig("normed"), sig("transposed")
                ss = stat[:, 0:4].rearrange("p (t a) -> p t a", t=T)
                halves = (0, B_IN // 2, B_IN)

                @block.tensor
                def _(pe):
                    arrived(pe, j0)
                    w = ring[:, j0 % SLOTS, 0:KD * B_IN].rearrange("p (k n) -> p k n", k=KD)
                    for t in range(T):
                        for c in range(2):
                            for k in range(KD):
                                last = pe.matmul(bank(2 * t + c)[:, 0:B_IN // 2], xT[:, k, t * P:(t + 1) * P], w[:, k, halves[c]:halves[c + 1]], start=(k == 0), stop=(k == KD - 1))
                            last.then_inc(mm.up(), 1)
                    unit_done(j0, mm)
                    for t in range(T):
                        pe.wait_ge(ready.sem, ready.at(t + 1))
                        for k in range(4):
                            last = pe.transpose(bank(4 + t)[:, k * P:(k + 1) * P], cin[:, t, k * P:(k + 1) * P], ident[:])
                        last.then_inc(tp.up(), 1)
                    pe.wait_ge(ready.sem, ready.at(T + 1))
                    for a in range(2):
                        for t in range(T):
                            last = pe.transpose(bank(6)[:, (a * T + t) * P:(a * T + t + 1) * P], kpad[:, t, a, :], ident[:])
                    last.then_inc(tp.up(), 1)

                @block.scalar
                def _(act):
                    for t in range(T):
                        for c in range(2):
                            act.wait_ge(mm.sem, mm.at(2 * t + c + 1))
                            act.copy(cin[:, t, halves[c]:halves[c + 1]], bank(2 * t + c)[:, 0:B_IN // 2]).then_inc(ev.up(), 1)
                    act.wait_ge(ev.sem, ev.at(4))
                    for t in range(T):
                        for a in range(2):
                            act.activation(blk(3)[:, (2 * t + a) * 256:(2 * t + a + 1) * 256], cin[:, t, a * 256:(a + 1) * 256], ACT.Square, accum_out=ss[:, t, a:a + 1]).then_inc(sq.up(), 1)
                    act.wait_ge(ms.sem, ms.at(1))
                    act.activation(stat[:, 8:12], stat[:, 4:8], ACT.Sqrt).then_inc(root.up(), 1)
                    act.wait_ge(tp.sem, tp.at(T + 1))
                    for hd in range(KD):
                        act.copy(kT[96:128, hd, :], bank(6)[96:128, 0:SEQ])
                    act.copy(kiT, bank(6)[:, SEQ:2 * SEQ])

                @block.vector
                def _(dve):
                    def step(ins):
                        link(dve, "dve_step", ins)
                    step(dve.memset(kpad, 0.0))
                    dve.wait_ge(sq.sem, sq.at(4))
                    dve.tensor_scalar(stat[:, 4:8], stat[:, 0:4], 1.0 / Q_RANK, LN_EPS, ALU.mult, ALU.add).then_inc(ms.up(), 1)
                    dve.wait_ge(root.sem, root.at(1))
                    step(dve.reciprocal(stat[:, 12:16], stat[:, 8:12]))
                    for t in range(T):
                        for a in range(2):
                            x = cin[:, t, a * 256:(a + 1) * 256]
                            ins = dve.tensor_scalar(x, x, stat[:, 12 + 2 * t + a:13 + 2 * t + a], None, ALU.mult)
                        ins.then_inc(ready.up(), 1)
                    tmp = blk(3)[:, 1024:1536]
                    r0 = Q_RANK + KV_RANK
                    for t in range(T):
                        step(rope(dve, cin[:, t, r0:r0 + 32], 1, 32, 0, MLA_ROPE, cosr[:, t, :], sinr[:, t, :], tmp))
                        step(rope(dve, cin[:, t, r0 + 32:r0 + 96], 1, 64, 0, DIFF_ROPE, cosd[:, t, :], sind[:, t, :], tmp))
                        dve.tensor_copy(kpad[:, t, 0, 96:128], cin[:, t, r0:r0 + 32])
                        for a in range(2):
                            ins = dve.tensor_copy(kpad[:, t, 1, a * 64:(a + 1) * 64], cin[:, t, r0 + 32:r0 + 96])
                        step(ins)
                        x = cin[:, t, r0 + 96:r0 + 112]
                        step(dve.tensor_scalar(x, x, (IDX_HEADS * IDX_DIM) ** -0.5, None, ALU.mult))
                    dve.tensor_scalar(kpad[:, 0, 2, 0:1], kpad[:, 0, 2, 0:1], 1.0, None, ALU.mult).then_inc(ready.up(), 1)
                    for t in range(T):
                        dve.wait_ge(tp.sem, tp.at(t + 1))
                        for a, g in enumerate(("q_norm", "kv_norm")):
                            g3 = col(g, 0, 2).rearrange("p (k o) -> p k o", o=1).broadcast_to([P, 2, P])
                            dve.tensor_tensor(cT[:, 2 * a:2 * a + 2, t * P:(t + 1) * P], bank(4 + t)[:, a * 256:(a + 1) * 256].rearrange("p (k s) -> p k s", k=2), g3, ALU.mult)
                stream(block, 1)
            j0 = next_unit(2)
            with new_block() as block:
                mm, ev = sig("product_ready"), sig("act_evacuated")

                @block.tensor
                def _(pe):
                    n = 0
                    arrived(pe, j0)
                    w = ring[:, j0 % SLOTS, 0:4096].rearrange("p (a k n) -> p a k n", a=2, k=2)
                    for a in range(2):
                        for c in range(2):
                            for t in range(T):
                                if n >= 8:
                                    pe.wait_ge(ev.sem, ev.at(n - 7))
                                for k in range(2):
                                    last = pe.matmul(bank(n % 8), cT[:, k, t * P:(t + 1) * P], w[:, a, k, c * 512:(c + 1) * 512], start=(k == 0), stop=(k == 1))
                                last.then_inc(mm.up(), 1)
                                n += 1
                    unit_done(j0, mm)
                    arrived(pe, j0 + 1)
                    wk = ring[:, (j0 + 1) % SLOTS, 0:1536].rearrange("p (k n) -> p k n", k=2)
                    wv = ring[:, (j0 + 1) % SLOTS, 1536:3584].rearrange("p (k n) -> p k n", k=2)
                    for hd in range(KD):
                        if hd % 2 == 0:
                            pe.wait_ge(ev.sem, ev.at(n - 7))
                        for k in range(2):
                            last = pe.matmul(bank(n % 8)[0:MLA_NOPE, (hd % 2) * SEQ:(hd % 2 + 1) * SEQ], wk[:, k, hd * MLA_NOPE:(hd + 1) * MLA_NOPE], cT[:, 2 + k, :], start=(k == 0), stop=(k == 1))
                        if hd % 2:
                            last.then_inc(mm.up(), 1)
                            n += 1
                    for c in range(2):
                        for t in range(T):
                            pe.wait_ge(ev.sem, ev.at(n - 7))
                            for k in range(2):
                                last = pe.matmul(bank(n % 8), cT[:, 2 + k, t * P:(t + 1) * P], wv[:, k, c * 512:(c + 1) * 512], start=(k == 0), stop=(k == 1))
                            last.then_inc(mm.up(), 1)
                            n += 1
                    unit_done(j0 + 1, mm)
                stream(block, 2)

                @block.scalar
                def _(act):
                    n = 0
                    for a in (q_tok, qi_tok):
                        for c in range(2):
                            for t in range(T):
                                act.wait_ge(mm.sem, mm.at(n + 1))
                                act.copy(a[:, t, c * 512:(c + 1) * 512], bank(n % 8)).then_inc(ev.up(), 1)
                                n += 1
                    for hd in range(0, KD, 2):
                        act.wait_ge(mm.sem, mm.at(n + 1))
                        act.copy(kT[0:96, hd:hd + 2, :], bank(n % 8)[0:96, :].rearrange("p (a s) -> p a s", a=2)).then_inc(ev.up(), 1)
                        n += 1
                    for c in range(2):
                        for t in range(T):
                            act.wait_ge(mm.sem, mm.at(n + 1))
                            act.copy(v_tok[:, t, c * 512:(c + 1) * 512], bank(n % 8)).then_inc(ev.up(), 1)
                            n += 1

                @block.vector
                def _(dve):
                    tmp = blk(2)[:, 1280:2048]
                    for t in range(T):
                        dve.wait_ge(ev.sem, ev.at(4))
                        link(dve, "dve_step", rope(dve, q_tok[:, t, :], 8, P, MLA_NOPE, MLA_ROPE, cosr[:, t, :], sinr[:, t, :], tmp))
                    for t in range(T):
                        dve.wait_ge(ev.sem, ev.at(8))
                        link(dve, "dve_step", rope(dve, qi_tok[:, t, :], 16, IDX_DIM, 0, DIFF_ROPE, cosd[:, t, :], sind[:, t, :], tmp))
            transpose_all([(q_tok, qT), (qi_tok, qiT)])
            score, left, relu = (blk(3)[:, a:a + 512].rearrange("p (t s) -> p t s", t=T) for a in (0, 512, 1024))
            relus = blk(3)[:, 1024:2048].rearrange("p (b t s) -> p b t s", b=2, t=T)
            top8 = stat[:, 0:16].rearrange("p (t n) -> p t n", t=T)
            with new_block() as block:
                mm, ev, dv = sig("product_ready"), sig("act_evacuated"), sig("dve_evacuated")

                @block.tensor
                def _(pe):
                    for i in range(IDX_HEADS):
                        hs = slice(64 * (i % 2), 64 * (i % 2) + 64)
                        if i >= 2:
                            pe.wait_ge(ev.sem, ev.at(i - 1))
                        for t in range(T):
                            last = pe.matmul(bank(i % 2)[:, t * SEQ:(t + 1) * SEQ], qiT[hs, i // 2, t * P:(t + 1) * P], kiT[hs, :], start=True, stop=True)
                        last.then_inc(mm.up(), 1)

                @block.scalar
                def _(act):
                    for i in range(IDX_HEADS):
                        act.wait_ge(mm.sem, mm.at(i + 1))
                        if i >= 2:
                            act.wait_ge(dv.sem, dv.at(T * (i - 1)))
                        act.activation(relus[:, i % 2], bank(i % 2).rearrange("p (t s) -> p t s", t=T), ACT.Relu).then_inc(ev.up(), 1)

                @block.vector
                def _(dve):
                    w0 = Q_RANK + KV_RANK + MLA_ROPE + IDX_DIM
                    for i in range(IDX_HEADS):
                        dve.wait_ge(ev.sem, ev.at(i + 1))
                        for t in range(T):
                            if i:
                                dve.wait_ge(dv.sem, dv.at(T * (i - 1) + t + 1))
                            wi = cin[:, t, w0 + i:w0 + i + 1]
                            if i == 0:
                                dve.tensor_scalar(score[:, t, :], relus[:, 0, t, :], wi, None, ALU.mult).then_inc(dv.up(), 1)
                            else:
                                dve.scalar_tensor_tensor(score[:, t, :], relus[:, i % 2, t, :], wi, score[:, t, :], ALU.mult, ALU.add).then_inc(dv.up(), 1)
                    dve.wait_ge(dv.sem, dv.at(T * IDX_HEADS))
                    link(dve, "dve_step", dve.tensor_tensor(left, score, mask[:], ALU.add))
                    for _ in range(TOPK // 8):
                        for t in range(T):
                            ins = dve.max(top8[:, t, :], left[:, t, :])
                        link(dve, "dve_step", ins)
                        for t in range(T):
                            ins = dve.match_replace(left[:, t, :], top8[:, t, :], left[:, t, :], TAKEN)
                        link(dve, "dve_step", ins)
                    dve.tensor_scalar(mask[:], left, TAKEN / 2, MASKED, ALU.is_gt, ALU.mult)
            attention(KD, lambda m, t: [qT[:, m, t * P:(t + 1) * P]], lambda m: [kT[:, m, :]], lambda m, kt: v_tok[:, kt, m * P:(m + 1) * P], P,
                      lambda m, t: tok(4)[:, t, m * P:(m + 1) * P], (MLA_ROPE + MLA_NOPE) ** -0.5, True, (blk(0), blk(1)))
            transpose_all([(tok(4), xT)])
            project(2, residual=ALPHA, row_src=(d["ln_g"][3], d["ln_b"][3]))
            norm("ln", LN_EPS, None)

        first_attention()
        norm("rms", RMS_EPS, tok(0), gains=col("norm_ffn", 0, KD))
        ffn_stage(FU, 0)
        rwkv()
        norm("rms", RMS_EPS, tok(0), gains=col("norm_ffn", KD, KD))
        ffn_stage(FU, 1, row_src=(d["norm_final"],))
        norm("rms_rows", RMS_EPS, tok(0))
        memory_kv()
        differential()
        cross_attention(0)
        mixture(0)
        sparse_mla()
        cross_attention(1)
        mixture(1, store=out)


def _units(w, width):
    k, n = w.shape
    return w.reshape(k // P, P, n // width, width).transpose(2, 1, 0, 3).reshape(n // width, P, k // P * width)


def _ffn_units(gate, up, down):
    n = gate.shape[1] // (2 * P)
    dn = down.reshape(n, 2, P, D).transpose(0, 2, 1, 3).reshape(n, P, 2 * D)
    return np.concatenate([_units(gate, 2 * P), _units(up, 2 * P), dn], axis=2)


def _features(v):
    return v.reshape(-1, P).T


def _rows(w):
    return w.reshape(-1, P, w.shape[-1]).transpose(1, 0, 2).reshape(P, -1)


def _constants():
    f = np.float32
    pos = np.arange(SEQ, dtype=f)
    e0 = np.arange(0, HD, 2, dtype=f) / f(HD)
    inv0 = f(1) / (10000.0 ** e0.astype(np.float64)).astype(f)
    ang = (pos[:, None] * inv0[None, :]).astype(np.float64)
    c, s = np.cos(ang).astype(f), np.sin(ang).astype(f)

    def by_token(a):
        return np.ascontiguousarray(a.reshape(T, P, -1).transpose(1, 0, 2))

    def inv(rot):
        e = np.arange(0, rot, 2, dtype=f) / f(rot)
        return (500000.0 ** (-e.astype(np.float64))).astype(f)
    i = np.arange(SEQ)
    head = np.arange(D) // HD
    onehot = (head[:, None] == np.arange(HEADS)[None, :]).astype(f)
    s_, t_ = np.arange(CHUNK)[:, None], np.arange(CHUNK)[None, :]
    before, upto = (s_ < t_).astype(f), (s_ <= t_).astype(f)
    return {
        "ident": np.eye(P, dtype=f),
        "causal": by_token(np.where(i[None, :] <= i[:, None], 0, MASKED).astype(f)),
        "chunk_mask": by_token(np.where(i[None, :] // CHUNK <= i[:, None] // CHUNK, 0, MASKED).astype(f)),
        "cos0": by_token(np.concatenate([c, c], 1)), "sin0": by_token(np.concatenate([-s, s], 1)),
        "inv": np.concatenate([inv(DIFF_ROPE), inv(MLA_ROPE)]),
        "spread": np.ascontiguousarray(onehot.T.reshape(HEADS, KD, P)), "heads16": np.ascontiguousarray(onehot.reshape(KD, P, HEADS).transpose(1, 0, 2)),
        "pair": np.ascontiguousarray(onehot[0:P, 0:2]), "reset": np.tile((np.arange(SEQ) % CHUNK != 0).astype(f), (P, 1)),
        "gmask": np.tile(np.concatenate([before, upto], 1), (2, 1)), "lmask": np.ascontiguousarray(before.T),
        "rank": np.array([4, 3, 2, 1], f),
    }


def _pack(a):
    cols = np.concatenate([_features(a["norm_mix"]), _features(a["norm_ffn"]), _features(a["rwkv_mu"]), _features(a["rwkv_w0"]), _features(a["rwkv_a0"]),
                           _features(a["rwkv_k_k"]), _features(a["rwkv_k_a"]), _features(a["rwkv_r_k"].reshape(-1)), _features(a["ffn_conv_w"]),
                           _features(a["ffn_conv_b"]), _features(a["a_subln_g_2"]), _features(a["b_q_norm_g_2"]), _features(a["b_kv_norm_g_2"]),
                           *[_rows(np.concatenate([a["moe_w_group_2"][i], a["moe_w_expert_2"][i]], 1)) for i in range(2)]], axis=1)
    rkv = a["rwkv_w_rkv"][0]
    w_proj = np.concatenate([_units(w, COLS) for w in (
        a["attn_w_qkv"][0], a["attn_w_o"][0], rkv[0], rkv[1], rkv[2], a["rwkv_w_o"][0], a["mem_w_kv_2"], a["a_w_in_2"][0], a["a_w_out_2"][0],
        a["xa_w_q_2"][0], a["xa_w_out_2"][0], a["b_w_out_2"][0], a["xa_w_q_2"][1], a["xa_w_out_2"][1])])
    z = np.zeros((P - 64, D), np.float32)
    lora = np.concatenate([_rows(a["rwkv_w1"][0]), _rows(a["rwkv_a1"][0]), _rows(a["rwkv_g1"][0]), np.concatenate([a["rwkv_w2"][0], z]),
                           np.concatenate([a["rwkv_a2"][0], z]), a["rwkv_g2"][0]], axis=1)
    uq = a["b_w_uq_2"][0].reshape(Q_RANK, KD, P)
    uq = np.concatenate([uq[:, :, MLA_ROPE:], uq[:, :, :MLA_ROPE]], 2).reshape(Q_RANK, D)
    uk = a["b_w_uk_2"][0].transpose(1, 0, 2).reshape(KV_RANK, -1)
    uv = a["b_w_uv_2"][0].transpose(1, 0, 2).reshape(KV_RANK, -1)

    moe = np.concatenate([_ffn_units(a["moe_w_gate_2"][l, e], a["moe_w_up_2"][l, e], a["moe_w_down_2"][l, e]) for l in range(2) for e in range(N_EXPERTS)])
    arrays = {
        "x": a["x"][0], "mem": a["mem_2"][0], "pos": a["positions_2"].reshape(T, P).T, "cols": cols, "w_proj": w_proj, "w_lora": lora,
        "w_ffn": np.concatenate([_ffn_units(a["ffn_w_gate"][i], a["ffn_w_up"][i], a["ffn_w_down"][i]) for i in range(2)]), "w_moe": moe,
        "w_b_in": _rows(a["b_w_in_2"][0]), "w_uq": np.concatenate([_rows(uq), _rows(a["b_w_qidx_2"][0])], 1), "w_ukv": np.concatenate([_rows(uk), _rows(uv)], 1),
        "lam": a["a_lambda_2"][0].reshape(-1), "ln_g": a["ln_g_2"].reshape(6, D), "ln_b": a["ln_b_2"].reshape(6, D), "norm_final": a["norm_final"],
        "lnx_w": a["rwkv_lnx_w"][0], "lnx_b": a["rwkv_lnx_b"][0],
        "route_b": np.concatenate([a["moe_b_group_2"], a["moe_b_expert_2"]], 1),
    }
    return {k: np.ascontiguousarray(v) for k, v in arrays.items()} | _constants()


def kernel(**inputs):
    import concourse.bacc as bacc
    from concourse.bass_utils import run_bass_kernel_spmd as run

    arrays = _pack({k: np.asarray(v) for k, v in inputs.items()})
    nc = bacc.Bacc("TRN2", target_bir_lowering=False, num_devices=1)
    d = {n: nc.dram_tensor(f"in_{n}", v.shape, mybir.dt.from_np(v.dtype), kind="ExternalInput").ap() for n, v in arrays.items()}
    out = nc.dram_tensor("out_0", (SEQ, D), F32, kind="ExternalOutput").ap()
    build_program(nc, d, out)
    r = run(nc, [{f"in_{n}": v for n, v in arrays.items()}], core_ids=[0])
    return r.results[0]["out_0"].reshape(1, SEQ, D)
```

```python
import math
from contextlib import ExitStack

import numpy as np
import concourse.bass as bass
from concourse import mybir

F32 = mybir.dt.float32
I32 = mybir.dt.int32
ALU = mybir.AluOpType
ACT = mybir.ActivationFunctionType
AX = mybir.AxisListType.X

P = 128
SEQ = 256
D = 1024
T = SEQ // P
KD = D // P
COLS = 512
F_FF = ((8 * D // 3 + 127) // 128) * 128
FT = F_FF // P
FU = FT // 2
N_EXPERTS, N_GROUPS, PER_GROUP, EXPERT_FF = 16, 4, 4, 512
EU = N_EXPERTS * EXPERT_FF // (2 * P)
EPG = 4
SLOTS_E = 64
PAIRS = N_EXPERTS // 2
UNIT = 2 * KD * 2 * P + 2 * D
SLOTS = 4
CHUNK = 64
NCH = SEQ // CHUNK
HEADS, HD = 16, 64
ALPHA = 4.0 ** 0.25
LN_EPS, RMS_EPS, LNX_EPS = 1e-5, 1e-6, 64e-5
DECAY = -math.exp(-0.5)
LAMBDA_INIT = 0.8 - 0.6 * math.exp(-0.3 * 0)
MASKED = -1e30
TAKEN = -3e38
TOPK = min(256, SEQ // 4)
Q_RANK, KV_RANK, MLA_ROPE, MLA_NOPE, IDX_DIM, IDX_HEADS = 256, 256, 32, 96, 64, 16
B_IN = Q_RANK + KV_RANK + MLA_ROPE + IDX_DIM + IDX_HEADS
DIFF_ROPE = 16
ROUTE = N_GROUPS + N_EXPERTS
BLK = 2048

_COLS = [("norm_mix", 2 * KD), ("norm_ffn", 2 * KD), ("mu", 6 * KD), ("w0", KD), ("a0", KD), ("k_k", KD),
         ("k_a", KD), ("r_k", KD), ("conv_w", 2 * 3 * FT), ("conv_b", 2 * FT), ("subln", 1),
         ("q_norm", 2), ("kv_norm", 2), ("route", 2 * KD * ROUTE)]
COL, _at = {}, 0
for _n, _w in _COLS:
    COL[_n] = _at
    _at += _w
N_COLS = _at


class Signal:

    def __init__(self, sem):
        self.sem, self.base, self.count = sem, 0, 0

    def up(self, step=1, runs=1):
        self.count += step * runs
        return self.sem

    def at(self, n):
        return self.base + n


def build_program(nc, d, out):
    with ExitStack() as ctx:
        def sb(name, shape, dt=F32):
            return ctx.enter_context(nc.sbuf_tensor(name, shape, dt))

        ring = sb("ring", [P, SLOTS, UNIT])
        arena = sb("arena", [P, 10, BLK])
        h = sb("h", [P, T, D])
        xT = sb("xT", [P, KD, SEQ])
        rows = sb("rows", [P, 2, D])
        ident = sb("ident", [P, P])
        cols = sb("cols", [P, N_COLS])
        mask = sb("mask", [P, T, SEQ])
        cos0, sin0 = sb("cos0", [P, T, HD]), sb("sin0", [P, T, HD])
        cosd, sind = sb("cosd", [P, T, DIFF_ROPE]), sb("sind", [P, T, DIFF_ROPE])
        cosr, sinr = sb("cosr", [P, T, MLA_ROPE]), sb("sinr", [P, T, MLA_ROPE])
        stat = sb("stat", [P, 128])
        overflow = sb("overflow", [P, 1], I32)
        nlam = sb("nlam", [P, 1])
        ps = ctx.enter_context(nc.psum_tensor("ps", [P, 8, 512], F32))

        def bank(b):
            return ps[:, b, :]

        def blk(i):
            return arena[:, i, :]

        def tok(i):
            return arena[:, i, :].rearrange("p (t f) -> p t f", t=T)

        def fm(i):
            return arena[:, i, :].rearrange("p (k s) -> p k s", k=KD)

        def col(name, i, n=1):
            return cols[:, COL[name] + i:COL[name] + i + n]

        signals = {}

        def sig(name):
            if name not in signals:
                signals[name] = Signal(ctx.enter_context(nc.semaphore(name)))
            return signals[name]

        def new_block():
            for s in signals.values():
                s.base = s.count
            return nc.Block(no_gpsimd_drain=True)

        def link(eng, name, ins, step=1):
            s = sig(name)
            ins.then_inc(s.up(step), step)
            eng.wait_ge(s.sem, s.count)

        proj, ffn, moe = d["w_proj"], d["w_ffn"], d["w_moe"]
        n_proj = [0]

        def take(n):
            n_proj[0] += n
            return [proj[n_proj[0] - n + i] for i in range(n)]

        loads = take(6) + take(2)
        loads += [ffn[i] for i in range(FU)]
        loads += take(6) + [d["w_lora"]] + take(2)
        loads += [ffn[FU + i] for i in range(FU)]
        loads += take(4) + take(6) + take(2)
        loads += take(4)
        moe_at = [len(loads)]
        loads += [moe[i] for i in range(EU)]
        loads += [d["w_b_in"], d["w_uq"], d["w_ukv"]] + take(2) + take(4)
        moe_at.append(len(loads))
        loads += [moe[EU + i] for i in range(EU)]
        loaded = [sig(f"weights_loaded{s}") for s in range(SLOTS)]
        pos = {"issued": 0, "unit": 0}
        release = {}

        def load(sp, j):
            if j >= SLOTS:
                sem, value = release[j - SLOTS]
                sp.wait_ge(sem, value)
            w = loads[j].shape[-1]
            sp.dma_start(ring[:, j % SLOTS, 0:w], loads[j]).then_inc(loaded[j % SLOTS].up(16), 16)

        def stream(block, n):
            first = pos["issued"]
            last = min(first + n, len(loads))
            pos["issued"] = last

            @block.sync
            def _(sp):
                for j in range(first, last):
                    load(sp, j)

        def arrived(pe, j):
            pe.wait_ge(loaded[j % SLOTS].sem, 16 * (j // SLOTS + 1))

        def unit_done(j, signal):
            release[j] = signal.sem, signal.count

        def next_unit(n=1):
            pos["unit"] += n
            return pos["unit"] - n

        def norm(kind, eps, xn, gains=None, store=None):
            src = xn if kind == "rms" else h
            with new_block() as block:
                sq_done, ms_ready, root, ready = sig("row_stats"), sig("mean_square"), sig("row_root"), sig("normed")
                tp, rows_in = sig("transposed"), sig("rows_loaded")
                ss, ms, std, rstd = stat[:, 0:2], stat[:, 2:4], stat[:, 4:6], stat[:, 6:8]
                bn, mv = stat[:, 8:32].rearrange("p (t c s) -> p t c s", t=T, c=2), stat[:, 32:36].rearrange("p (t s) -> p t s", t=T)

                @block.scalar
                def _(act):
                    if kind != "ln":
                        for t in range(T):
                            act.activation(xn[:, t, :], h[:, t, :], ACT.Square, accum_out=ss[:, t:t + 1]).then_inc(sq_done.up(), 1)
                    act.wait_ge(ms_ready.sem, ms_ready.at(1))
                    act.activation(std, ms, ACT.Sqrt).then_inc(root.up(), 1)
                    if gains is None:
                        for t in range(T):
                            act.wait_ge(tp.sem, tp.at(2 * t + 1))
                            act.copy(xT[:, 0:4, t * P:(t + 1) * P], bank(2 * t).rearrange("p (k s) -> p k s", k=4))

                @block.vector
                def _(dve):
                    if kind == "ln":
                        for t in range(T):
                            for c in range(2):
                                link(dve, "dve_step", dve.bn_stats(bn[:, t, c, :], h[:, t, c * 512:(c + 1) * 512]))
                            link(dve, "dve_step", dve.bn_aggr(mv[:, t, :], bn[:, t, :, :]))
                        dve.tensor_scalar(ms, mv[:, :, 1], eps, None, ALU.add).then_inc(ms_ready.up(), 1)
                    else:
                        dve.wait_ge(sq_done.sem, sq_done.at(T))
                        dve.tensor_scalar(ms, ss, 1.0 / D, eps, ALU.mult, ALU.add).then_inc(ms_ready.up(), 1)
                    dve.wait_ge(root.sem, root.at(1))
                    link(dve, "dve_step", dve.reciprocal(rstd, std))
                    for t in range(T):
                        if kind == "rms":
                            dve.tensor_scalar(xn[:, t, :], h[:, t, :], rstd[:, t:t + 1], None, ALU.mult).then_inc(ready.up(), 1)
                        elif kind == "rms_rows":
                            dve.wait_ge(rows_in.sem, rows_in.count)
                            dve.scalar_tensor_tensor(h[:, t, :], h[:, t, :], rstd[:, t:t + 1], rows[:, 0, :], ALU.mult, ALU.mult).then_inc(ready.up(), 1)
                        else:
                            dve.wait_ge(rows_in.sem, rows_in.count)
                            link(dve, "dve_step", dve.tensor_scalar(h[:, t, :], h[:, t, :], mv[:, t, 0:1], rstd[:, t:t + 1], ALU.subtract, ALU.mult))
                            link(dve, "dve_step", dve.tensor_tensor(h[:, t, :], h[:, t, :], rows[:, 0, :], ALU.mult))
                            dve.tensor_tensor(h[:, t, :], h[:, t, :], rows[:, 1, :], ALU.add).then_inc(ready.up(), 1)
                    for t in range(T):
                        for f in range(2):
                            if gains is None and f == 0:
                                continue
                            dve.wait_ge(tp.sem, tp.at(2 * t + f + 1))
                            o, i = xT[:, 4 * f:4 * f + 4, t * P:(t + 1) * P], bank(2 * t + f).rearrange("p (k s) -> p k s", k=4)
                            if gains is None:
                                dve.tensor_copy(o, i)
                            else:
                                g = gains[:, 4 * f:4 * f + 4].rearrange("p (k o) -> p k o", o=1).broadcast_to([P, 4, P])
                                dve.tensor_tensor(o, i, g, ALU.mult)

                @block.tensor
                def _(pe):
                    for t in range(T):
                        pe.wait_ge(ready.sem, ready.at(t + 1))
                        for f in range(2):
                            for k in range(4):
                                c = (4 * f + k) * P
                                last = pe.transpose(bank(2 * t + f)[:, k * P:(k + 1) * P], src[:, t, c:c + P], ident[:])
                            last.then_inc(tp.up(), 1)

                if store is not None:
                    @block.sync
                    def _(sp):
                        sp.wait_ge(ready.sem, ready.at(T))
                        stored = sig("stored")
                        sp.dma_start(store.rearrange("(t p) f -> p t f", p=P), h[:]).then_inc(stored.up(16), 16)
                        sp.wait_ge(stored.sem, stored.at(16))

        def transpose_all(pairs, scale=None):
            with new_block() as block:
                tp, free = sig("transposed"), [sig("act_evacuated"), sig("dve_evacuated")]
                jobs = [(s, o, t, f) for s, o in pairs for t in range(T) for f in range(2)]

                @block.tensor
                def _(pe):
                    for n, (s, o, t, f) in enumerate(jobs):
                        if n >= 8:
                            pe.wait_ge(free[n % 2].sem, free[n % 2].at(n // 2 - 3))
                        for k in range(4):
                            c = (4 * f + k) * P
                            last = pe.transpose(bank(n % 8)[:, k * P:(k + 1) * P], s[:, t, c:c + P], ident[:])
                        last.then_inc(tp.up(), 1)

                def evacuate(e):
                    def body(eng):
                        for n, (s, o, t, f) in enumerate(jobs):
                            if n % 2 != e:
                                continue
                            eng.wait_ge(tp.sem, tp.at(n + 1))
                            i = bank(n % 8).rearrange("p (k s) -> p k s", k=4)
                            q = o[:, 4 * f:4 * f + 4, t * P:(t + 1) * P]
                            if e == 0:
                                ins = eng.copy(q, i) if scale is None else eng.activation(q, i, ACT.Copy, scale=scale)
                            else:
                                ins = eng.tensor_copy(q, i) if scale is None else eng.tensor_scalar(q, i, scale, None, ALU.mult)
                            ins.then_inc(free[e].up(), 1)
                    return body

                block.scalar(evacuate(0))
                block.vector(evacuate(1))

        def rope(dve, x, heads, dh, at, rot, cos, sin, tmp):
            half = rot // 2
            v = x.rearrange("p (a f) -> p a f", a=heads)[:, :, at:at + rot]
            a = tmp[:, 0:heads * rot].rearrange("p (a f) -> p a f", a=heads)
            b = tmp[:, heads * rot:2 * heads * rot].rearrange("p (a f) -> p a f", a=heads)

            def wide(c):
                return c.rearrange("p (o f) -> p o f", o=1).broadcast_to([P, heads, c.shape[-1]])

            dve.tensor_tensor(a, v, wide(cos), ALU.mult)
            dve.tensor_tensor(b[:, :, 0:half], v[:, :, half:rot], wide(sin[:, 0:half]), ALU.mult)
            link(dve, "dve_step", dve.tensor_tensor(b[:, :, half:rot], v[:, :, 0:half], wide(sin[:, half:rot]), ALU.mult))
            return dve.tensor_tensor(v, a, b, ALU.add)

        def project(units, dest=None, src=None, rotary=None, residual=None, row_src=()):
            src = xT if src is None else src
            j0 = next_unit(units)
            with new_block() as block:
                mm, evac, free = sig("product_ready"), sig("act_evacuated"), sig("dve_evacuated")
                rows_in = sig("rows_loaded")

                @block.tensor
                def _(pe):
                    for u in range(units):
                        arrived(pe, j0 + u)
                        w = ring[:, (j0 + u) % SLOTS, 0:KD * COLS].rearrange("p (k n) -> p k n", k=KD)
                        for t in range(T):
                            n = T * u + t
                            if n >= 4:
                                pe.wait_ge((evac if residual is None else free).sem, (evac if residual is None else free).at(n - 3))
                            for k in range(KD):
                                last = pe.matmul(bank(n % 4), src[:, k, t * P:(t + 1) * P], w[:, k, :], start=(k == 0), stop=(k == KD - 1))
                            last.then_inc(mm.up(), 1)
                        unit_done(j0 + u, mm)
                stream(block, units)

                @block.scalar
                def _(act):
                    for i, r in enumerate(row_src):
                        act.dma_start(rows[:, i, :], r.rearrange("(o f) -> o f", o=1).broadcast_to([P, D])).then_inc(rows_in.up(16), 16)
                    if residual is None:
                        for n in range(T * units):
                            act.wait_ge(mm.sem, mm.at(n + 1))
                            act.copy(dest(n // T, n % T), bank(n % 4)).then_inc(evac.up(), 1)

                @block.vector
                def _(dve):
                    for n in range(T * units):
                        u, t = n // T, n % T
                        if residual is not None:
                            dve.wait_ge(mm.sem, mm.at(n + 1))
                            x = h[:, t, u * COLS:(u + 1) * COLS]
                            dve.scalar_tensor_tensor(x, x, residual, bank(n % 4), ALU.mult, ALU.add).then_inc(free.up(), 1)
                        elif rotary is not None and rotary(u) is not None:
                            heads, dh, at, rot, cos, sin, tmp = rotary(u)
                            dve.wait_ge(evac.sem, evac.at(n + 1))
                            link(dve, "dve_step", rope(dve, dest(u, t), heads, dh, at, rot, cos[:, t, :], sin[:, t, :], tmp))

        def project_fm(pe, w, src, n, out_bank, free):
            for m in range(4):
                if m % 2 == 0 and n + m // 2 >= 4:
                    pe.wait_ge(free.sem, free.at(n + m // 2 - 3))
                for k in range(KD):
                    last = pe.matmul(bank((n + m // 2) % 4)[:, (m % 2) * SEQ:(m % 2 + 1) * SEQ], w[:, k, m * P:(m + 1) * P],
                                     src[:, k, :], start=(k == 0), stop=(k == KD - 1))
                if m % 2:
                    last.then_inc(out_bank.up(), 1)
            return last

        def project_features(src, dst, units=2):
            j0 = next_unit(units)
            with new_block() as block:
                mm, evac = sig("product_ready"), sig("act_evacuated")

                @block.tensor
                def _(pe):
                    for u in range(units):
                        arrived(pe, j0 + u)
                        w = ring[:, (j0 + u) % SLOTS, 0:KD * COLS].rearrange("p (k n) -> p k n", k=KD)
                        project_fm(pe, w, src, 2 * u, mm, evac)
                        unit_done(j0 + u, mm)
                stream(block, units)

                @block.scalar
                def _(act):
                    for n in range(2 * units):
                        act.wait_ge(mm.sem, mm.at(n + 1))
                        act.copy(dst[:, 2 * n:2 * n + 2, :], bank(n % 4).rearrange("p (m s) -> p m s", m=2)).then_inc(evac.up(), 1)

        def attention(maps, q, k, v, dv, o, scale, use_mask, work, diff=False):
            s_sb = work[0][:, 0:1024].rearrange("p (b t s) -> p b t s", b=2, t=T)
            p_sb = work[0][:, 1024:2048].rearrange("p (b t s) -> p b t s", b=2, t=T)
            pT = work[1][:, 0:1024].rearrange("p (b c s) -> p b c s", b=2, c=4)
            nmax = stat[:, 0:4].rearrange("p (b t) -> p b t", b=2)
            sums = stat[:, 4:8].rearrange("p (b t) -> p b t", b=2)
            rs = stat[:, 8:12].rearrange("p (b t) -> p b t", b=2)
            pmax = stat[:, 12:16].rearrange("p (b t) -> p b t", b=2)
            with new_block() as block:
                s_mm, p_mm, o_mm = sig("scores_ready"), sig("transposed"), sig("product_ready")
                s_out, m_ready, p_ready = sig("scores_copied"), sig("max_ready"), sig("probs_ready")
                pT_ready, o_out = sig("act_evacuated"), sig("dve_evacuated")

                @block.tensor
                def _(pe):
                    for i in range(maps + 2):
                        if i < maps:
                            if i >= 2:
                                pe.wait_ge(s_out.sem, s_out.at(i - 1))
                            for t in range(T):
                                parts = list(zip(q(i, t), k(i)))
                                for n, (a, b) in enumerate(parts):
                                    last = pe.matmul(bank(i % 2)[:, t * SEQ:(t + 1) * SEQ], a, b, start=(n == 0), stop=(n == len(parts) - 1))
                            last.then_inc(s_mm.up(), 1)
                        if 1 <= i <= maps:
                            m = i - 1
                            pe.wait_ge(p_ready.sem, p_ready.at(T * (m + 1)))
                            if m >= 2:
                                pe.wait_ge(pT_ready.sem, pT_ready.at(m - 1))
                            for c in range(4):
                                last = pe.transpose(bank(2 + m % 2)[:, c * P:(c + 1) * P], p_sb[:, m % 2, c // 2, (c % 2) * P:(c % 2 + 1) * P], ident[:])
                            last.then_inc(p_mm.up(), 1)
                        if i >= 2:
                            m = i - 2
                            pe.wait_ge(pT_ready.sem, pT_ready.at(m + 1))
                            if m >= 2:
                                pe.wait_ge(o_out.sem, o_out.at(m - 1))
                            for t in range(T):
                                for kt in range(2):
                                    last = pe.matmul(bank(4 + m % 2)[:, t * dv:(t + 1) * dv], pT[:, m % 2, 2 * t + kt, :], v(m, kt), start=(kt == 0), stop=(kt == 1))
                            last.then_inc(o_mm.up(), 1)

                @block.vector
                def _(dve):
                    for i in range(maps + 2):
                        if i < maps:
                            b = i % 2
                            dve.wait_ge(s_mm.sem, s_mm.at(i + 1))
                            if i >= 2:
                                dve.wait_ge(p_ready.sem, p_ready.at(T * (i - 1)))
                            s = bank(b).rearrange("p (t s) -> p t s", t=T)
                            if use_mask:
                                ins = dve.scalar_tensor_tensor(s_sb[:, b], s, scale, mask[:], ALU.mult, ALU.add)
                            else:
                                ins = dve.tensor_scalar(s_sb[:, b], s, scale, None, ALU.mult)
                            ins.then_inc(s_out.up(), 1)
                            dve.wait_ge(s_out.sem, s_out.at(i + 1))
                            link(dve, "dve_step", dve.tensor_reduce(pmax[:, b, :], s_sb[:, b], AX, ALU.max))
                            dve.tensor_scalar(nmax[:, b, :], pmax[:, b, :], -1.0, None, ALU.mult).then_inc(m_ready.up(), 1)
                        if i >= 2:
                            m = i - 2
                            b = m % 2
                            dve.wait_ge(p_ready.sem, p_ready.at(T * (m + 1)))
                            link(dve, "dve_step", dve.reciprocal(rs[:, b, :], sums[:, b, :]))
                            if diff and m % 2:
                                link(dve, "dve_step", dve.tensor_scalar(rs[:, b, :], rs[:, b, :], nlam[:], None, ALU.mult))
                            dve.wait_ge(o_mm.sem, o_mm.at(m + 1))
                            for t in range(T):
                                x, r = bank(4 + b)[:, t * dv:(t + 1) * dv], rs[:, b, t:t + 1]
                                if diff and m % 2:
                                    ins = dve.scalar_tensor_tensor(o(m, t), x, r, o(m, t), ALU.mult, ALU.add)
                                else:
                                    ins = dve.tensor_scalar(o(m, t), x, r, None, ALU.mult)
                            ins.then_inc(o_out.up(), 1)
                            dve.wait_ge(o_out.sem, o_out.at(m + 1))

                @block.scalar
                def _(act):
                    for i in range(maps + 1):
                        if i < maps:
                            b = i % 2
                            act.wait_ge(m_ready.sem, m_ready.at(i + 1))
                            if i >= 2:
                                act.wait_ge(p_mm.sem, p_mm.at(i - 1))
                                act.wait_ge(o_out.sem, o_out.at(i - 1))
                            for t in range(T):
                                act.activation(p_sb[:, b, t, :], s_sb[:, b, t, :], ACT.Exp, bias=nmax[:, b, t:t + 1], accum_out=sums[:, b, t:t + 1]).then_inc(p_ready.up(), 1)
                        if i >= 1:
                            m = i - 1
                            act.wait_ge(p_mm.sem, p_mm.at(m + 1))
                            if m >= 2:
                                act.wait_ge(o_mm.sem, o_mm.at(m - 1))
                            act.copy(pT[:, m % 2], bank(2 + m % 2).rearrange("p (c s) -> p c s", c=4)).then_inc(pT_ready.up(), 1)

        pos["issued"] = SLOTS
        with new_block() as block:
            const_in, small_in = sig("inputs_loaded"), sig("small_loaded")
            trig = sig("angles_ready")
            posn = sb("posn", [P, T], I32)
            inv = blk(2)[:, 0:24]
            lam = blk(2)[:, 64:64 + 4 * HD].rearrange("p (a f) -> p a f", a=4)
            posf, ang, turn = stat[:, 0:2], blk(2)[:, 512:560], blk(2)[:, 576:624]
            red = blk(2)[:, 640:736].rearrange("p (c n) -> p c n", c=2)
            trigs = blk(2)[:, 768:864].rearrange("p (c n) -> p c n", c=2)
            lsum, lexp, lprod = stat[:, 4:6], stat[:, 6:8], blk(2)[:, 1024:1024 + 2 * HD].rearrange("p (a f) -> p a f", a=2)

            @block.sync
            def _(sp):
                for n, (o, i) in enumerate([(h[:], d["x"].rearrange("(t p) f -> p t f", p=P)), (ident[:], d["ident"]), (cols[:], d["cols"]),
                                            (mask[:], d["causal"]), (cos0[:], d["cos0"]), (sin0[:], d["sin0"])]):
                    sp.dma_start(o, i).then_inc(const_in.up(16), 16)
                    if n == 0:
                        load(sp, 0)
                for j in range(1, SLOTS):
                    load(sp, j)
                sp.wait_ge(const_in.sem, const_in.at(6 * 16))

            @block.scalar
            def _(act):
                act.dma_start(posn[:], d["pos"]).then_inc(small_in.up(16), 16)
                act.dma_start(inv, d["inv"].rearrange("(o f) -> o f", o=1).broadcast_to([P, 24])).then_inc(small_in.up(16), 16)
                act.dma_start(lam.rearrange("p a f -> p (a f)"), d["lam"].rearrange("(o f) -> o f", o=1).broadcast_to([P, 4 * HD])).then_inc(small_in.up(16), 16)
                act.wait_ge(trig.sem, trig.at(1))
                for c in range(2):
                    act.activation(trigs[:, c, :], red[:, c, :], ACT.Sin).then_inc(sig("trig_ready").up(), 1)
                act.wait_ge(sig("lambda_sums").sem, sig("lambda_sums").at(1))
                act.activation(lexp, lsum, ACT.Exp).then_inc(sig("lambda_exp").up(), 1)

            @block.vector
            def _(dve):
                def step(ins):
                    link(dve, "dve_step", ins)
                dve.wait_ge(small_in.sem, small_in.at(48))
                step(dve.tensor_copy(posf, posn[:]))
                two_pi = 2 * math.pi
                c1 = 6.28125
                c2 = math.floor((two_pi - c1) * 2 ** 19) / 2 ** 19
                c3 = two_pi - c1 - c2
                big = 1.5 * 2 ** 23
                for t in range(T):
                    step(dve.tensor_scalar(ang[:, t * 24:(t + 1) * 24], inv, posf[:, t:t + 1], None, ALU.mult))
                for c in range(2):
                    step(dve.tensor_scalar(turn, ang, 1 / two_pi, 0.25 * c, ALU.mult, ALU.add))
                    step(dve.tensor_scalar(turn, turn, big, None, ALU.add))
                    step(dve.tensor_scalar(turn, turn, big, None, ALU.subtract))
                    step(dve.scalar_tensor_tensor(red[:, c, :], turn, -c1, ang, ALU.mult, ALU.add))
                    step(dve.scalar_tensor_tensor(red[:, c, :], turn, -c2, red[:, c, :], ALU.mult, ALU.add))
                    step(dve.scalar_tensor_tensor(red[:, c, :], turn, -c3, red[:, c, :], ALU.mult, ALU.add))
                    if c:
                        step(dve.tensor_scalar(red[:, c, :], red[:, c, :], math.pi / 2, None, ALU.add))
                    step(dve.tensor_scalar(red[:, c, :], red[:, c, :], 3.1415925, -3.1415925, ALU.min, ALU.max))
                dve.tensor_scalar(red[:, 0, 0:1], red[:, 0, 0:1], 1.0, None, ALU.mult).then_inc(trig.up(), 1)
                dve.wait_ge(sig("trig_ready").sem, sig("trig_ready").at(2))
                for t in range(T):
                    for n, (c, s, half) in enumerate([(cosd, sind, DIFF_ROPE // 2), (cosr, sinr, MLA_ROPE // 2)]):
                        a = t * 24 + 8 * n
                        sn, cs = trigs[:, 0, a:a + half], trigs[:, 1, a:a + half]
                        dve.tensor_copy(c[:, t, 0:half], cs)
                        dve.tensor_copy(c[:, t, half:2 * half], cs)
                        dve.tensor_scalar(s[:, t, 0:half], sn, -1.0, None, ALU.mult)
                        dve.tensor_copy(s[:, t, half:2 * half], sn)
                step(dve.tensor_tensor(lprod, lam[:, 0:4:2, :], lam[:, 1:4:2, :], ALU.mult))
                step(dve.tensor_reduce(lsum, lprod, AX, ALU.add))
                dve.tensor_scalar(lsum, lsum, 1.0, None, ALU.mult).then_inc(sig("lambda_sums").up(), 1)
                dve.wait_ge(sig("lambda_exp").sem, sig("lambda_exp").at(1))
                step(dve.tensor_tensor(nlam[:], lexp[:, 1:2], lexp[:, 0:1], ALU.subtract))
                step(dve.tensor_scalar(nlam[:], nlam[:], LAMBDA_INIT, None, ALU.subtract))

        def ffn_stage(n_units, layer, row_src=()):
            j0 = next_unit(n_units)
            hid = blk(0)[:, 0:1024].rearrange("p (b f s) -> p b f s", b=2, f=2)
            act_out = blk(1)[:, 0:1024].rearrange("p (b f s) -> p b f s", b=2, f=2)
            conv = blk(2)[:, 0:1024].rearrange("p (b f s) -> p b f s", b=2, f=2)
            with new_block() as block:
                gu, dn = sig("gate_up_ready"), sig("down_done")
                biased, conv_ready, act_ready, hid_ready = sig("gate_biased"), sig("conv_ready"), sig("gate_active"), sig("hidden_ready")
                rows_in = sig("rows_loaded")

                @block.tensor
                def _(pe):
                    def down(u):
                        pe.wait_ge(hid_ready.sem, hid_ready.at(u + 1))
                        w = ring[:, (j0 + u) % SLOTS, 2 * KD * 2 * P:UNIT].rearrange("p (f n) -> p f n", f=2)
                        for t in range(T):
                            for c in range(2):
                                for f in range(2):
                                    mm = pe.matmul(bank(4 + 2 * t + c), hid[:, u % 2, f, t * P:(t + 1) * P], w[:, f, c * 512:(c + 1) * 512],
                                                   start=(u == 0 and f == 0), stop=(u == n_units - 1 and f == 1), skip_group_check=True)
                        mm.then_inc(dn.up(), 1)
                        unit_done(j0 + u, dn)

                    for u in range(n_units):
                        arrived(pe, j0 + u)
                        if u >= 2:
                            pe.wait_ge(hid_ready.sem, hid_ready.at(u - 1))
                        w = ring[:, (j0 + u) % SLOTS, 0:2 * KD * 2 * P].rearrange("p (g k n) -> p g k n", g=2, k=KD)
                        for g in range(2):
                            for f in range(2):
                                for k in range(KD):
                                    mm = pe.matmul(bank(2 * (u % 2) + g)[:, f * SEQ:(f + 1) * SEQ], w[:, g, k, f * P:(f + 1) * P], xT[:, k, :],
                                                   start=(k == 0), stop=(k == KD - 1))
                        mm.then_inc(gu.up(), 1)
                        if u >= 1:
                            down(u - 1)
                    down(n_units - 1)
                stream(block, n_units)

                @block.scalar
                def _(act):
                    for n, r in enumerate(row_src):
                        act.dma_start(rows[:, n, :], r.rearrange("(o f) -> o f", o=1).broadcast_to([P, D])).then_inc(rows_in.up(16), 16)
                    for u in range(n_units):
                        b = u % 2
                        act.wait_ge(gu.sem, gu.at(u + 1))
                        g = bank(2 * b).rearrange("p (f s) -> p f s", f=2)
                        if u >= 2:
                            act.wait_ge(hid_ready.sem, hid_ready.at(u - 1))
                        for f in range(2):
                            ft = 2 * u + f
                            act.activation(conv[:, b, f, :], g[:, f, :], ACT.Identity, bias=col("conv_b", layer * FT + ft),
                                           scale=col("conv_w", (layer * 3 + 2) * FT + ft)).then_inc(biased.up(), 1)
                        act.wait_ge(conv_ready.sem, conv_ready.at(u + 1))
                        act.activation(act_out[:, b], conv[:, b], ACT.Silu).then_inc(act_ready.up(), 1)

                @block.vector
                def _(dve):
                    for u in range(n_units):
                        b = u % 2
                        gt = bank(2 * b).rearrange("p (f s) -> p f s", f=2)
                        up = bank(2 * b + 1).rearrange("p (f s) -> p f s", f=2)
                        dve.wait_ge(biased.sem, biased.at(2 * u + 2))
                        for lag, w in ((1, 1), (2, 0)):
                            for f in range(2):
                                ft = 2 * u + f
                                x = conv[:, b, f, lag:SEQ]
                                ins = dve.scalar_tensor_tensor(x, gt[:, f, 0:SEQ - lag], col("conv_w", (layer * 3 + w) * FT + ft), x, ALU.mult, ALU.add)
                            if lag == 1:
                                link(dve, "dve_step", ins)
                        ins.then_inc(conv_ready.up(), 1)
                        dve.wait_ge(act_ready.sem, act_ready.at(u + 1))
                        if u >= 2:
                            dve.wait_ge(dn.sem, dn.at(u - 1))
                        dve.tensor_tensor(hid[:, b], act_out[:, b], up, ALU.mult).then_inc(hid_ready.up(), 1)
                    dve.wait_ge(dn.sem, dn.at(n_units))
                    for t in range(T):
                        for c in range(2):
                            x = h[:, t, c * 512:(c + 1) * 512]
                            dve.scalar_tensor_tensor(x, x, 1.0, bank(4 + 2 * t + c), ALU.mult, ALU.add)

        def experts(layer, comb, hid4, xg, swT, row_src):
            j0 = next_unit(EU)
            steps = EU // EPG
            with new_block() as block:
                gu, dn = sig("gate_up_ready"), sig("down_done")
                act_ready, hid_ready, summed = sig("gate_active"), sig("hidden_ready"), sig("experts_summed")
                rows_in = sig("rows_loaded")
                weights_out, weights_in = sig(f"weight_rows_ready{layer}"), sig(f"weight_rows_copied{layer}")
                weighted = sig(f"gate_weighted{layer}")
                rowsE = arena[:, 3:5, :].rearrange("p a f -> p (a f)").rearrange("p (e s) -> p e s", e=N_EXPERTS)
                hid = blk(1)[:, 0:1024].rearrange("p (b f s) -> p b f s", b=2, f=2)
                act_out = blk(1)[:, 1024:2048].rearrange("p (b f s) -> p b f s", b=2, f=2)
                copied = [sig(f"outputs_copied_act{layer}"), sig(f"outputs_copied_dve{layer}")]
                act_sp = blk(1)[:, 0:4 * SLOTS_E].rearrange("p (b f s) -> p b f s", b=2, f=2)
                sw_now = blk(1)[:, 512:512 + SEQ]
                y_now = blk(2)[:, 0:D]

                def runs(eng, body):
                    for u in range(EPG):
                        body(0, u, 1)
                    with eng.Fori(1, steps - 1) as i:
                        for u in range(EPG):
                            body(i, u, steps - 2)
                    for u in range(EPG):
                        body(steps - 1, u, 1)

                def start(i, n=0, u=0):
                    return isinstance(i, int) and i == 0 and (n == 0 or u < n)

                def at(i, u):
                    return i * EPG + u

                def either(eng, dense, sparse):
                    counts = {s: s.count for s in signals.values()}
                    full = eng.value_load(overflow[0:1, 0:1], min_val=0, max_val=1)
                    with eng.If(full == 1):
                        dense()
                    for s, n in counts.items():
                        s.count = n
                    with eng.Else():
                        sparse()

                @block.tensor
                def _(pe):
                    def dense():
                        for e in range(N_EXPERTS):
                            if e >= 8 and e % 2 == 0:
                                pe.wait_ge(weights_in.sem, weights_in.at(e // 2 - 3))
                            for t in range(T):
                                c = comb[:, t, e // 4, e % 4:e % 4 + 1].broadcast_to([P, P])
                                mm = pe.matmul(bank((e // 2) % 4)[:, ((e % 2) * T + t) * P:((e % 2) * T + t + 1) * P], c, ident[:], start=True, stop=True)
                            if e % 2:
                                mm.then_inc(weights_out.up(), 1)
                        pe.wait_ge(weights_in.sem, weights_in.at(PAIRS))

                        def down(i, u, r):
                            pe.wait_ge(hid_ready.sem, hid_ready.at(at(i, u) + 1))
                            w = ring[:, (j0 + u) % SLOTS, 2 * KD * 2 * P:UNIT].rearrange("p (f n) -> p f n", f=2)
                            for t in range(T):
                                for c in range(2):
                                    for f in range(2):
                                        mm = pe.matmul(bank(4 + 2 * t + c), hid[:, u % 2, f, t * P:(t + 1) * P], w[:, f, c * 512:(c + 1) * 512],
                                                       start=(start(i) and u == 0 and f == 0), stop=False, skip_group_check=True)
                            mm.then_inc(dn.up(1, r), 1)

                        def body(i, u, r):
                            s = (j0 + u) % SLOTS
                            pe.wait_ge(loaded[s].sem, i * 16 * (EPG // SLOTS) + 16 * ((j0 + u) // SLOTS + 1))
                            if not start(i, 2, u):
                                pe.wait_ge(hid_ready.sem, hid_ready.at(at(i, u) - 1))
                            w = ring[:, s, 0:2 * KD * 2 * P].rearrange("p (g k n) -> p g k n", g=2, k=KD)
                            for g in range(2):
                                for f in range(2):
                                    for k in range(KD):
                                        mm = pe.matmul(bank(2 * (u % 2) + g)[:, f * SEQ:(f + 1) * SEQ], w[:, g, k, f * P:(f + 1) * P], xT[:, k, :],
                                                       start=(k == 0), stop=(k == KD - 1))
                            mm.then_inc(gu.up(1, r), 1)
                            if u > 0:
                                down(i, u - 1, r)
                            elif not start(i):
                                down(i - 1, EPG - 1, r)
                        runs(pe, body)
                        down(steps - 1, EPG - 1, 1)
                        pe.matmul(bank(0)[:, 0:P], ident[:], ident[:], start=True, stop=True).then_inc(summed.up(), 1)

                    def sparse():
                        def down(i, u, r):
                            pe.wait_ge(hid_ready.sem, hid_ready.at(at(i, u) + 1))
                            if u == 0 and not start(i):
                                for c in range(2):
                                    pe.wait_ge(copied[c].sem, copied[c].at(i))
                            w = ring[:, (j0 + u) % SLOTS, 2 * KD * 2 * P:UNIT].rearrange("p (f n) -> p f n", f=2)
                            for c in range(2):
                                for f in range(2):
                                    mm = pe.matmul(bank(2 + c), hid4[:, u, f, :], w[:, f, c * 512:(c + 1) * 512],
                                                   start=(u == 0 and f == 0), stop=(u == EPG - 1 and f == 1), skip_group_check=True)
                            mm.then_inc(dn.up(1, r), 1)

                        def scatter(i):
                            for c in range(2):
                                pe.wait_ge(copied[c].sem, copied[c].at(i + 1))
                            for t in range(T):
                                for c in range(2):
                                    mm = pe.matmul(bank(4 + 2 * t + c), sw_now[:, t * P:(t + 1) * P], y_now[:, c * 512:(c + 1) * 512],
                                                   start=start(i), stop=False, skip_group_check=True)
                            return mm

                        def body(i, u, r):
                            s = (j0 + u) % SLOTS
                            pe.wait_ge(loaded[s].sem, i * 16 * (EPG // SLOTS) + 16 * ((j0 + u) // SLOTS + 1))
                            if not start(i, 2, u):
                                pe.wait_ge(hid_ready.sem, hid_ready.at(at(i, u) - 1))
                            w = ring[:, s, 0:2 * KD * 2 * P].rearrange("p (g k n) -> p g k n", g=2, k=KD)
                            e = i * 2 + u // 2
                            for g in range(2):
                                for f in range(2):
                                    for k in range(KD):
                                        mm = pe.matmul(bank(u % 2)[:, (2 * g + f) * SLOTS_E:(2 * g + f + 1) * SLOTS_E], w[:, g, k, f * P:(f + 1) * P],
                                                       xg[:, k, bass.ds(e * SLOTS_E, SLOTS_E)], start=(k == 0), stop=(k == KD - 1))
                            mm.then_inc(gu.up(1, r), 1)
                            if u > 0:
                                down(i, u - 1, r)
                            elif not start(i):
                                down(i - 1, EPG - 1, r)
                            if u == 1 and not start(i):
                                scatter(i - 1)
                        for b in range(4, 8):
                            pe.matmul(bank(b), hid4[:, 0, 0, :], hid4[:, 0:2].rearrange("p u f s -> p (u f s)"), start=True, stop=False, skip_group_check=True)
                        runs(pe, body)
                        down(steps - 1, EPG - 1, 1)
                        scatter(steps - 1).then_inc(summed.up(), 1)
                    either(pe, dense, sparse)

                @block.scalar
                def _(act):
                    for n, r in enumerate(row_src):
                        act.dma_start(rows[:, n, :], r.rearrange("(o f) -> o f", o=1).broadcast_to([P, D])).then_inc(rows_in.up(16), 16)

                    def dense():
                        for n in range(PAIRS):
                            act.wait_ge(weights_out.sem, weights_out.at(n + 1))
                            act.copy(rowsE[:, 2 * n:2 * n + 2, :], bank(n % 4).rearrange("p (e s) -> p e s", e=2)).then_inc(weights_in.up(), 1)

                        def body(i, u, r):
                            b = u % 2
                            act.wait_ge(gu.sem, gu.at(at(i, u) + 1))
                            if not start(i, 2, u):
                                act.wait_ge(hid_ready.sem, hid_ready.at(at(i, u) - 1))
                            act.activation(act_out[:, b], bank(2 * b).rearrange("p (f s) -> p f s", f=2), ACT.Silu).then_inc(act_ready.up(1, r), 1)
                        runs(act, body)

                    def sparse():
                        def copy_out(i):
                            act.wait_ge(dn.sem, dn.at(at(i, EPG)))
                            act.copy(y_now[:, 0:512], bank(2)).then_inc(copied[0].up(), 1)

                        def body(i, u, r):
                            b = u % 2
                            act.wait_ge(gu.sem, gu.at(at(i, u) + 1))
                            if not start(i, 2, u):
                                act.wait_ge(hid_ready.sem, hid_ready.at(at(i, u) - 1))
                            act.activation(act_sp[:, b], bank(b)[:, 0:2 * SLOTS_E].rearrange("p (f s) -> p f s", f=2), ACT.Silu).then_inc(act_ready.up(1, r), 1)
                            if u == 0 and not start(i):
                                copy_out(i - 1)
                            if u == EPG - 1:
                                act.copy(sw_now, swT[:, bass.ds(i * SEQ, SEQ)])
                        runs(act, body)
                        copy_out(steps - 1)
                    either(act, dense, sparse)

                @block.vector
                def _(dve):
                    def dense():
                        dve.wait_ge(weights_in.sem, weights_in.at(PAIRS))

                        def body(i, u, r):
                            b = u % 2
                            up = bank(2 * b + 1).rearrange("p (f s) -> p f s", f=2)
                            dve.wait_ge(act_ready.sem, act_ready.at(at(i, u) + 1))
                            if not start(i, 2, u):
                                dve.wait_ge(dn.sem, dn.at(at(i, u) - 1))
                            e = rowsE[:, bass.ds(i * 2 + u // 2, 1), :]
                            dve.tensor_tensor(act_out[:, b], act_out[:, b], e.broadcast_to([P, 2, SEQ]), ALU.mult).then_inc(weighted.up(1, r), 1)
                            dve.wait_ge(weighted.sem, weighted.at(at(i, u) + 1))
                            dve.tensor_tensor(hid[:, b], act_out[:, b], up, ALU.mult).then_inc(hid_ready.up(1, r), 1)
                        runs(dve, body)

                    def sparse():
                        def copy_out(i):
                            dve.wait_ge(dn.sem, dn.at(at(i, EPG)))
                            dve.tensor_copy(y_now[:, 512:1024], bank(3)).then_inc(copied[1].up(), 1)

                        def body(i, u, r):
                            b, c = u % 2, SLOTS_E * (u // 2)
                            up = bank(b)[:, 2 * SLOTS_E:4 * SLOTS_E].rearrange("p (f s) -> p f s", f=2)
                            dve.wait_ge(act_ready.sem, act_ready.at(at(i, u) + 1))
                            if not start(i):
                                dve.wait_ge(dn.sem, dn.at(at(i, u) - EPG + 1))
                            dve.tensor_tensor(hid4[:, u, :, c:c + SLOTS_E], act_sp[:, b], up, ALU.mult).then_inc(hid_ready.up(1, r), 1)
                            if u == 0 and not start(i):
                                copy_out(i - 1)
                        runs(dve, body)
                        copy_out(steps - 1)
                    either(dve, dense, sparse)
                    dve.wait_ge(summed.sem, summed.at(1))
                    for t in range(T):
                        for c in range(2):
                            x = h[:, t, c * 512:(c + 1) * 512]
                            dve.scalar_tensor_tensor(x, x, ALPHA, bank(4 + 2 * t + c), ALU.mult, ALU.add)

                for n in range(EU):
                    release[j0 + n] = dn.sem, dn.base + n + 1
                moe_i = moe_at.index(j0)
                first, last = pos["issued"], min(pos["issued"] + EU, len(loads))
                pos["issued"] = last

                @block.sync
                def _(sp):
                    with sp.Fori(0, steps - 1) as i:
                        for u in range(EPG):
                            sp.wait_ge(dn.sem, dn.at(i * EPG + (u + 1)))
                            src = moe[bass.ds(i * EPG + (moe_i * EU + EPG + u), 1), :, :].rearrange("a p n -> p (a n)")
                            sp.dma_start(ring[:, (first + u) % SLOTS, :], src).then_inc(loaded[(first + u) % SLOTS].up(16, steps - 1), 16)
                    for j in range(first + EU - EPG, last):
                        load(sp, j)

        def first_attention():
            norm("rms", RMS_EPS, tok(0), gains=col("norm_mix", 0, KD))
            project(6, dest=lambda u, t: tok(u // 2)[:, t, (u % 2) * COLS:(u % 2 + 1) * COLS],
                    rotary=lambda u: (8, HD, 0, HD, cos0, sin0, blk(3)) if u < 4 else None)
            transpose_all([(tok(0), fm(3)), (tok(1), fm(4))])

            def hs(m):
                return slice(64 * (m % 2), 64 * (m % 2) + 64)
            attention(HEADS, lambda m, t: [fm(3)[hs(m), m // 2, t * P:(t + 1) * P]], lambda m: [fm(4)[hs(m), m // 2, :]],
                      lambda m, kt: tok(2)[:, kt, m * HD:(m + 1) * HD], HD, lambda m, t: tok(5)[:, t, m * HD:(m + 1) * HD],
                      HD ** -0.5, True, (blk(6), blk(7)))
            transpose_all([(tok(5), xT)])
            project(2, residual=1.0)

        def rwkv():
            A_, R_ = 1, 7
            BKs = arena[:, 2:4, :].rearrange("p a f -> p (a f)").rearrange("p (m c w s) -> p m c w s", m=KD, c=NCH, w=2)
            UV = arena[:, 5:7, :].rearrange("p a f -> p (a f)").rearrange("p (c g m v) -> p c g m v", c=NCH, g=2, m=KD)
            gT = fm(9)
            sgm, xx = fm(3), fm(0)
            mixes = [fm(1), fm(2)]
            kx, ax, rx = fm(8), fm(4), fm(R_)
            pc = stat[:, 64:96].rearrange("p (m c) -> p m c", m=KD)
            bonus = sb("bonus", [P, NCH, HEADS])
            norm("rms", RMS_EPS, tok(0), gains=col("norm_mix", KD, KD))
            j0 = next_unit(7)
            order = [0, 2, 3, 1, 4, 5]
            hw, ha, hg = rows[0:64, 0, 0:SEQ], rows[0:64, 0, 256:512], rows[:, 0, 512:768]
            with new_block() as block:
                mix_ready, mm, evac = sig("mix_ready"), sig("product_ready"), sig("act_evacuated")
                reads = [4, 8, 12, 13]

                @block.vector
                def _(dve):
                    link(dve, "dve_step", dve.tensor_tensor(xx[:, :, 1:SEQ], xT[:, :, 0:SEQ - 1], xT[:, :, 1:SEQ], ALU.subtract))
                    link(dve, "dve_step", dve.tensor_scalar(xx[:, :, 0:1], xT[:, :, 0:1], -1.0, None, ALU.mult))
                    for n, i in enumerate(order):
                        if n >= 2:
                            dve.wait_ge(mm.sem, mm.at(reads[n - 2]))
                        for k in range(KD):
                            ins = dve.scalar_tensor_tensor(mixes[n % 2][:, k, :], xx[:, k, :], col("mu", i * KD + k), xT[:, k, :], ALU.mult, ALU.add)
                        ins.then_inc(mix_ready.up(), 1)

                @block.tensor
                def _(pe):
                    n = 0
                    for i in range(2):
                        pe.wait_ge(mix_ready.sem, mix_ready.at(i + 1))
                        for u in range(2):
                            arrived(pe, j0 + 2 * i + u)
                            w = ring[:, (j0 + 2 * i + u) % SLOTS, 0:KD * COLS].rearrange("p (k n) -> p k n", k=KD)
                            project_fm(pe, w, mixes[i], n, mm, evac)
                            unit_done(j0 + 2 * i + u, mm)
                            n += 2
                    pe.wait_ge(mix_ready.sem, mix_ready.at(3))
                    for u in range(2):
                        arrived(pe, j0 + 4 + u)
                        w = ring[:, (j0 + 4 + u) % SLOTS, 0:KD * COLS].rearrange("p (k n) -> p k n", k=KD)
                        for t in range(T):
                            pe.wait_ge(evac.sem, evac.at(n - 3))
                            for k in range(KD):
                                last = pe.matmul(bank(n % 4), mixes[0][:, k, t * P:(t + 1) * P], w[:, k, :], start=(k == 0), stop=(k == KD - 1))
                            last.then_inc(mm.up(), 1)
                            n += 1
                        unit_done(j0 + 4 + u, mm)
                    arrived(pe, j0 + 6)
                    lora = ring[:, (j0 + 6) % SLOTS, :]
                    w1, a1 = (lora[:, a:a + 512].rearrange("p (k n) -> p k n", k=KD) for a in (0, 512))
                    g1 = lora[:, 1024:2048].rearrange("p (k n) -> p k n", k=KD)
                    w2, a2, g2 = lora[0:64, 2048:3072], lora[0:64, 3072:4096], lora[:, 4096:5120]
                    for i, (wi, rank, wo, hid) in enumerate([(w1, 64, w2, hw), (a1, 64, a2, ha), (g1, 128, g2, hg)]):
                        pe.wait_ge(mix_ready.sem, mix_ready.at(4 + i))
                        pe.wait_ge(evac.sem, evac.at(n - 3))
                        for k in range(KD):
                            last = pe.matmul(bank(n % 4)[0:rank, 0:SEQ], wi[:, k, :], mixes[(3 + i) % 2][:, k, :], start=(k == 0), stop=(k == KD - 1))
                        last.then_inc(mm.up(), 1)
                        n += 1
                        pe.wait_ge(evac.sem, evac.at(n))
                        for f in range(4):
                            pe.wait_ge(evac.sem, evac.at(n - 3))
                            for m in range(2):
                                c = (2 * f + m) * P
                                last = pe.matmul(bank(n % 4)[:, m * SEQ:(m + 1) * SEQ], wo[:, c:c + P], hid, start=True, stop=True)
                            last.then_inc(mm.up(), 1)
                            n += 1
                    unit_done(j0 + 6, mm)
                stream(block, 7)

                @block.scalar
                def _(act):
                    n = 0
                    for dst in (rx, kx):
                        for f in range(4):
                            act.wait_ge(mm.sem, mm.at(n + 1))
                            act.copy(dst[:, 2 * f:2 * f + 2, :], bank(n % 4).rearrange("p (m s) -> p m s", m=2)).then_inc(evac.up(), 1)
                            n += 1
                    for u in range(2):
                        for t in range(T):
                            act.wait_ge(mm.sem, mm.at(n + 1))
                            for half in range(2):
                                o = UV[64:128, 2 * t + half, :, 4 * u:4 * u + 4, :].rearrange("p g m v -> p m g v")
                                ins = act.copy(o, bank(n % 4)[64 * half:64 * half + 64, :].rearrange("p (m g v) -> p m g v", m=4, g=2))
                            ins.then_inc(evac.up(), 1)
                            n += 1
                    for i, (hid, fn, rank, dst, fn2, bias) in enumerate([(hw, ACT.Tanh, 64, sgm, ACT.Sigmoid, "w0"), (ha, ACT.Copy, 64, ax, ACT.Sigmoid, "a0"),
                                                                         (hg, ACT.Sigmoid, 128, gT, ACT.Copy, None)]):
                        act.wait_ge(mm.sem, mm.at(n + 1))
                        act.activation(hid, bank(n % 4)[0:rank, 0:SEQ], fn).then_inc(evac.up(), 1)
                        n += 1
                        for f in range(4):
                            act.wait_ge(mm.sem, mm.at(n + 1))
                            for m in range(2):
                                k = 2 * f + m
                                src = bank(n % 4)[:, m * SEQ:(m + 1) * SEQ]
                                ins = act.activation(dst[:, k, :], src, fn2) if bias is None else act.activation(dst[:, k, :], src, fn2, bias=col(bias, k))
                            ins.then_inc(evac.up(), 1)
                            n += 1

            cum, kk, scratch = fm(0), fm(A_), fm(2)
            spread = rows[0:HEADS, 0, :].rearrange("p (m f) -> p m f", m=KD)
            heads16 = rows[:, 1, 0:KD * HEADS].rearrange("p (m a) -> p m a", m=KD)
            reset = rows[:, 1, 256:512]
            pair = rows[:, 1, 512:514]
            with new_block() as block:
                c_in, step_a = sig("small_loaded"), sig("act_step")
                kk_raw, sq, ss_mm, nrm, inv_ready, wide_mm, wide_used = (sig(x) for x in ("kk_ready", "squares_ready", "scores_ready", "row_root", "inverse_ready", "product_ready", "dve_evacuated"))
                rk_ready, bonus_mm, cum_ready, diff_ready = sig("bonus_terms"), sig("transposed"), sig("cumsum_ready"), sig("cumsum_before")
                exp_ready, exp_used = sig("exps_ready"), sig("exps_used")
                root = mask.rearrange("p t s -> p (t s)")[0:HEADS, 0:SEQ]
                rin = mask.rearrange("p t s -> p (t s)")[0:HEADS, SEQ:2 * SEQ]

                @block.sync
                def _(sp):
                    sp.dma_start(spread, d["spread"]).then_inc(c_in.up(16), 16)
                    sp.dma_start(heads16, d["heads16"]).then_inc(c_in.up(16), 16)
                    sp.dma_start(reset, d["reset"]).then_inc(c_in.up(16), 16)
                    sp.dma_start(pair, d["pair"]).then_inc(c_in.up(16), 16)

                @block.vector
                def _(dve):
                    def step(ins):
                        link(dve, "dve_step", ins)
                    for m in range(KD):
                        dve.tensor_scalar(kk[:, m, :], kx[:, m, :], col("k_k", m), None, ALU.mult).then_inc(kk_raw.up(), 1)
                    dve.wait_ge(c_in.sem, c_in.at(64))
                    for m in range(KD):
                        ins = dve.tensor_tensor_scan(cum[:, m, :], reset, sgm[:, m, :], 0.0, ALU.mult, ALU.add)
                    ins.then_inc(cum_ready.up(), 1)
                    dve.wait_ge(sq.sem, sq.at(2))
                    dve.wait_ge(ss_mm.sem, ss_mm.at(1))
                    for m in range(KD):
                        ins = dve.tensor_scalar(scratch[:, m, :], ax[:, m, :], 1.0, col("k_a", m), ALU.subtract, ALU.mult)
                    step(ins)
                    step(dve.scalar_tensor_tensor(kx, scratch, 1.0, kx, ALU.add, ALU.mult))
                    for m in range(KD):
                        ins = dve.scalar_tensor_tensor(xT[:, m, :], rx[:, m, :], col("r_k", m), kx[:, m, :], ALU.mult, ALU.mult)
                    ins.then_inc(rk_ready.up(), 1)
                    dve.wait_ge(nrm.sem, nrm.at(1))
                    step(dve.tensor_scalar(root, root, 1e-12, None, ALU.max))
                    dve.reciprocal(rin, root).then_inc(inv_ready.up(), 1)
                    for n in range(4):
                        dve.wait_ge(wide_mm.sem, wide_mm.at(n + 1))
                        x = kk[:, 2 * n:2 * n + 2, :]
                        ins = dve.tensor_tensor(x, x, bank(n + 1).rearrange("p (m s) -> p m s", m=2), ALU.mult)
                    step(ins)
                    step(dve.tensor_tensor(ax, kk, ax, ALU.mult))
                    dve.tensor_tensor(sgm, cum, sgm, ALU.subtract).then_inc(diff_ready.up(), 1)
                    dve.wait_ge(exp_ready.sem, exp_ready.at(1))
                    step(dve.tensor_copy(pc, scratch.rearrange("p m (c s) -> p m c s", c=NCH)[:, :, :, CHUNK - 1]))
                    dve.tensor_tensor(rx, rx, scratch, ALU.mult).then_inc(exp_used.up(), 1)
                    dve.wait_ge(exp_ready.sem, exp_ready.at(2))
                    dve.scalar_tensor_tensor(kk, kk, -1.0, sgm, ALU.mult, ALU.mult).then_inc(exp_used.up(), 1)
                    dve.wait_ge(exp_ready.sem, exp_ready.at(3))
                    dve.wait_ge(exp_used.sem, exp_used.at(2))
                    for w, x in enumerate((ax, kx)):
                        dve.tensor_tensor(BKs[:, :, :, w, :], x.rearrange("p m (c s) -> p m c s", c=NCH), cum.rearrange("p m (c s) -> p m c s", c=NCH), ALU.mult)
                    dve.wait_ge(bonus_mm.sem, bonus_mm.at(1))
                    dve.tensor_copy(bonus[64:128].rearrange("p c a -> p (c a)"), bank(5)[64:128, 0:NCH * HEADS])

                @block.scalar
                def _(act):
                    act.wait_ge(kk_raw.sem, kk_raw.at(KD))
                    act.activation(scratch, kk, ACT.Square).then_inc(sq.up(2), 2)
                    act.wait_ge(ss_mm.sem, ss_mm.at(1))
                    act.activation(root, bank(0)[0:HEADS, 0:SEQ], ACT.Sqrt).then_inc(nrm.up(), 1)
                    act.wait_ge(rk_ready.sem, rk_ready.at(1))
                    act.wait_ge(cum_ready.sem, cum_ready.at(1))
                    act.activation(scratch, cum, ACT.Exp, scale=DECAY).then_inc(exp_ready.up(), 1)
                    act.wait_ge(diff_ready.sem, diff_ready.at(1))
                    act.activation(sgm, sgm, ACT.Exp, scale=DECAY).then_inc(exp_ready.up(), 1)
                    act.wait_ge(exp_ready.sem, exp_ready.at(1))
                    act.activation(cum, cum, ACT.Exp, scale=-DECAY).then_inc(exp_ready.up(), 1)

                @block.tensor
                def _(pe):
                    pe.wait_ge(c_in.sem, c_in.at(64))
                    pe.wait_ge(sq.sem, sq.at(2))
                    for m in range(KD):
                        last = pe.matmul(bank(0)[0:HEADS, 0:SEQ], heads16[:, m, :], scratch[:, m, :], start=(m == 0), stop=(m == KD - 1))
                    last.then_inc(ss_mm.up(), 1)
                    pe.wait_ge(rk_ready.sem, rk_ready.at(1))
                    for c in range(NCH):
                        for m in range(KD):
                            last = pe.matmul(bank(5)[64:128, c * HEADS + 2 * m:c * HEADS + 2 * m + 2], xT[:, m, c * CHUNK:(c + 1) * CHUNK], pair, start=True, stop=True)
                    last.then_inc(bonus_mm.up(), 1)
                    pe.wait_ge(inv_ready.sem, inv_ready.at(1))
                    for m in range(KD):
                        last = pe.matmul(bank(1 + m // 2)[:, (m % 2) * SEQ:(m % 2 + 1) * SEQ], spread[:, m, :], rin, start=True, stop=True)
                        if m % 2:
                            last.then_inc(wide_mm.up(), 1)

            view = arena[:, :, :].rearrange("p b (m c s) -> p b m c s", m=KD, c=NCH)

            def AR(m, c):
                return view[:, A_:R_ + 1:R_ - A_, m, c, :]

            def BK(m, c):
                return BKs[:, m, c, :, :].rearrange("p w s -> p (w s)")

            G = blk(0).rearrange("p (g m s) -> p g m s", g=2, m=KD)
            BKt = blk(4)[:, 0:1024].rearrange("p (m s) -> p m s", m=KD)
            M = blk(4)[0:64, 1024:2048].rearrange("p (g m s) -> p g m s", g=2, m=KD)
            X = blk(8)[0:64, 0:1024].rearrange("p (g m s) -> p g m s", g=2, m=KD)
            Y = blk(4)[64:128, 1024:2048]
            Z = blk(8)[64:128, 0:1024]
            W1 = blk(8)[64:128, 1024:2048]
            lmask = stat[0:64, 0:64]
            ST = mask.rearrange("p t s -> p (t s)").rearrange("p (m v) -> p m v", m=KD)
            gm = cos0.rearrange("p t f -> p (t f)")
            ROUNDS = 5

            with new_block() as block:
                c_in = sig("small_loaded")
                n = {x: sig(x) for x in ("bk_turned", "bk_copied", "g_ready", "g_masked", "m_ready", "m_masked", "squared", "n_copied", "m_copied",
                                         "x_step", "x_added", "rhs_ready", "rhs_copied", "u_ready", "u_copied", "y_ready", "state_ready", "state_updated",
                                         "y_copied", "z_ready", "z_turned", "z_gated")}

                @block.sync
                def _(sp):
                    sp.dma_start(gm, d["gmask"]).then_inc(c_in.up(16), 16)
                    sp.dma_start(lmask, d["lmask"]).then_inc(c_in.up(16), 16)
                    sp.dma_start(rows[:, 0, :], d["lnx_w"].rearrange("(o f) -> o f", o=1).broadcast_to([P, D])).then_inc(c_in.up(16), 16)
                    sp.dma_start(rows[:, 1, :], d["lnx_b"].rearrange("(o f) -> o f", o=1).broadcast_to([P, D])).then_inc(c_in.up(16), 16)

                @block.tensor
                def _(pe):
                    def z_turn(c):
                        pe.wait_ge(n["z_ready"].sem, n["z_ready"].at(c + 1))
                        if c:
                            pe.wait_ge(n["z_gated"].sem, n["z_gated"].at(c))
                        for m in range(KD):
                            last = pe.transpose(bank(7)[:, m * CHUNK:(m + 1) * CHUNK], Z[:, m * P:(m + 1) * P], ident[64:128, 64:128])
                        last.then_inc(n["z_turned"].up(), 1)

                    for c in range(NCH):
                        if c:
                            pe.wait_ge(n["u_copied"].sem, n["u_copied"].at(2 * c))
                            pe.wait_ge(n["state_updated"].sem, n["state_updated"].at(c))
                            pe.wait_ge(n["y_copied"].sem, n["y_copied"].at(2 * c))
                        for m in range(KD):
                            last = pe.transpose(bank(m // 4)[:, (m % 4) * P:(m % 4 + 1) * P], BK(m, c), ident[:])
                            if m % 4 == 3:
                                last.then_inc(n["bk_turned"].up(), 1)
                        for m in range(KD):
                            for g in range(2):
                                hs = slice(64 * g, 64 * g + 64)
                                last = pe.matmul(bank(2 + 2 * g + m // 4)[:, (m % 4) * P:(m % 4 + 1) * P], BK(m, c)[hs], AR(m, c)[hs], start=True, stop=True)
                        last.then_inc(n["g_ready"].up(), 1)
                        if c:
                            z_turn(c - 1)
                            pe.wait_ge(n["z_gated"].sem, n["z_gated"].at(c))
                        for m in range(KD):
                            for g in range(2):
                                hs = slice(64 * g, 64 * g + 64)
                                last = pe.matmul(bank(6 + g)[0:64, m * 64:(m + 1) * 64], view[hs, A_, m, c, :], BKs[hs, m, c, 0, :], start=True, stop=True)
                        last.then_inc(n["m_ready"].up(), 1)
                        for j in range(ROUNDS):
                            r = c * ROUNDS + j
                            pe.wait_ge(n["g_masked"].sem, n["g_masked"].at(5 * (c + 1)))
                            pe.wait_ge(n["m_masked"].sem, n["m_masked"].at(c + 1))
                            if j:
                                pe.wait_ge(n["n_copied"].sem, n["n_copied"].at(c * (ROUNDS - 1) + j))
                            for g in range(2):
                                for m in range(KD):
                                    N_ = G[0:64, g, m, 0:64]
                                    if j < ROUNDS - 1:
                                        pe.matmul(bank(2 + g)[0:64, m * 64:(m + 1) * 64], M[:, g, m, :], N_, start=True, stop=True)
                                    last = pe.matmul(bank(4 + g)[0:64, m * 64:(m + 1) * 64], N_, M[:, g, m, :], start=True, stop=True)
                            last.then_inc(n["squared"].up(), 1)
                            pe.wait_ge(n["m_copied"].sem, n["m_copied"].at(r + 1))
                            if r:
                                pe.wait_ge(n["x_added"].sem, n["x_added"].at(r))
                            for g in range(2):
                                for m in range(KD):
                                    last = pe.matmul(bank(6 + g)[0:64, m * 64:(m + 1) * 64], M[:, g, m, :], X[:, g, m, :], start=True, stop=True)
                            last.then_inc(n["x_step"].up(), 1)
                        pe.wait_ge(n["bk_copied"].sem, n["bk_copied"].at(2 * c + 2))
                        if c:
                            pe.wait_ge(n["state_updated"].sem, n["state_updated"].at(c))
                            for g in range(2):
                                for m in range(KD):
                                    hs = slice(64 * g, 64 * g + 64)
                                    last = pe.matmul(bank(g)[0:64, m * 64:(m + 1) * 64], view[hs, A_, m, c, :], ST[hs, m, :], start=(m == 0), stop=False, skip_group_check=True)
                            last.then_inc(sig("from_state").up(), 1)
                            pe.wait_ge(sig("from_state").sem, sig("from_state").at(c))
                        for g in range(2):
                            for m in range(KD):
                                last = pe.matmul(bank(g)[0:64, m * 64:(m + 1) * 64], G[64:128, g, m, 0:64], UV[64:128, c, g, m, :],
                                                 start=(c == 0 and m == 0), stop=(m == KD - 1), skip_group_check=True)
                        last.then_inc(n["rhs_ready"].up(), 1)
                        pe.wait_ge(n["rhs_copied"].sem, n["rhs_copied"].at(2 * c + 2))
                        pe.wait_ge(n["x_added"].sem, n["x_added"].at((c + 1) * ROUNDS))
                        for g in range(2):
                            for m in range(KD):
                                last = pe.matmul(bank(2 + g)[0:64, m * 64:(m + 1) * 64], X[:, g, m, :], M[:, g, m, :], start=True, stop=True)
                        last.then_inc(n["u_ready"].up(), 1)
                        if c:
                            for g in range(2):
                                for m in range(KD):
                                    hs = slice(64 * g, 64 * g + 64)
                                    pe.matmul(bank(4 + g)[64:128, m * 64:(m + 1) * 64], view[hs, R_, m, c, :], ST[hs, m, :], start=(m == 0), stop=False, skip_group_check=True)
                        pe.wait_ge(n["u_copied"].sem, n["u_copied"].at(2 * c + 2))
                        for g in range(2):
                            for m in range(KD):
                                last = pe.matmul(bank(4 + g)[64:128, m * 64:(m + 1) * 64], G[:, g, m, 64:128], UV[:, c, g, m, :],
                                                 start=(c == 0 and m == 0), stop=(m == KD - 1), skip_group_check=True)
                        last.then_inc(n["y_ready"].up(), 1)
                        for g in range(2):
                            for m in range(KD):
                                last = pe.matmul(bank(6)[64 * g:64 * g + 64, m * 64:(m + 1) * 64], BKt[:, m, 64 * g:64 * g + 64], UV[:, c, g, m, :], start=True, stop=True)
                        last.then_inc(n["state_ready"].up(), 1)
                    z_turn(NCH - 1)

                @block.scalar
                def _(act):
                    def post(c):
                        act.wait_ge(sig("centred").sem, sig("centred").at(c + 1))
                        act.activation(W1, Y, ACT.Square).then_inc(sig("squares_ready").up(), 1)
                        act.wait_ge(sig("mean_square").sem, sig("mean_square").at(c + 1))
                        act.activation(stat[64:128, 32:48], stat[64:128, 16:32], ACT.Sqrt).then_inc(sig("row_root").up(), 1)

                    for c in range(NCH):
                        for f in range(2):
                            act.wait_ge(n["bk_turned"].sem, n["bk_turned"].at(2 * c + f + 1))
                            act.copy(BKt[:, 4 * f:4 * f + 4, :], bank(f).rearrange("p (m s) -> p m s", m=4)).then_inc(n["bk_copied"].up(), 1)
                        if c:
                            post(c - 1)
                        for j in range(ROUNDS - 1):
                            act.wait_ge(n["squared"].sem, n["squared"].at(c * ROUNDS + j + 1))
                            for g in range(2):
                                ins = act.copy(G[0:64, g, :, 0:64], bank(2 + g)[0:64, :].rearrange("p (m s) -> p m s", m=KD))
                            ins.then_inc(n["n_copied"].up(), 1)
                        act.wait_ge(n["rhs_ready"].sem, n["rhs_ready"].at(c + 1))
                        act.wait_ge(n["x_step"].sem, n["x_step"].at((c + 1) * ROUNDS))
                        act.copy(M[:, 0], bank(0)[0:64, :].rearrange("p (m s) -> p m s", m=KD)).then_inc(n["rhs_copied"].up(), 1)
                        act.wait_ge(n["u_ready"].sem, n["u_ready"].at(c + 1))
                        act.copy(UV[0:64, c, 0, :, :], bank(2)[0:64, :].rearrange("p (m s) -> p m s", m=KD)).then_inc(n["u_copied"].up(), 1)
                        act.wait_ge(n["y_ready"].sem, n["y_ready"].at(c + 1))
                        if c:
                            act.wait_ge(n["z_ready"].sem, n["z_ready"].at(c))
                        for g in range(2):
                            act.copy(Y.rearrange("p (m g v) -> p m g v", m=KD, g=2)[:, :, g, :], bank(4 + g)[64:128, :].rearrange("p (m v) -> p m v", m=KD)).then_inc(n["y_copied"].up(), 1)
                    post(NCH - 1)

                @block.vector
                def _(dve):
                    def step(ins):
                        link(dve, "dve_step", ins)

                    def by_head(s):
                        return s.rearrange("p (a o) -> p a o", o=1).broadcast_to([64, HEADS, HD])

                    def rows3(x):
                        return x.rearrange("p (a v) -> p a v", a=HEADS)

                    sm = stat[64:128, 0:16]

                    def post_a(c):
                        dve.wait_ge(n["y_copied"].sem, n["y_copied"].at(2 * c + 2))
                        step(dve.tensor_reduce(sm, rows3(Y), AX, ALU.add))
                        step(dve.tensor_scalar(sm, sm, 1.0 / HD, None, ALU.mult))
                        dve.tensor_tensor(rows3(Y), rows3(Y), by_head(sm), ALU.subtract).then_inc(sig("centred").up(), 1)

                    def post_b(c):
                        dve.wait_ge(sig("squares_ready").sem, sig("squares_ready").at(c + 1))
                        step(dve.tensor_reduce(sm, rows3(W1), AX, ALU.add))
                        dve.tensor_scalar(stat[64:128, 16:32], sm, 1.0 / HD, LNX_EPS, ALU.mult, ALU.add).then_inc(sig("mean_square").up(), 1)
                        v = UV[64:128, c, :, :, :]
                        for g in range(2):
                            s = bonus[64:128, c, g:HEADS:2].rearrange("p (m o) -> p m o", o=1).broadcast_to([64, KD, HD])
                            ins = dve.tensor_tensor(W1.rearrange("p (m g v) -> p m g v", m=KD, g=2)[:, :, g, :], v[:, g], s, ALU.mult)
                        step(ins)
                        step(dve.tensor_tensor(W1, W1, rows[64:128, 1, :], ALU.add))
                        dve.wait_ge(sig("row_root").sem, sig("row_root").at(c + 1))
                        step(dve.reciprocal(stat[64:128, 48:64], stat[64:128, 32:48]))
                        step(dve.tensor_tensor(rows3(Y), rows3(Y), by_head(stat[64:128, 48:64]), ALU.mult))
                        step(dve.tensor_tensor(Y, Y, rows[64:128, 0, :], ALU.mult))
                        if c:
                            dve.wait_ge(n["z_turned"].sem, n["z_turned"].at(c))
                        dve.tensor_tensor(Z, Y, W1, ALU.add).then_inc(n["z_ready"].up(), 1)

                    def post_c(c):
                        dve.wait_ge(n["z_turned"].sem, n["z_turned"].at(c + 1))
                        x = bank(7).rearrange("p (m s) -> p m s", m=KD)
                        dve.tensor_tensor(xT[:, :, c * CHUNK:(c + 1) * CHUNK], x, gT[:, :, c * CHUNK:(c + 1) * CHUNK], ALU.mult).then_inc(n["z_gated"].up(), 1)

                    dve.wait_ge(c_in.sem, c_in.at(64))
                    wide_g = gm.rearrange("p (o s) -> p o s", o=1).broadcast_to([P, 4, P])
                    wide_l = lmask.rearrange("p (o s) -> p o s", o=1).broadcast_to([64, KD, 64])
                    wide_i = ident[0:64, 0:64].rearrange("p (o s) -> p o s", o=1).broadcast_to([64, KD, 64])
                    for c in range(NCH):
                        dve.wait_ge(n["g_ready"].sem, n["g_ready"].at(c + 1))
                        for b in range(4):
                            dve.tensor_tensor(G[:, b // 2, 4 * (b % 2):4 * (b % 2) + 4, :], bank(2 + b).rearrange("p (m s) -> p m s", m=4), wide_g, ALU.mult).then_inc(n["g_masked"].up(), 1)
                        if c:
                            post_b(c - 1)
                            post_c(c - 1)
                        dve.wait_ge(n["m_ready"].sem, n["m_ready"].at(c + 1))
                        for g in range(2):
                            ins = dve.tensor_tensor(M[:, g], bank(6 + g)[0:64, :].rearrange("p (m s) -> p m s", m=KD), wide_l, ALU.mult)
                        ins.then_inc(n["m_masked"].up(), 1)
                        dve.wait_ge(n["g_masked"].sem, n["g_masked"].at(5 * c + 4))
                        for g in range(2):
                            ins = dve.tensor_tensor(X[:, g], G[0:64, g, :, 0:64], wide_i, ALU.add)
                        ins.then_inc(n["g_masked"].up(), 1)
                        for j in range(ROUNDS):
                            r = c * ROUNDS + j
                            dve.wait_ge(n["squared"].sem, n["squared"].at(r + 1))
                            for g in range(2):
                                ins = dve.tensor_copy(M[:, g], bank(4 + g)[0:64, :].rearrange("p (m s) -> p m s", m=KD))
                            ins.then_inc(n["m_copied"].up(), 1)
                            dve.wait_ge(n["x_step"].sem, n["x_step"].at(r + 1))
                            for g in range(2):
                                ins = dve.tensor_tensor(X[:, g], X[:, g], bank(6 + g)[0:64, :].rearrange("p (m s) -> p m s", m=KD), ALU.add)
                            link(dve, "x_added", ins)
                        dve.wait_ge(n["rhs_ready"].sem, n["rhs_ready"].at(c + 1))
                        dve.tensor_copy(M[:, 1], bank(1)[0:64, :].rearrange("p (m s) -> p m s", m=KD)).then_inc(n["rhs_copied"].up(), 1)
                        dve.wait_ge(n["u_ready"].sem, n["u_ready"].at(c + 1))
                        dve.tensor_copy(UV[0:64, c, 1, :, :], bank(3)[0:64, :].rearrange("p (m s) -> p m s", m=KD)).then_inc(n["u_copied"].up(), 1)
                        dve.wait_ge(n["state_ready"].sem, n["state_ready"].at(c + 1))
                        new = bank(6).rearrange("p (m v) -> p m v", m=KD)
                        decay = pc[:, :, c:c + 1].broadcast_to([P, KD, HD])
                        if c:
                            step(dve.tensor_tensor(ST, ST, new, ALU.add))
                            dve.tensor_tensor(ST, ST, decay, ALU.mult).then_inc(n["state_updated"].up(), 1)
                        else:
                            dve.tensor_tensor(ST, new, decay, ALU.mult).then_inc(n["state_updated"].up(), 1)
                        dve.wait_ge(n["state_updated"].sem, n["state_updated"].at(c + 1))
                        post_a(c)
                    post_b(NCH - 1)
                    post_c(NCH - 1)
            project(2, residual=1.0)

        memK, memV = fm(8), tok(9)

        def memory_kv():
            with new_block() as block:
                got = sig("inputs_loaded")

                @block.sync
                def _(sp):
                    sp.dma_start(tok(0), d["mem"].rearrange("(t p) f -> p t f", p=P)).then_inc(got.up(16), 16)
                    sp.dma_start(mask[:], d["chunk_mask"]).then_inc(got.up(16), 16)
                    sp.wait_ge(got.sem, got.at(32))
            transpose_all([(tok(0), fm(1))])
            project_features(fm(1), memK)
            project(2, dest=lambda u, t: memV[:, t, u * COLS:(u + 1) * COLS], src=fm(1))

        def differential():
            project(6, dest=lambda u, t: tok(u // 2)[:, t, (u % 2) * COLS:(u % 2 + 1) * COLS],
                    rotary=lambda u: (8, HD, 0, DIFF_ROPE, cosd, sind, blk(3)) if u < 4 else None)
            transpose_all([(tok(0), fm(3)), (tok(1), fm(4))])

            def hs(m):
                return slice(64 * (m % 2), 64 * (m % 2) + 64)
            o = tok(5)
            attention(16, lambda m, t: [fm(3)[hs(m), m // 2, t * P:(t + 1) * P]], lambda m: [fm(4)[hs(m), m // 2, :]],
                      lambda m, kt: tok(2)[:, kt, (m // 2) * P:(m // 2 + 1) * P], P, lambda m, t: o[:, t, (m // 2) * P:(m // 2 + 1) * P],
                      HD ** -0.5, True, (blk(6), blk(7)), diff=True)
            with new_block() as block:
                sq, ms, root = sig("squares_ready"), sig("mean_square"), sig("row_root")
                o3 = blk(5).rearrange("p (a f) -> p a f", f=P)

                @block.scalar
                def _(act):
                    act.activation(blk(0), blk(5), ACT.Square).then_inc(sq.up(), 1)
                    act.wait_ge(ms.sem, ms.at(1))
                    act.activation(stat[:, 16:32], stat[:, 0:16], ACT.Sqrt).then_inc(root.up(), 1)

                @block.vector
                def _(dve):
                    dve.wait_ge(sq.sem, sq.at(1))
                    link(dve, "dve_step", dve.tensor_reduce(stat[:, 0:16], blk(0).rearrange("p (a f) -> p a f", f=P), AX, ALU.add))
                    dve.tensor_scalar(stat[:, 0:16], stat[:, 0:16], 1.0 / P, LN_EPS, ALU.mult, ALU.add).then_inc(ms.up(), 1)
                    link(dve, "dve_step", dve.tensor_scalar(stat[:, 48:49], col("subln", 0), 1.0 - LAMBDA_INIT, None, ALU.mult))
                    dve.wait_ge(root.sem, root.at(1))
                    link(dve, "dve_step", dve.reciprocal(stat[:, 32:48], stat[:, 16:32]))
                    link(dve, "dve_step", dve.tensor_tensor(o3, o3, stat[:, 32:48].rearrange("p (a o) -> p a o", o=1).broadcast_to([P, 16, P]), ALU.mult))
            transpose_all([(o, xT)], scale=stat[:, 48:49])
            project(2, residual=ALPHA, row_src=(d["ln_g"][0], d["ln_b"][0]))
            norm("ln", LN_EPS, None)

        def cross_attention(layer):
            project_features(xT, fm(0))
            o = tok(1)
            attention(4, lambda m, t: [fm(0)[:, 2 * m + i, t * P:(t + 1) * P] for i in range(2)], lambda m: [memK[:, 2 * m + i, :] for i in range(2)],
                      lambda m, kt: memV[:, kt, m * 256:(m + 1) * 256], 256, lambda m, t: o[:, t, m * 256:(m + 1) * 256],
                      256 ** -0.5, False, (blk(6), blk(7)))
            transpose_all([(o, xT)])
            project(2, residual=ALPHA, row_src=(d["ln_g"][3 * layer + 1], d["ln_b"][3 * layer + 1]))
            norm("ln", LN_EPS, None)

        def mixture(layer, store=None):
            w = blk(0)
            lg, key = w[:, 0:40].rearrange("p (t n) -> p t n", t=T), w[:, 40:48].rearrange("p (t n) -> p t n", t=T)
            gsel, es = w[:, 48:56].rearrange("p (t n) -> p t n", t=T), w[:, 56:64].rearrange("p (t n) -> p t n", t=T)
            eg = w[:, 64:96].rearrange("p (t e g) -> p t e g", t=T, e=4)
            oh1, oh2 = w[:, 96:104].rearrange("p (t n) -> p t n", t=T), w[:, 104:112].rearrange("p (t n) -> p t n", t=T)
            es2, gexp = w[:, 112:120].rearrange("p (t n) -> p t n", t=T), w[:, 120:128].rearrange("p (t n) -> p t n", t=T)
            gmx, kmx, m1, m2 = w[:, 128:130], w[:, 130:132], w[:, 132:134], w[:, 134:136]
            gsum, dm, de, den = w[:, 136:138], w[:, 138:140], w[:, 140:142], w[:, 142:144]
            w1, w2, tmp = w[:, 144:146], w[:, 146:148], w[:, 148:156].rearrange("p (t n) -> p t n", t=T)
            comb = w[:, 160:192].rearrange("p (t g e) -> p t g e", t=T, g=4)
            bias, rank = w[:, 192:212], w[:, 212:216]
            sel, place = w[:, 224:256].rearrange("p (t g e) -> p t g e", t=T, g=4), w[:, 256:288]
            tri, ones, slot_no = w[:, 512:512 + P], w[:, 640:640 + P], w[:, 768:768 + SLOTS_E]
            hid4 = w[:, 1024:2048].rearrange("p (u f s) -> p u f s", u=EPG, f=2)
            put, put_w = blk(2), blk(1)
            xg = arena[:, 3:7, :].rearrange("p a f -> p (a f)").rearrange("p (k n) -> p k n", k=KD)
            swT = blk(7)
            half = PAIRS * SLOTS_E
            with new_block() as block:
                got, mm, e_in, e_out = sig("small_loaded"), sig("product_ready"), sig("max_ready"), sig("exps_ready")
                chosen, placed, tp, ev = sig("experts_chosen"), sig("tokens_placed"), sig("transposed"), [sig("act_evacuated"), sig("dve_evacuated")]

                def copy_out(copy, eng, e):
                    for n in range(e, 2 * KD, 2):
                        eng.wait_ge(mm.sem, mm.at(n + 3))
                        copy(xg[:, n // 2, e * half:(e + 1) * half], bank(2 + n % 4)).then_inc(ev[e].up(), 1)
                    for n in range(e, PAIRS // 2, 2):
                        eng.wait_ge(tp.sem, tp.at(n + 1))
                        copy(swT[:, n * 2 * SEQ:(n + 1) * 2 * SEQ], bank(2 + n))

                @block.sync
                def _(sp):
                    sp.dma_start(bias, d["route_b"][layer].rearrange("(o f) -> o f", o=1).broadcast_to([P, ROUTE])).then_inc(got.up(16), 16)
                    sp.dma_start(w[:, 512:512 + 2 * P + SLOTS_E], d["slots"]).then_inc(got.up(16), 16)
                    sp.dma_start(rank, d["rank"].rearrange("(o f) -> o f", o=1).broadcast_to([P, 4])).then_inc(got.up(16), 16)

                @block.tensor
                def _(pe):
                    for t in range(T):
                        for k in range(KD):
                            last = pe.matmul(bank(0)[:, t * ROUTE:(t + 1) * ROUTE], xT[:, k, t * P:(t + 1) * P], col("route", (layer * KD + k) * ROUTE, ROUTE),
                                             start=(k == 0), stop=(k == KD - 1))
                    last.then_inc(mm.up(), 1)
                    pe.wait_ge(got.sem, got.at(48))
                    pe.wait_ge(chosen.sem, chosen.at(1))
                    s0, s1 = [sel[:, t].rearrange("p g e -> p (g e)") for t in range(T)]
                    n = N_EXPERTS
                    pe.matmul(bank(1)[:, 0:n], tri, s0, start=True, stop=True)
                    for o, a in ((n, tri), (2 * n, ones)):
                        pe.matmul(bank(1)[:, o:o + n], a, s1, start=True, stop=False)
                        last = pe.matmul(bank(1)[:, o:o + n], ones, s0, start=False, stop=True)
                    last.then_inc(mm.up(), 1)
                    pe.wait_ge(placed.sem, placed.at(1))
                    for n in range(2 * KD):
                        if n >= 4:
                            pe.wait_ge(ev[n % 2].sem, ev[n % 2].at(n // 2 - 1))
                        k, c = n // 2, n % 2
                        for t in range(T):
                            last = pe.matmul(bank(2 + n % 4), h[:, t, k * P:(k + 1) * P], put[:, t * D + c * half:t * D + (c + 1) * half], start=(t == 0), stop=(t == T - 1))
                        last.then_inc(mm.up(), 1)
                    pe.wait_ge(placed.sem, placed.at(2))
                    for n in range(PAIRS // 2):
                        pe.wait_ge(ev[n % 2].sem, ev[n % 2].at(KD - 1 + n // 2))
                        for q in range(2):
                            for t in range(T):
                                last = pe.transpose(bank(2 + n)[:, (q * T + t) * P:(q * T + t + 1) * P], put_w[:, t * D + (2 * n + q) * P:t * D + (2 * n + q + 1) * P], ident[:])
                        last.then_inc(tp.up(), 1)

                @block.scalar
                def _(act):
                    act.wait_ge(e_in.sem, e_in.at(1))
                    act.activation(gexp, gexp, ACT.Exp).then_inc(e_out.up(), 1)
                    act.wait_ge(e_in.sem, e_in.at(2))
                    act.activation(de, dm, ACT.Exp).then_inc(e_out.up(), 1)
                    copy_out(act.copy, act, 0)

                @block.vector
                def _(dve):
                    def step(ins):
                        link(dve, "dve_step", ins)

                    def w4(x):
                        return x.rearrange("p (t o) -> p t o", o=1).broadcast_to([P, T, 4])

                    wr = rank.rearrange("p (o n) -> p o n", o=1).broadcast_to([P, T, 4])

                    def first_max(x, m, onehot):
                        step(dve.tensor_reduce(m, x, AX, ALU.max))
                        step(dve.tensor_tensor(key, x, w4(m), ALU.is_equal))
                        step(dve.tensor_tensor(key, key, wr, ALU.mult))
                        step(dve.tensor_reduce(kmx, key, AX, ALU.max))
                        step(dve.tensor_tensor(onehot, key, w4(kmx), ALU.is_equal))

                    dve.wait_ge(mm.sem, mm.at(1))
                    dve.wait_ge(got.sem, got.at(48))
                    step(dve.tensor_tensor(lg, bank(0)[:, 0:T * ROUTE].rearrange("p (t n) -> p t n", t=T), bias.rearrange("p (o n) -> p o n", o=1).broadcast_to([P, T, ROUTE]), ALU.add))
                    first_max(lg[:, :, 0:4], gmx, gsel)
                    dve.tensor_tensor(gexp, lg[:, :, 0:4], w4(gmx), ALU.subtract).then_inc(e_in.up(), 1)
                    for t in range(T):
                        el = lg[:, t, 4:ROUTE].rearrange("p (g e) -> p e g", g=4)
                        ins = dve.tensor_tensor(eg[:, t], el, gsel[:, t:t + 1, :].broadcast_to([P, 4, 4]), ALU.mult)
                    step(ins)
                    step(dve.tensor_reduce(es, eg, AX, ALU.add))
                    first_max(es, m1, oh1)
                    step(dve.scalar_tensor_tensor(es2, oh1, MASKED, es, ALU.mult, ALU.add))
                    first_max(es2, m2, oh2)
                    dve.tensor_tensor(dm, m2, m1, ALU.subtract).then_inc(e_in.up(), 1)
                    step(dve.tensor_tensor(tmp, oh1, oh2, ALU.add))
                    for t in range(T):
                        g = gsel[:, t, :].rearrange("p (g o) -> p g o", o=1).broadcast_to([P, 4, 4])
                        ins = dve.tensor_tensor(sel[:, t], tmp[:, t:t + 1, :].broadcast_to([P, 4, 4]), g, ALU.mult)
                    ins.then_inc(chosen.up(), 1)
                    dve.memset(hid4, 0.0)
                    dve.wait_ge(e_out.sem, e_out.at(2))
                    step(dve.tensor_reduce(gsum, gexp, AX, ALU.add))
                    step(dve.tensor_scalar(den, de, 1.0, None, ALU.add))
                    step(dve.tensor_tensor(den, den, gsum, ALU.mult))
                    step(dve.reciprocal(w1, den))
                    step(dve.tensor_tensor(w2, w1, de, ALU.mult))
                    step(dve.tensor_tensor(oh1, oh1, w4(w1), ALU.mult))
                    step(dve.tensor_tensor(oh2, oh2, w4(w2), ALU.mult))
                    step(dve.tensor_tensor(tmp, oh1, oh2, ALU.add))
                    for t in range(T):
                        g = gsel[:, t, :].rearrange("p (g o) -> p g o", o=1).broadcast_to([P, 4, 4])
                        ins = dve.tensor_tensor(comb[:, t], tmp[:, t:t + 1, :].broadcast_to([P, 4, 4]), g, ALU.mult)
                    step(ins)
                    dve.wait_ge(mm.sem, mm.at(2))
                    step(dve.scalar_tensor_tensor(place, bank(1)[:, 0:T * N_EXPERTS], 1.0, w[:, 224:256], ALU.add, ALU.mult))
                    put3, put_w3 = [x.rearrange("p (a s) -> p a s", s=SLOTS_E) for x in (put, put_w)]

                    def by_expert(x):
                        return x.rearrange("p (a o) -> p a o", o=1).broadcast_to([P, T * N_EXPERTS, SLOTS_E])
                    ins = dve.tensor_tensor(put3, by_expert(place), slot_no.rearrange("p (o s) -> p o s", o=1).broadcast_to([P, T * N_EXPERTS, SLOTS_E]), ALU.is_equal)
                    ins.then_inc(placed.up(), 1)
                    dve.wait_ge(placed.sem, placed.at(1))
                    dve.tensor_tensor(put_w3, put3, by_expert(w[:, 160:192]), ALU.mult).then_inc(placed.up(), 1)
                    step(dve.tensor_reduce(stat[:, 0:1], bank(1)[:, T * N_EXPERTS:(T + 1) * N_EXPERTS], AX, ALU.max))
                    dve.tensor_scalar(overflow[:], stat[:, 0:1], float(SLOTS_E), None, ALU.is_gt)
                    copy_out(dve.tensor_copy, dve, 1)
            experts(layer, comb, hid4, xg, swT, (d["ln_g"][3 * layer + 2], d["ln_b"][3 * layer + 2]))
            norm("ln", LN_EPS, None, store=store)

        def sparse_mla():
            cin = arena[:, 0:2, :].rearrange("p a f -> p (a f)")[:, 0:T * 640].rearrange("p (t f) -> p t f", t=T)
            kpad = blk(1)[:, 1024:2048].rearrange("p (t a f) -> p t a f", t=T, a=4)
            cT = blk(2)[:, 0:1024].rearrange("p (k s) -> p k s", k=4)
            kiT = blk(2)[:, 1024:1280]
            q_tok, qi_tok, v_tok = tok(3), tok(4), tok(5)
            qT, kT, qiT = fm(6), fm(7), xT
            j0 = next_unit(1)
            with new_block() as block:
                mm, ev, dv = sig("product_ready"), sig("act_evacuated"), sig("dve_evacuated")
                sq, ms, root, ready, tp = sig("row_stats"), sig("mean_square"), sig("row_root"), sig("normed"), sig("transposed")
                ss = stat[:, 0:4].rearrange("p (t a) -> p t a", t=T)
                halves = (0, B_IN // 2, B_IN)

                @block.tensor
                def _(pe):
                    arrived(pe, j0)
                    w = ring[:, j0 % SLOTS, 0:KD * B_IN].rearrange("p (k n) -> p k n", k=KD)
                    for t in range(T):
                        for c in range(2):
                            for k in range(KD):
                                last = pe.matmul(bank(2 * t + c)[:, 0:B_IN // 2], xT[:, k, t * P:(t + 1) * P], w[:, k, halves[c]:halves[c + 1]], start=(k == 0), stop=(k == KD - 1))
                            last.then_inc(mm.up(), 1)
                    unit_done(j0, mm)
                    for t in range(T):
                        pe.wait_ge(ready.sem, ready.at(t + 1))
                        for k in range(4):
                            last = pe.transpose(bank(4 + t)[:, k * P:(k + 1) * P], cin[:, t, k * P:(k + 1) * P], ident[:])
                        last.then_inc(tp.up(), 1)
                    pe.wait_ge(ready.sem, ready.at(T + 1))
                    for a in range(2):
                        for t in range(T):
                            last = pe.transpose(bank(6)[:, (a * T + t) * P:(a * T + t + 1) * P], kpad[:, t, a, :], ident[:])
                    last.then_inc(tp.up(), 1)

                @block.scalar
                def _(act):
                    for t in range(T):
                        for c in range(2):
                            act.wait_ge(mm.sem, mm.at(2 * t + c + 1))
                            act.copy(cin[:, t, halves[c]:halves[c + 1]], bank(2 * t + c)[:, 0:B_IN // 2]).then_inc(ev.up(), 1)
                    act.wait_ge(ev.sem, ev.at(4))
                    for t in range(T):
                        for a in range(2):
                            act.activation(blk(3)[:, (2 * t + a) * 256:(2 * t + a + 1) * 256], cin[:, t, a * 256:(a + 1) * 256], ACT.Square, accum_out=ss[:, t, a:a + 1]).then_inc(sq.up(), 1)
                    act.wait_ge(ms.sem, ms.at(1))
                    act.activation(stat[:, 8:12], stat[:, 4:8], ACT.Sqrt).then_inc(root.up(), 1)
                    act.wait_ge(tp.sem, tp.at(T + 1))
                    for hd in range(KD):
                        act.copy(kT[96:128, hd, :], bank(6)[96:128, 0:SEQ])
                    act.copy(kiT, bank(6)[:, SEQ:2 * SEQ])

                @block.vector
                def _(dve):
                    def step(ins):
                        link(dve, "dve_step", ins)
                    step(dve.memset(kpad, 0.0))
                    dve.wait_ge(sq.sem, sq.at(4))
                    dve.tensor_scalar(stat[:, 4:8], stat[:, 0:4], 1.0 / Q_RANK, LN_EPS, ALU.mult, ALU.add).then_inc(ms.up(), 1)
                    dve.wait_ge(root.sem, root.at(1))
                    step(dve.reciprocal(stat[:, 12:16], stat[:, 8:12]))
                    for t in range(T):
                        for a in range(2):
                            x = cin[:, t, a * 256:(a + 1) * 256]
                            ins = dve.tensor_scalar(x, x, stat[:, 12 + 2 * t + a:13 + 2 * t + a], None, ALU.mult)
                        ins.then_inc(ready.up(), 1)
                    tmp = blk(3)[:, 1024:1536]
                    r0 = Q_RANK + KV_RANK
                    for t in range(T):
                        step(rope(dve, cin[:, t, r0:r0 + 32], 1, 32, 0, MLA_ROPE, cosr[:, t, :], sinr[:, t, :], tmp))
                        step(rope(dve, cin[:, t, r0 + 32:r0 + 96], 1, 64, 0, DIFF_ROPE, cosd[:, t, :], sind[:, t, :], tmp))
                        dve.tensor_copy(kpad[:, t, 0, 96:128], cin[:, t, r0:r0 + 32])
                        for a in range(2):
                            ins = dve.tensor_copy(kpad[:, t, 1, a * 64:(a + 1) * 64], cin[:, t, r0 + 32:r0 + 96])
                        step(ins)
                        x = cin[:, t, r0 + 96:r0 + 112]
                        step(dve.tensor_scalar(x, x, (IDX_HEADS * IDX_DIM) ** -0.5, None, ALU.mult))
                    dve.tensor_scalar(kpad[:, 0, 2, 0:1], kpad[:, 0, 2, 0:1], 1.0, None, ALU.mult).then_inc(ready.up(), 1)
                    for t in range(T):
                        dve.wait_ge(tp.sem, tp.at(t + 1))
                        for a, g in enumerate(("q_norm", "kv_norm")):
                            g3 = col(g, 0, 2).rearrange("p (k o) -> p k o", o=1).broadcast_to([P, 2, P])
                            dve.tensor_tensor(cT[:, 2 * a:2 * a + 2, t * P:(t + 1) * P], bank(4 + t)[:, a * 256:(a + 1) * 256].rearrange("p (k s) -> p k s", k=2), g3, ALU.mult)
                stream(block, 1)
            j0 = next_unit(2)
            with new_block() as block:
                mm, ev = sig("product_ready"), sig("act_evacuated")

                @block.tensor
                def _(pe):
                    n = 0
                    arrived(pe, j0)
                    w = ring[:, j0 % SLOTS, 0:4096].rearrange("p (a k n) -> p a k n", a=2, k=2)
                    for a in range(2):
                        for c in range(2):
                            for t in range(T):
                                if n >= 8:
                                    pe.wait_ge(ev.sem, ev.at(n - 7))
                                for k in range(2):
                                    last = pe.matmul(bank(n % 8), cT[:, k, t * P:(t + 1) * P], w[:, a, k, c * 512:(c + 1) * 512], start=(k == 0), stop=(k == 1))
                                last.then_inc(mm.up(), 1)
                                n += 1
                    unit_done(j0, mm)
                    arrived(pe, j0 + 1)
                    wk = ring[:, (j0 + 1) % SLOTS, 0:1536].rearrange("p (k n) -> p k n", k=2)
                    wv = ring[:, (j0 + 1) % SLOTS, 1536:3584].rearrange("p (k n) -> p k n", k=2)
                    for hd in range(KD):
                        if hd % 2 == 0:
                            pe.wait_ge(ev.sem, ev.at(n - 7))
                        for k in range(2):
                            last = pe.matmul(bank(n % 8)[0:MLA_NOPE, (hd % 2) * SEQ:(hd % 2 + 1) * SEQ], wk[:, k, hd * MLA_NOPE:(hd + 1) * MLA_NOPE], cT[:, 2 + k, :], start=(k == 0), stop=(k == 1))
                        if hd % 2:
                            last.then_inc(mm.up(), 1)
                            n += 1
                    for c in range(2):
                        for t in range(T):
                            pe.wait_ge(ev.sem, ev.at(n - 7))
                            for k in range(2):
                                last = pe.matmul(bank(n % 8), cT[:, 2 + k, t * P:(t + 1) * P], wv[:, k, c * 512:(c + 1) * 512], start=(k == 0), stop=(k == 1))
                            last.then_inc(mm.up(), 1)
                            n += 1
                    unit_done(j0 + 1, mm)
                stream(block, 2)

                @block.scalar
                def _(act):
                    n = 0
                    for a in (q_tok, qi_tok):
                        for c in range(2):
                            for t in range(T):
                                act.wait_ge(mm.sem, mm.at(n + 1))
                                act.copy(a[:, t, c * 512:(c + 1) * 512], bank(n % 8)).then_inc(ev.up(), 1)
                                n += 1
                    for hd in range(0, KD, 2):
                        act.wait_ge(mm.sem, mm.at(n + 1))
                        act.copy(kT[0:96, hd:hd + 2, :], bank(n % 8)[0:96, :].rearrange("p (a s) -> p a s", a=2)).then_inc(ev.up(), 1)
                        n += 1
                    for c in range(2):
                        for t in range(T):
                            act.wait_ge(mm.sem, mm.at(n + 1))
                            act.copy(v_tok[:, t, c * 512:(c + 1) * 512], bank(n % 8)).then_inc(ev.up(), 1)
                            n += 1

                @block.vector
                def _(dve):
                    tmp = blk(2)[:, 1280:2048]
                    for t in range(T):
                        dve.wait_ge(ev.sem, ev.at(4))
                        link(dve, "dve_step", rope(dve, q_tok[:, t, :], 8, P, MLA_NOPE, MLA_ROPE, cosr[:, t, :], sinr[:, t, :], tmp))
                    for t in range(T):
                        dve.wait_ge(ev.sem, ev.at(8))
                        link(dve, "dve_step", rope(dve, qi_tok[:, t, :], 16, IDX_DIM, 0, DIFF_ROPE, cosd[:, t, :], sind[:, t, :], tmp))
            transpose_all([(q_tok, qT), (qi_tok, qiT)])
            score, left, relu = (blk(3)[:, a:a + 512].rearrange("p (t s) -> p t s", t=T) for a in (0, 512, 1024))
            relus = blk(3)[:, 1024:2048].rearrange("p (b t s) -> p b t s", b=2, t=T)
            top8 = stat[:, 0:16].rearrange("p (t n) -> p t n", t=T)
            with new_block() as block:
                mm, ev, dv = sig("product_ready"), sig("act_evacuated"), sig("dve_evacuated")

                @block.tensor
                def _(pe):
                    for i in range(IDX_HEADS):
                        hs = slice(64 * (i % 2), 64 * (i % 2) + 64)
                        if i >= 2:
                            pe.wait_ge(ev.sem, ev.at(i - 1))
                        for t in range(T):
                            last = pe.matmul(bank(i % 2)[:, t * SEQ:(t + 1) * SEQ], qiT[hs, i // 2, t * P:(t + 1) * P], kiT[hs, :], start=True, stop=True)
                        last.then_inc(mm.up(), 1)

                @block.scalar
                def _(act):
                    for i in range(IDX_HEADS):
                        act.wait_ge(mm.sem, mm.at(i + 1))
                        if i >= 2:
                            act.wait_ge(dv.sem, dv.at(T * (i - 1)))
                        act.activation(relus[:, i % 2], bank(i % 2).rearrange("p (t s) -> p t s", t=T), ACT.Relu).then_inc(ev.up(), 1)

                @block.vector
                def _(dve):
                    w0 = Q_RANK + KV_RANK + MLA_ROPE + IDX_DIM
                    for i in range(IDX_HEADS):
                        dve.wait_ge(ev.sem, ev.at(i + 1))
                        for t in range(T):
                            if i:
                                dve.wait_ge(dv.sem, dv.at(T * (i - 1) + t + 1))
                            wi = cin[:, t, w0 + i:w0 + i + 1]
                            if i == 0:
                                dve.tensor_scalar(score[:, t, :], relus[:, 0, t, :], wi, None, ALU.mult).then_inc(dv.up(), 1)
                            else:
                                dve.scalar_tensor_tensor(score[:, t, :], relus[:, i % 2, t, :], wi, score[:, t, :], ALU.mult, ALU.add).then_inc(dv.up(), 1)
                    dve.wait_ge(dv.sem, dv.at(T * IDX_HEADS))
                    link(dve, "dve_step", dve.tensor_tensor(left, score, mask[:], ALU.add))
                    for _ in range(TOPK // 8):
                        for t in range(T):
                            ins = dve.max(top8[:, t, :], left[:, t, :])
                        link(dve, "dve_step", ins)
                        for t in range(T):
                            ins = dve.match_replace(left[:, t, :], top8[:, t, :], left[:, t, :], TAKEN)
                        link(dve, "dve_step", ins)
                    dve.tensor_scalar(mask[:], left, TAKEN / 2, MASKED, ALU.is_gt, ALU.mult)
            attention(KD, lambda m, t: [qT[:, m, t * P:(t + 1) * P]], lambda m: [kT[:, m, :]], lambda m, kt: v_tok[:, kt, m * P:(m + 1) * P], P,
                      lambda m, t: tok(4)[:, t, m * P:(m + 1) * P], (MLA_ROPE + MLA_NOPE) ** -0.5, True, (blk(0), blk(1)))
            transpose_all([(tok(4), xT)])
            project(2, residual=ALPHA, row_src=(d["ln_g"][3], d["ln_b"][3]))
            norm("ln", LN_EPS, None)

        first_attention()
        norm("rms", RMS_EPS, tok(0), gains=col("norm_ffn", 0, KD))
        ffn_stage(FU, 0)
        rwkv()
        norm("rms", RMS_EPS, tok(0), gains=col("norm_ffn", KD, KD))
        ffn_stage(FU, 1, row_src=(d["norm_final"],))
        norm("rms_rows", RMS_EPS, tok(0))
        memory_kv()
        differential()
        cross_attention(0)
        mixture(0)
        sparse_mla()
        cross_attention(1)
        mixture(1, store=out)


def _units(w, width):
    k, n = w.shape
    return w.reshape(k // P, P, n // width, width).transpose(2, 1, 0, 3).reshape(n // width, P, k // P * width)


def _ffn_units(gate, up, down):
    n = gate.shape[1] // (2 * P)
    dn = down.reshape(n, 2, P, D).transpose(0, 2, 1, 3).reshape(n, P, 2 * D)
    return np.concatenate([_units(gate, 2 * P), _units(up, 2 * P), dn], axis=2)


def _features(v):
    return v.reshape(-1, P).T


def _rows(w):
    return w.reshape(-1, P, w.shape[-1]).transpose(1, 0, 2).reshape(P, -1)


def _constants():
    f = np.float32
    pos = np.arange(SEQ, dtype=f)
    e0 = np.arange(0, HD, 2, dtype=f) / f(HD)
    inv0 = f(1) / (10000.0 ** e0.astype(np.float64)).astype(f)
    ang = (pos[:, None] * inv0[None, :]).astype(np.float64)
    c, s = np.cos(ang).astype(f), np.sin(ang).astype(f)

    def by_token(a):
        return np.ascontiguousarray(a.reshape(T, P, -1).transpose(1, 0, 2))

    def inv(rot):
        e = np.arange(0, rot, 2, dtype=f) / f(rot)
        return (500000.0 ** (-e.astype(np.float64))).astype(f)
    i = np.arange(SEQ)
    head = np.arange(D) // HD
    onehot = (head[:, None] == np.arange(HEADS)[None, :]).astype(f)
    s_, t_ = np.arange(CHUNK)[:, None], np.arange(CHUNK)[None, :]
    before, upto = (s_ < t_).astype(f), (s_ <= t_).astype(f)
    return {
        "ident": np.eye(P, dtype=f),
        "causal": by_token(np.where(i[None, :] <= i[:, None], 0, MASKED).astype(f)),
        "chunk_mask": by_token(np.where(i[None, :] // CHUNK <= i[:, None] // CHUNK, 0, MASKED).astype(f)),
        "cos0": by_token(np.concatenate([c, c], 1)), "sin0": by_token(np.concatenate([-s, s], 1)),
        "inv": np.concatenate([inv(DIFF_ROPE), inv(MLA_ROPE)]),
        "spread": np.ascontiguousarray(onehot.T.reshape(HEADS, KD, P)), "heads16": np.ascontiguousarray(onehot.reshape(KD, P, HEADS).transpose(1, 0, 2)),
        "pair": np.ascontiguousarray(onehot[0:P, 0:2]), "reset": np.tile((np.arange(SEQ) % CHUNK != 0).astype(f), (P, 1)),
        "gmask": np.tile(np.concatenate([before, upto], 1), (2, 1)), "lmask": np.ascontiguousarray(before.T),
        "rank": np.array([4, 3, 2, 1], f),
        "slots": np.concatenate([np.triu(np.ones((P, P), f), 1), np.ones((P, P), f), np.tile(np.arange(1, SLOTS_E + 1, dtype=f), (P, 1))], 1),
    }


def _pack(a):
    cols = np.concatenate([_features(a["norm_mix"]), _features(a["norm_ffn"]), _features(a["rwkv_mu"]), _features(a["rwkv_w0"]), _features(a["rwkv_a0"]),
                           _features(a["rwkv_k_k"]), _features(a["rwkv_k_a"]), _features(a["rwkv_r_k"].reshape(-1)), _features(a["ffn_conv_w"]),
                           _features(a["ffn_conv_b"]), _features(a["a_subln_g_2"]), _features(a["b_q_norm_g_2"]), _features(a["b_kv_norm_g_2"]),
                           *[_rows(np.concatenate([a["moe_w_group_2"][i], a["moe_w_expert_2"][i]], 1)) for i in range(2)]], axis=1)
    rkv = a["rwkv_w_rkv"][0]
    w_proj = np.concatenate([_units(w, COLS) for w in (
        a["attn_w_qkv"][0], a["attn_w_o"][0], rkv[0], rkv[1], rkv[2], a["rwkv_w_o"][0], a["mem_w_kv_2"], a["a_w_in_2"][0], a["a_w_out_2"][0],
        a["xa_w_q_2"][0], a["xa_w_out_2"][0], a["b_w_out_2"][0], a["xa_w_q_2"][1], a["xa_w_out_2"][1])])
    z = np.zeros((P - 64, D), np.float32)
    lora = np.concatenate([_rows(a["rwkv_w1"][0]), _rows(a["rwkv_a1"][0]), _rows(a["rwkv_g1"][0]), np.concatenate([a["rwkv_w2"][0], z]),
                           np.concatenate([a["rwkv_a2"][0], z]), a["rwkv_g2"][0]], axis=1)
    uq = a["b_w_uq_2"][0].reshape(Q_RANK, KD, P)
    uq = np.concatenate([uq[:, :, MLA_ROPE:], uq[:, :, :MLA_ROPE]], 2).reshape(Q_RANK, D)
    uk = a["b_w_uk_2"][0].transpose(1, 0, 2).reshape(KV_RANK, -1)
    uv = a["b_w_uv_2"][0].transpose(1, 0, 2).reshape(KV_RANK, -1)

    moe = np.concatenate([_ffn_units(a["moe_w_gate_2"][l, e], a["moe_w_up_2"][l, e], a["moe_w_down_2"][l, e]) for l in range(2) for e in range(N_EXPERTS)])
    arrays = {
        "x": a["x"][0], "mem": a["mem_2"][0], "pos": a["positions_2"].reshape(T, P).T, "cols": cols, "w_proj": w_proj, "w_lora": lora,
        "w_ffn": np.concatenate([_ffn_units(a["ffn_w_gate"][i], a["ffn_w_up"][i], a["ffn_w_down"][i]) for i in range(2)]), "w_moe": moe,
        "w_b_in": _rows(a["b_w_in_2"][0]), "w_uq": np.concatenate([_rows(uq), _rows(a["b_w_qidx_2"][0])], 1), "w_ukv": np.concatenate([_rows(uk), _rows(uv)], 1),
        "lam": a["a_lambda_2"][0].reshape(-1), "ln_g": a["ln_g_2"].reshape(6, D), "ln_b": a["ln_b_2"].reshape(6, D), "norm_final": a["norm_final"],
        "lnx_w": a["rwkv_lnx_w"][0], "lnx_b": a["rwkv_lnx_b"][0],
        "route_b": np.concatenate([a["moe_b_group_2"], a["moe_b_expert_2"]], 1),
    }
    return {k: np.ascontiguousarray(v) for k, v in arrays.items()} | _constants()


def kernel(**inputs):
    import concourse.bacc as bacc
    from concourse.bass_utils import run_bass_kernel_spmd as run

    arrays = _pack({k: np.asarray(v) for k, v in inputs.items()})
    nc = bacc.Bacc("TRN2", target_bir_lowering=False, num_devices=1)
    d = {n: nc.dram_tensor(f"in_{n}", v.shape, mybir.dt.from_np(v.dtype), kind="ExternalInput").ap() for n, v in arrays.items()}
    out = nc.dram_tensor("out_0", (SEQ, D), F32, kind="ExternalOutput").ap()
    build_program(nc, d, out)
    r = run(nc, [{f"in_{n}": v for n, v in arrays.items()}], core_ids=[0])
    return r.results[0]["out_0"].reshape(1, SEQ, D)
```

```python
import math
from contextlib import ExitStack, contextmanager

import numpy as np
import concourse.bass as bass
from concourse import mybir

F32 = mybir.dt.float32
F32R = mybir.dt.float32r
I32 = mybir.dt.int32
ALU = mybir.AluOpType
ACT = mybir.ActivationFunctionType
AX = mybir.AxisListType.X

P = 128
SEQ = 256
D = 1024
T = SEQ // P
KD = D // P
COLS = 512
F_FF = ((8 * D // 3 + 127) // 128) * 128
FT = F_FF // P
FU = FT // 2
N_EXPERTS, N_GROUPS, PER_GROUP, EXPERT_FF = 16, 4, 4, 512
EU = N_EXPERTS * EXPERT_FF // (2 * P)
EPG = 4
SLOTS_E = 64
PAIRS = N_EXPERTS // 2
UNIT = 2 * KD * 2 * P + 2 * D
SLOTS = 4
CHUNK = 64
NCH = SEQ // CHUNK
HEADS, HD = 16, 64
ALPHA = 4.0 ** 0.25
LN_EPS, RMS_EPS, LNX_EPS = 1e-5, 1e-6, 64e-5
DECAY = -math.exp(-0.5)
LAMBDA_INIT = 0.8 - 0.6 * math.exp(-0.3 * 0)
MASKED = -1e30
TAKEN = -3e38
TOPK = min(256, SEQ // 4)
Q_RANK, KV_RANK, MLA_ROPE, MLA_NOPE, IDX_DIM, IDX_HEADS = 256, 256, 32, 96, 64, 16
B_IN = Q_RANK + KV_RANK + MLA_ROPE + IDX_DIM + IDX_HEADS
DIFF_ROPE = 16
ROUTE = N_GROUPS + N_EXPERTS
BLK = 2048

_COLS = [("norm_mix", 2 * KD), ("norm_ffn", 2 * KD), ("mu", 6 * KD), ("w0", KD), ("a0", KD), ("k_k", KD),
         ("k_a", KD), ("r_k", KD), ("conv_w", 2 * 3 * FT), ("conv_b", 2 * FT), ("subln", 1),
         ("norm_final", KD), ("q_norm", 2), ("kv_norm", 2), ("route", 2 * KD * ROUTE)]
COL, _at = {}, 0
for _n, _w in _COLS:
    COL[_n] = _at
    _at += _w
N_COLS = _at
COL["ln_g"], COL["ln_b"] = 0, 6 * KD
LN_COLS = 2 * 6 * KD


class Signal:

    def __init__(self, sem):
        self.sem, self.base, self.count = sem, 0, 0

    def up(self, step=1, runs=1):
        self.count += step * runs
        return self.sem

    def at(self, n):
        return self.base + n


def build_program(nc, d, out):
    with ExitStack() as ctx:
        def sb(name, shape, dt=F32):
            return ctx.enter_context(nc.sbuf_tensor(name, shape, dt))

        ring = sb("ring", [P, SLOTS, UNIT])
        h = sb("h", [P, T, D])
        xT = sb("xT", [P, KD, SEQ])
        rows = sb("rows", [P, 2, D])
        ident = sb("ident", [P, P])
        cols = sb("cols", [P, N_COLS])
        mask = sb("mask", [P, T, SEQ])
        cos0, sin0 = sb("cos0", [P, T, HD]), sb("sin0", [P, T, HD])
        cosd, sind = sb("cosd", [P, T, DIFF_ROPE]), sb("sind", [P, T, DIFF_ROPE])
        cosr, sinr = sb("cosr", [P, T, MLA_ROPE]), sb("sinr", [P, T, MLA_ROPE])
        stat = sb("stat", [P, 128])
        overflow = sb("overflow", [P, 1], I32)
        nlam = sb("nlam", [P, 1])
        bonus = sb("bonus", [P, NCH, HEADS])
        posn = sb("posn", [P, T], I32)

        PARTS = (range(0, 3), range(3, 6), range(6, 10))
        parts, opened = [], [0]

        def open_part():
            space = ExitStack()
            n = len(PARTS[len(parts)])
            parts.append((space, space.enter_context(nc.sbuf_tensor(f"arena{len(parts)}_{opened[0]}", [P, n, BLK], F32))))
            opened[0] += 1

        def close_part():
            parts.pop()[0].close()

        def span(a, b):
            i = next(i for i, r in enumerate(PARTS) if a in r)
            return parts[i][1][:, a - PARTS[i][0]:b - PARTS[i][0], :].rearrange("p a f -> p (a f)")

        for _ in PARTS:
            open_part()

        @ctx.callback
        def close_parts():
            while parts:
                close_part()
        ps = ctx.enter_context(nc.psum_tensor("ps", [P, 8, 512], F32))

        def bank(b):
            return ps[:, b, :]

        def blk(i):
            return span(i, i + 1)

        def tok(i):
            return blk(i).rearrange("p (t f) -> p t f", t=T)

        def fm(i):
            return blk(i).rearrange("p (k s) -> p k s", k=KD)

        def col(name, i, n=1):
            return cols[:, COL[name] + i:COL[name] + i + n]

        signals = {}

        def sig(name):
            if name not in signals:
                signals[name] = Signal(ctx.enter_context(nc.semaphore(name)))
            return signals[name]

        def new_block():
            for s in signals.values():
                s.base = s.count
            return nc.Block(no_gpsimd_drain=True)

        def link(eng, name, ins, step=1):
            s = sig(name)
            ins.then_inc(s.up(step), step)
            eng.wait_ge(s.sem, s.count)

        proj, ffn, moe = d["w_proj"], d["w_ffn"], d["w_moe"]
        n_proj = [0]

        def take(n):
            n_proj[0] += n
            return [proj[n_proj[0] - n + i] for i in range(n)]

        loads = take(6) + take(2)
        loads += [ffn[i] for i in range(FU)]
        loads += take(6) + [d["w_lora"]] + take(2)
        loads += [ffn[FU + i] for i in range(FU)]
        loads += take(4) + take(6) + take(2)
        loads += take(4)
        moe_at = [len(loads)]
        loads += [moe[i] for i in range(EU)]
        loads += [d["w_b_in"], d["w_uq"], d["w_ukv"]] + take(2) + take(4)
        moe_at.append(len(loads))
        loads += [moe[EU + i] for i in range(EU)]
        loaded = [sig(f"weights_loaded{s}") for s in range(SLOTS)]
        pos = {"issued": 0, "unit": 0}
        release = {}

        def load(sp, j):
            if j >= SLOTS:
                sem, value = release[j - SLOTS]
                sp.wait_ge(sem, value)
            w = loads[j].shape[-1]
            sp.dma_start(ring[:, j % SLOTS, 0:w], loads[j]).then_inc(loaded[j % SLOTS].up(16), 16)

        def stream(block, n):
            first = pos["issued"]
            last = min(first + n, len(loads))
            pos["issued"] = last

            @block.sync
            def _(sp):
                for j in range(first, last):
                    load(sp, j)

        def arrived(pe, j):
            pe.wait_ge(loaded[j % SLOTS].sem, 16 * (j // SLOTS + 1))

        def unit_done(j, signal):
            release[j] = signal.sem, signal.count

        def next_unit(n=1):
            pos["unit"] += n
            return pos["unit"] - n

        bn, mv = stat[:, 8:32].rearrange("p (t c s) -> p t c s", t=T, c=2), stat[:, 32:36].rearrange("p (t s) -> p t s", t=T)
        unscaled = []

        def row_stats(dve, t, c):
            return dve.bn_stats(bn[:, t, c, :], h[:, t, c * 512:(c + 1) * 512])

        def add_residual(dve, t, c, scale, product):
            x = h[:, t, c * 512:(c + 1) * 512]
            link(dve, "dve_step", dve.scalar_tensor_tensor(x, x, scale, product, ALU.mult, ALU.add))
            return row_stats(dve, t, c)

        def scale_rows(dve):
            rows_in = sig("rows_loaded")
            for bias in unscaled:
                dve.wait_ge(rows_in.sem, rows_in.base)
                for t in range(T):
                    ins = dve.tensor_tensor(h[:, t, :], h[:, t, :], rows[:, 0, :], ALU.mult)
                link(dve, "dve_step", ins)
                if bias:
                    for t in range(T):
                        ins = dve.tensor_tensor(h[:, t, :], h[:, t, :], rows[:, 1, :], ALU.add)
                    link(dve, "dve_step", ins)
            unscaled.clear()

        def norm(kind, gain, bias=None, z=None, first=False, store=None):
            src = z if kind == "rms" else h
            with new_block() as block:
                ms_ready, root, inv_ready = sig("mean_square"), sig("row_root"), sig("inverse_ready")
                ready, tp, rows_in = [sig("normed_dve"), sig("normed_act")], sig("transposed"), sig("rows_loaded")
                ms, std, rstd, shift, warm = stat[:, 2:4], stat[:, 4:6], stat[:, 6:8], stat[:, 36:38], stat[:, 38:39]
                mean, var = mv[:, :, 0], mv[:, :, 1]

                @block.scalar
                def _(act):
                    act.activation(warm, ident[:, 0:1], ACT.Sqrt)
                    act.wait_ge(ms_ready.sem, ms_ready.at(1))
                    act.activation(std, ms, ACT.Sqrt).then_inc(root.up(), 1)
                    act.wait_ge(inv_ready.sem, inv_ready.at(1))
                    if kind == "ln":
                        act.activation(h[:, 1, :], h[:, 1, :], ACT.Identity, bias=shift[:, 1:2], scale=rstd[:, 1:2]).then_inc(ready[1].up(), 1)
                    else:
                        act.activation(src[:, 1, :], h[:, 1, :], ACT.Copy, scale=rstd[:, 1:2]).then_inc(ready[1].up(), 1)
                    if store is None:
                        for t in range(T):
                            act.wait_ge(tp.sem, tp.at(2 * t + 1))
                            for k in range(4):
                                i, o = bank(2 * t)[:, k * P:(k + 1) * P], xT[:, k, t * P:(t + 1) * P]
                                if bias is None:
                                    act.activation(o, i, ACT.Copy, scale=gain[:, k:k + 1])
                                else:
                                    act.activation(o, i, ACT.Identity, bias=bias[:, k:k + 1], scale=gain[:, k:k + 1])

                @block.vector
                def _(dve):
                    if first:
                        for t in range(T):
                            for c in range(2):
                                ins = row_stats(dve, t, c)
                        link(dve, "dve_step", ins)
                    for t in range(T):
                        ins = dve.bn_aggr(mv[:, t, :], bn[:, t, :, :])
                    link(dve, "dve_step", ins)
                    if kind == "ln":
                        dve.tensor_scalar(ms, var, LN_EPS, None, ALU.add).then_inc(ms_ready.up(), 1)
                    else:
                        link(dve, "dve_step", dve.tensor_tensor(ms, mean, mean, ALU.mult))
                        dve.scalar_tensor_tensor(ms, ms, RMS_EPS, var, ALU.add, ALU.add).then_inc(ms_ready.up(), 1)
                    dve.wait_ge(root.sem, root.at(1))
                    link(dve, "dve_step", dve.reciprocal(rstd, std))
                    dve.scalar_tensor_tensor(shift, mean, -1.0, rstd, ALU.mult, ALU.mult).then_inc(inv_ready.up(), 1)
                    if kind == "ln":
                        dve.tensor_scalar(h[:, 0, :], h[:, 0, :], mean[:, 0:1], rstd[:, 0:1], ALU.subtract, ALU.mult).then_inc(ready[0].up(), 1)
                    else:
                        dve.tensor_scalar(src[:, 0, :], h[:, 0, :], rstd[:, 0:1], None, ALU.mult).then_inc(ready[0].up(), 1)
                    if store is not None:
                        dve.wait_ge(rows_in.sem, rows_in.base)
                        for t in range(T):
                            dve.wait_ge(ready[t].sem, ready[t].at(1))
                            link(dve, "dve_step", dve.tensor_tensor(h[:, t, :], h[:, t, :], rows[:, 0, :], ALU.mult))
                            dve.tensor_tensor(h[:, t, :], h[:, t, :], rows[:, 1, :], ALU.add).then_inc(sig("rows_done").up(), 1)
                        return
                    for t in range(T):
                        dve.wait_ge(tp.sem, tp.at(2 * t + 2))
                        o, i = xT[:, 4:8, t * P:(t + 1) * P], bank(2 * t + 1).rearrange("p (k s) -> p k s", k=4)
                        g, b = (None if x is None else x[:, 4:8].rearrange("p (k o) -> p k o", o=1).broadcast_to([P, 4, P]) for x in (gain, bias))
                        ins = dve.tensor_tensor(o, i, g, ALU.mult)
                        if bias is not None:
                            link(dve, "dve_step", ins)
                            dve.tensor_tensor(o, o, b, ALU.add)

                if store is not None:
                    @block.sync
                    def _(sp):
                        done, stored = sig("rows_done"), sig("stored")
                        for t in range(T):
                            sp.wait_ge(done.sem, done.at(t + 1))
                            sp.dma_start(store[t * P:(t + 1) * P, :], h[:, t, :]).then_inc(stored.up(16), 16)
                        sp.wait_ge(stored.sem, stored.at(16 * T))
                    return

                @block.tensor
                def _(pe):
                    for t in range(T):
                        pe.wait_ge(ready[t].sem, ready[t].at(1))
                        for f in range(2):
                            for k in range(4):
                                c = (4 * f + k) * P
                                last = pe.transpose(bank(2 * t + f)[:, k * P:(k + 1) * P], src[:, t, c:c + P], ident[:])
                            last.then_inc(tp.up(), 1)
            if kind != "rms":
                unscaled.append(bias is not None)

        def transpose_all(pairs, scale=None):
            with new_block() as block:
                tp, free = sig("transposed"), [sig("act_evacuated"), sig("dve_evacuated")]
                jobs = [(s, o, t, f) for s, o in pairs for t in range(T) for f in range(2)]

                @block.tensor
                def _(pe):
                    for n, (s, o, t, f) in enumerate(jobs):
                        if n >= 8:
                            pe.wait_ge(free[n % 2].sem, free[n % 2].at(n // 2 - 3))
                        for k in range(4):
                            c = (4 * f + k) * P
                            last = pe.transpose(bank(n % 8)[:, k * P:(k + 1) * P], s[:, t, c:c + P], ident[:])
                        last.then_inc(tp.up(), 1)

                def evacuate(e):
                    def body(eng):
                        for n, (s, o, t, f) in enumerate(jobs):
                            if n % 2 != e:
                                continue
                            eng.wait_ge(tp.sem, tp.at(n + 1))
                            i = bank(n % 8).rearrange("p (k s) -> p k s", k=4)
                            q = o[:, 4 * f:4 * f + 4, t * P:(t + 1) * P]
                            if e == 0:
                                ins = eng.copy(q, i) if scale is None else eng.activation(q, i, ACT.Copy, scale=scale)
                            else:
                                ins = eng.tensor_copy(q, i) if scale is None else eng.tensor_scalar(q, i, scale, None, ALU.mult)
                            ins.then_inc(free[e].up(), 1)
                    return body

                block.scalar(evacuate(0))
                block.vector(evacuate(1))

        def rope(dve, x, heads, dh, at, rot, cos, sin, tmp):
            half = rot // 2
            v = x.rearrange("p (a f) -> p a f", a=heads)[:, :, at:at + rot]
            a = tmp[:, 0:heads * rot].rearrange("p (a f) -> p a f", a=heads)
            b = tmp[:, heads * rot:2 * heads * rot].rearrange("p (a f) -> p a f", a=heads)

            def wide(c):
                return c.rearrange("p (o f) -> p o f", o=1).broadcast_to([P, heads, c.shape[-1]])

            dve.tensor_tensor(a, v, wide(cos), ALU.mult)
            dve.tensor_tensor(b[:, :, 0:half], v[:, :, half:rot], wide(sin[:, 0:half]), ALU.mult)
            link(dve, "dve_step", dve.tensor_tensor(b[:, :, half:rot], v[:, :, 0:half], wide(sin[:, half:rot]), ALU.mult))
            return dve.tensor_tensor(v, a, b, ALU.add)

        PART = 1024
        CHUNKS_HELD = 3

        def split_act(act, high, x, ready):
            act.copy(high, x).then_inc(ready.up(), 1)

        def split_dve(dve, low, x, high):
            return dve.tensor_tensor(low, x, high.bitcast(F32), ALU.subtract)

        def three(pe, out, a, b, start, stop):
            for n, (x, y) in enumerate(((0, 0), (0, 1), (1, 0))):
                last = pe.matmul(out, a[x], b[y], start=start and n == 0, stop=stop and n == 2, skip_group_check=True)
            return last

        @contextmanager
        def split_operands(bufs, width):
            close_part()
            with ExitStack() as space:
                opened[0] += 1
                yield [[space.enter_context(nc.sbuf_tensor(f"{name}_{x}{opened[0]}", shape, F32R))[:] for x in "hl"]
                       for name, shape in (("x", [P, KD, SEQ]), ("w", [P, bufs, width]))]
            open_part()

        BUFS = 4
        EVAC_AT = BUFS - 1

        def split_projection(block, j0, units, src, xs, ws, act_evac, dve_evac, act_first=None, act_between=None, dve_between=None):
            x_high, x_split, high, split, used = (sig(x) for x in ("x_high", "x_split", "weights_high", "weights_split", "chunk_used"))
            n = KD * units

            def source(q):
                return ring[:, (j0 + q // KD) % SLOTS, (q % KD) * COLS:(q % KD + 1) * COLS]

            def evacuate(evac, q):
                u = (q - EVAC_AT) // KD - 1
                if (q - EVAC_AT) % KD == 0 and u >= 0:
                    evac(u)

            @block.scalar
            def _(act):
                if act_first is not None:
                    act_first(act)
                for q in range(n):
                    if q < KD and q % 2 == 0:
                        split_act(act, xs[0][:, q:q + 2, :], src[:, q:q + 2, :], x_high)
                    if q % KD == 0:
                        j = j0 + q // KD
                        act.wait_ge(loaded[j % SLOTS].sem, 16 * (j // SLOTS + 1))
                    if q >= BUFS:
                        act.wait_ge(used.sem, used.at(q - BUFS + 1))
                    split_act(act, ws[0][:, q % BUFS, :], source(q), high)
                    if q == KD - 1 and act_between is not None:
                        act_between(act)
                    evacuate(lambda u: act_evac(act, u), q)
                act_evac(act, units - 1)

            @block.vector
            def _(dve):
                for q in range(n):
                    if q < KD and q % 2 == 0:
                        dve.wait_ge(x_high.sem, x_high.at(q // 2 + 1))
                        split_dve(dve, xs[1][:, q:q + 2, :], src[:, q:q + 2, :], xs[0][:, q:q + 2, :]).then_inc(x_split.up(), 1)
                    dve.wait_ge(high.sem, high.at(q + 1))
                    split_dve(dve, ws[1][:, q % BUFS, :], source(q), ws[0][:, q % BUFS, :]).then_inc(split.up(), 1)
                    if q % KD == KD - 1:
                        unit_done(j0 + q // KD, split)
                    if q == KD - 1 and dve_between is not None:
                        dve_between(dve)
                    evacuate(lambda u: dve_evac(dve, u), q)
                dve_evac(dve, units - 1)

        def chunk_ready(pe, q):
            x_split, split = sig("x_split"), sig("weights_split")
            if q < KD and q % 2 == 0:
                pe.wait_ge(x_split.sem, x_split.at(q // 2 + 1))
            pe.wait_ge(split.sem, split.at(q + 1))

        def project(units, dest=None, src=None, rotary=None, residual=None, row_src=(), loads_due=None):
            src = xT if src is None else src
            j0 = next_unit(units)
            with split_operands(BUFS, COLS) as (xs, ws), new_block() as block:
                used, evac, free = sig("chunk_used"), sig("act_evacuated"), sig("dve_evacuated")
                rows_in = sig("rows_loaded")

                @block.tensor
                def _(pe):
                    for q in range(KD * units):
                        u, k = q // KD, q % KD
                        chunk_ready(pe, q)
                        if u >= 2 and k == 0:
                            if residual is None:
                                pe.wait_ge(evac.sem, evac.at(T * (u - 1)))
                            else:
                                pe.wait_ge(free.sem, free.at(T * (u - 1)))
                        for t in range(T):
                            last = three(pe, bank(T * (u % 2) + t), [x[:, k, t * P:(t + 1) * P] for x in xs], [w[:, q % BUFS, :] for w in ws], k == 0, k == KD - 1)
                        last.then_inc(used.up(), 1)

                def load_rows(act):
                    for i, r in enumerate(row_src):
                        act.dma_start(rows[:, i, :], r.rearrange("(o f) -> o f", o=1).broadcast_to([P, D])).then_inc(rows_in.up(16), 16)

                def act_evac(act, u):
                    if residual is None:
                        act.wait_ge(used.sem, used.at(KD * (u + 1)))
                        for t in range(T):
                            act.copy(dest(u, t), bank(T * (u % 2) + t)).then_inc(evac.up(), 1)

                def dve_evac(dve, u):
                    if residual is not None:
                        dve.wait_ge(used.sem, used.at(KD * (u + 1)))
                        for t in range(T):
                            add_residual(dve, t, u, residual, bank(T * (u % 2) + t)).then_inc(free.up(), 1)
                    elif rotary is not None and rotary(u) is not None:
                        heads, dh, at, rot, cos, sin, tmp = rotary(u)
                        for t in range(T):
                            dve.wait_ge(evac.sem, evac.at(T * u + t + 1))
                            link(dve, "dve_step", rope(dve, dest(u, t), heads, dh, at, rot, cos[:, t, :], sin[:, t, :], tmp))

                split_projection(block, j0, units, src, xs, ws, act_evac, dve_evac, act_first=load_rows)
                stream(block, units if loads_due is None else loads_due)

        def project_fm(pe, w, src, n, out_bank, free):
            for m in range(4):
                if m % 2 == 0 and n + m // 2 >= 4:
                    pe.wait_ge(free.sem, free.at(n + m // 2 - 3))
                for k in range(KD):
                    last = pe.matmul(bank((n + m // 2) % 4)[:, (m % 2) * SEQ:(m % 2 + 1) * SEQ], w[:, k, m * P:(m + 1) * P],
                                     src[:, k, :], start=(k == 0), stop=(k == KD - 1))
                if m % 2:
                    last.then_inc(out_bank.up(), 1)
            return last

        def project_features(src, dst, units=2, act_aside=None, dve_aside=None):
            j0 = next_unit(units)
            with split_operands(BUFS, COLS) as (xs, ws), new_block() as block:
                used, evac = sig("chunk_used"), sig("act_evacuated")

                @block.tensor
                def _(pe):
                    for q in range(KD * units):
                        u, k = q // KD, q % KD
                        chunk_ready(pe, q)
                        if u >= 2 and k == 0:
                            pe.wait_ge(evac.sem, evac.at(2 * (u - 1)))
                        for m in range(4):
                            last = three(pe, bank(2 * (u % 2) + m // 2)[:, (m % 2) * SEQ:(m % 2 + 1) * SEQ], [w[:, q % BUFS, m * P:(m + 1) * P] for w in ws],
                                         [x[:, k, :] for x in xs], k == 0 and m % 2 == 0, k == KD - 1)
                        last.then_inc(used.up(), 1)

                def act_evac(act, u):
                    act.wait_ge(used.sem, used.at(KD * (u + 1)))
                    for n in range(2):
                        o = dst[:, 4 * u + 2 * n:4 * u + 2 * n + 2, :]
                        act.copy(o, bank(2 * (u % 2) + n).rearrange("p (m s) -> p m s", m=2)).then_inc(evac.up(), 1)

                def on_the_side(dve):
                    if dve_aside is not None:
                        dve_aside(dve)
                    scale_rows(dve)

                split_projection(block, j0, units, src, xs, ws, act_evac, lambda dve, u: None, act_between=act_aside, dve_between=on_the_side)
                stream(block, units)

        def attention(maps, q, k, v, dv, o, scale, masked, work, diff=False):
            TURN, MIX = 2, 3
            s_sb = work[0].rearrange("p (b s) -> p b s", b=4)
            pT = work[1][:, 0:1024].rearrange("p (b c s) -> p b c s", b=2, c=4)
            nmax, sums, rs = (stat[:, a:a + 8].rearrange("p (b t) -> p b t", b=4) for a in (0, 8, 16))
            width = (P if masked else SEQ, SEQ)
            at = (0, width[0])
            total = sum(width)
            tiles = [(t, kt) for t in range(T) for kt in range(width[t] // P)]
            s_bank, p_bank, o_bank = (0, 1, 6), (2, 3), (4, 5)
            with new_block() as block:
                s_mm, p_mm, o_mm = sig("scores_ready"), sig("transposed"), sig("product_ready")
                s_out, m_ready, p_ready = sig("scores_copied"), sig("max_ready"), sig("probs_ready")
                pT_ready, o_out = sig("act_evacuated"), sig("dve_evacuated")

                @block.tensor
                def _(pe):
                    for i in range(maps + MIX):
                        if i < maps:
                            if i >= 3:
                                pe.wait_ge(s_out.sem, s_out.at(T * (i - 2)))
                            for t in range(T):
                                parts = list(zip(q(i, t), k(i)))
                                for n, (a, b) in enumerate(parts):
                                    last = pe.matmul(bank(s_bank[i % 3])[:, at[t]:at[t] + width[t]], a, b[:, 0:width[t]], start=(n == 0), stop=(n == len(parts) - 1))
                            last.then_inc(s_mm.up(), 1)
                        if TURN <= i < maps + TURN:
                            m = i - TURN
                            pe.wait_ge(p_ready.sem, p_ready.at(T * (m + 1)))
                            if m >= 2:
                                pe.wait_ge(pT_ready.sem, pT_ready.at(m - 1))
                            for c in range(len(tiles)):
                                last = pe.transpose(bank(p_bank[m % 2])[:, c * P:(c + 1) * P], s_sb[:, m % 4, c * P:(c + 1) * P], ident[:])
                            last.then_inc(p_mm.up(), 1)
                        if i >= MIX:
                            m = i - MIX
                            pe.wait_ge(pT_ready.sem, pT_ready.at(m + 1))
                            if m >= 2:
                                pe.wait_ge(o_out.sem, o_out.at(m - 1))
                            for c, (t, kt) in enumerate(tiles):
                                last = pe.matmul(bank(o_bank[m % 2])[:, t * dv:(t + 1) * dv], pT[:, m % 2, c, :], v(m, kt), start=(kt == 0), stop=(kt == width[t] // P - 1))
                            last.then_inc(o_mm.up(), 1)

                @block.vector
                def _(dve):
                    if masked:
                        dve.wait_ge(mask_in.sem, mask_in.count)
                    for i in range(maps + MIX):
                        if i < maps:
                            b = i % 4
                            dve.wait_ge(s_mm.sem, s_mm.at(i + 1))
                            if i >= 4:
                                dve.wait_ge(p_mm.sem, p_mm.at(i - 3))
                            for t in range(T):
                                c = slice(at[t], at[t] + width[t])
                                if masked:
                                    ins = dve.scalar_tensor_tensor(s_sb[:, b, c], bank(s_bank[i % 3])[:, c], scale, mask[:, t, 0:width[t]], ALU.mult, ALU.add)
                                else:
                                    ins = dve.tensor_scalar(s_sb[:, b, c], bank(s_bank[i % 3])[:, c], scale, None, ALU.mult)
                                ins.then_inc(s_out.up(), 1)
                            for t in range(T):
                                dve.wait_ge(s_out.sem, s_out.at(T * i + t + 1))
                                dve.tensor_reduce(nmax[:, b, t:t + 1], s_sb[:, b, at[t]:at[t] + width[t]], AX, ALU.max, negate=True).then_inc(m_ready.up(), 1)
                        if i >= MIX:
                            m = i - MIX
                            b = m % 4
                            dve.wait_ge(p_ready.sem, p_ready.at(T * (m + 1)))
                            link(dve, "dve_step", dve.reciprocal(rs[:, b, :], sums[:, b, :]))
                            if diff and m % 2:
                                link(dve, "dve_step", dve.tensor_scalar(rs[:, b, :], rs[:, b, :], nlam[:], None, ALU.mult))
                            dve.wait_ge(o_mm.sem, o_mm.at(m + 1))
                            if diff and m % 2:
                                dve.wait_ge(o_out.sem, o_out.at(m))
                            for t in range(T):
                                x, r = bank(o_bank[m % 2])[:, t * dv:(t + 1) * dv], rs[:, b, t:t + 1]
                                if diff and m % 2:
                                    ins = dve.scalar_tensor_tensor(o(m, t), x, r, o(m, t), ALU.mult, ALU.add)
                                else:
                                    ins = dve.tensor_scalar(o(m, t), x, r, None, ALU.mult)
                            ins.then_inc(o_out.up(), 1)

                @block.scalar
                def _(act):
                    for i in range(maps + TURN):
                        if i >= TURN:
                            m = i - TURN
                            act.wait_ge(p_mm.sem, p_mm.at(m + 1))
                            if m >= 2:
                                act.wait_ge(o_mm.sem, o_mm.at(m - 1))
                            n = len(tiles)
                            act.copy(pT[:, m % 2, 0:n, :], bank(p_bank[m % 2])[:, 0:total].rearrange("p (c s) -> p c s", c=n)).then_inc(pT_ready.up(), 1)
                        if i < maps:
                            b = i % 4
                            if i >= 4:
                                act.wait_ge(o_out.sem, o_out.at(i - 3))
                            for t in range(T):
                                act.wait_ge(m_ready.sem, m_ready.at(T * i + t + 1))
                                x = s_sb[:, b, at[t]:at[t] + width[t]]
                                act.activation(x, x, ACT.Exp, bias=nmax[:, b, t:t + 1], accum_out=sums[:, b, t:t + 1]).then_inc(p_ready.up(), 1)

        mask_in = sig("mask_loaded")
        pos["issued"] = SLOTS
        with new_block() as block:
            const_in = sig("inputs_loaded")

            @block.sync
            def _(sp):
                for o, i in [(h[:], d["x"].rearrange("(t p) f -> p t f", p=P)), (ident[:], d["ident"]), (cols[:], d["cols"]), (cos0[:], d["cos0"]), (sin0[:], d["sin0"])]:
                    sp.dma_start(o, i).then_inc(const_in.up(16), 16)
                for j in range(SLOTS):
                    load(sp, j)
                    if j == 0:
                        sp.dma_start(mask[:], d["causal"]).then_inc(mask_in.up(16), 16)
                sp.wait_ge(const_in.sem, const_in.at(5 * 16))

        tables = blk(2)
        inv = tables[:, 0:24]
        lam = tables[:, 64:64 + 4 * HD].rearrange("p (a f) -> p a f", a=4)
        posf, ang, turn = stat[:, 0:2], tables[:, 512:560], tables[:, 576:624]
        red = tables[:, 640:736].rearrange("p (c n) -> p c n", c=2)
        trigs = tables[:, 768:864].rearrange("p (c n) -> p c n", c=2)
        lsum, lexp, lprod = stat[:, 4:6], stat[:, 6:8], tables[:, 1024:1024 + 2 * HD].rearrange("p (a f) -> p a f", a=2)

        def tables_act(act):
            trig, sums = sig("angles_ready"), sig("lambda_sums")
            act.wait_ge(trig.sem, trig.at(1))
            for c in range(2):
                act.activation(trigs[:, c, :], red[:, c, :], ACT.Sin).then_inc(sig("trig_ready").up(), 1)
            act.wait_ge(sums.sem, sums.at(1))
            act.activation(lexp, lsum, ACT.Exp).then_inc(sig("lambda_exp").up(), 1)

        def tables_dve(dve):
            def step(ins):
                link(dve, "dve_step", ins)
            step(dve.tensor_copy(posf, posn[:]))
            two_pi = 2 * math.pi
            c1 = 6.28125
            c2 = math.floor((two_pi - c1) * 2 ** 19) / 2 ** 19
            c3 = two_pi - c1 - c2
            big = 1.5 * 2 ** 23
            for t in range(T):
                step(dve.tensor_scalar(ang[:, t * 24:(t + 1) * 24], inv, posf[:, t:t + 1], None, ALU.mult))
            for c in range(2):
                step(dve.tensor_scalar(turn, ang, 1 / two_pi, 0.25 * c, ALU.mult, ALU.add))
                step(dve.tensor_scalar(turn, turn, big, None, ALU.add))
                step(dve.tensor_scalar(turn, turn, big, None, ALU.subtract))
                step(dve.scalar_tensor_tensor(red[:, c, :], turn, -c1, ang, ALU.mult, ALU.add))
                step(dve.scalar_tensor_tensor(red[:, c, :], turn, -c2, red[:, c, :], ALU.mult, ALU.add))
                step(dve.scalar_tensor_tensor(red[:, c, :], turn, -c3, red[:, c, :], ALU.mult, ALU.add))
                if c:
                    step(dve.tensor_scalar(red[:, c, :], red[:, c, :], math.pi / 2, None, ALU.add))
                step(dve.tensor_scalar(red[:, c, :], red[:, c, :], 3.1415925, -3.1415925, ALU.min, ALU.max))
            dve.tensor_scalar(red[:, 0, 0:1], red[:, 0, 0:1], 1.0, None, ALU.mult).then_inc(sig("angles_ready").up(), 1)
            dve.wait_ge(sig("trig_ready").sem, sig("trig_ready").at(2))
            for t in range(T):
                for n, (c, s, half) in enumerate([(cosd, sind, DIFF_ROPE // 2), (cosr, sinr, MLA_ROPE // 2)]):
                    a = t * 24 + 8 * n
                    sn, cs = trigs[:, 0, a:a + half], trigs[:, 1, a:a + half]
                    dve.tensor_copy(c[:, t, 0:half], cs)
                    dve.tensor_copy(c[:, t, half:2 * half], cs)
                    dve.tensor_scalar(s[:, t, 0:half], sn, -1.0, None, ALU.mult)
                    dve.tensor_copy(s[:, t, half:2 * half], sn)
            step(dve.tensor_tensor(lprod, lam[:, 0:4:2, :], lam[:, 1:4:2, :], ALU.mult))
            step(dve.tensor_reduce(lsum, lprod, AX, ALU.add))
            dve.tensor_scalar(lsum, lsum, 1.0, None, ALU.mult).then_inc(sig("lambda_sums").up(), 1)
            dve.wait_ge(sig("lambda_exp").sem, sig("lambda_exp").at(1))
            step(dve.tensor_tensor(nlam[:], lexp[:, 1:2], lexp[:, 0:1], ALU.subtract))
            step(dve.tensor_scalar(nlam[:], nlam[:], LAMBDA_INIT, None, ALU.subtract))

        def ffn_stage(n_units, layer, row_src=(), ahead=()):
            j0 = next_unit(n_units)
            close_part()
            close_part()
            bufs = 4
            with ExitStack() as space:
                def parts_of(name, shape):
                    return [space.enter_context(nc.sbuf_tensor(f"{name}_{x}{layer}", shape, F32R))[:] for x in "hl"]
                xs, ws, hids = parts_of("ffn_x", [P, KD, SEQ]), parts_of("ffn_w", [P, bufs, PART]), parts_of("ffn_hid", [P, 2, 2, SEQ])
                act_out = blk(0)[:, 0:1024].rearrange("p (b f s) -> p b f s", b=2, f=2)
                conv = blk(0)[:, 1024:2048].rearrange("p (b f s) -> p b f s", b=2, f=2)
                order = []
                for u in range(n_units + 1):
                    order += [(u, c) for c in range(4) if u < n_units] + [(u - 1, c) for c in (4, 5) if u]
                number = {x: q for q, x in enumerate(order)}

                def source(u, c):
                    w = ring[:, (j0 + u) % SLOTS, :]
                    if c >= 4:
                        return w[:, 2 * KD * 2 * P + (c - 4) * D:2 * KD * 2 * P + (c - 3) * D]
                    return w[:, (c // 2) * KD * 2 * P:(c // 2 + 1) * KD * 2 * P].rearrange("p (k n) -> p k n", k=KD)[:, :, (c % 2) * P:(c % 2 + 1) * P]

                def chunk(part, u, c):
                    w = ws[part][:, number[u, c] % bufs, :]
                    return w if c >= 4 else w.rearrange("p (k n) -> p k n", k=KD)

                with new_block() as block:
                    x_high, x_ready, high, split, used = (sig(x) for x in ("x_high", "x_split", "weights_high", "weights_split", "chunk_used"))
                    biased, conv_ready, act_ready, hid_made, hid_high, hid_ready = (sig(x) for x in ("gate_biased", "conv_ready", "gate_active", "hidden_made", "hidden_high", "hidden_ready"))
                    rows_in, ahead_in = sig("rows_loaded"), sig("ahead_loaded")

                    def wait_used(eng, u, c):
                        eng.wait_ge(used.sem, used.at(number[u, c] + 1))

                    @block.tensor
                    def _(pe):
                        pe.wait_ge(x_ready.sem, x_ready.at(1))
                        for u, c in order:
                            pe.wait_ge(split.sem, split.at(number[u, c] + 1))
                            w = [chunk(part, u, c) for part in range(2)]
                            if c < 4:
                                if c == 0 and u >= 2:
                                    pe.wait_ge(hid_ready.sem, hid_ready.at(u - 1))
                                for k in range(KD):
                                    mm = three(pe, bank(2 * (u % 2) + c // 2)[:, (c % 2) * SEQ:(c % 2 + 1) * SEQ], [x[:, k, :] for x in w], [x[:, k, :] for x in xs],
                                               k == 0, k == KD - 1)
                            else:
                                pe.wait_ge(hid_ready.sem, hid_ready.at(u + 1))
                                for t in range(T):
                                    for n in range(2):
                                        mm = three(pe, bank(4 + 2 * t + n), [x[:, u % 2, c - 4, t * P:(t + 1) * P] for x in hids], [x[:, n * 512:(n + 1) * 512] for x in w],
                                                   u == 0 and c == 4, u == n_units - 1 and c == 5)
                            mm.then_inc(used.up(), 1)

                    @block.scalar
                    def _(act):
                        for n, r in enumerate(row_src):
                            act.dma_start(rows[:, n, :], r.rearrange("(o f) -> o f", o=1).broadcast_to([P, D])).then_inc(rows_in.up(16), 16)
                        for o, x in ahead:
                            act.dma_start(o, x).then_inc(ahead_in.up(16), 16)
                        split_act(act, xs[0], xT[:], x_high)

                        def split_chunk(u, c):
                            q = number[u, c]
                            if c == 0:
                                act.wait_ge(loaded[(j0 + u) % SLOTS].sem, 16 * ((j0 + u) // SLOTS + 1))
                            if q >= bufs:
                                act.wait_ge(used.sem, used.at(q - bufs + 1))
                            split_act(act, chunk(0, u, c), source(u, c), high)

                        for u in range(n_units + 1):
                            b = u % 2
                            if u < n_units:
                                for c in range(4):
                                    split_chunk(u, c)
                                wait_used(act, u, 1)
                                if u >= 2:
                                    act.wait_ge(hid_ready.sem, hid_ready.at(u - 1))
                                g = bank(2 * b).rearrange("p (f s) -> p f s", f=2)
                                for f in range(2):
                                    ft = 2 * u + f
                                    act.activation(conv[:, b, f, :], g[:, f, :], ACT.Identity, bias=col("conv_b", layer * FT + ft),
                                                   scale=col("conv_w", (layer * 3 + 2) * FT + ft)).then_inc(biased.up(), 1)
                            if u:
                                for c in (4, 5):
                                    split_chunk(u - 1, c)
                            if u < n_units:
                                act.wait_ge(conv_ready.sem, conv_ready.at(u + 1))
                                act.activation(act_out[:, b], conv[:, b], ACT.Silu).then_inc(act_ready.up(), 1)
                                act.wait_ge(hid_made.sem, hid_made.at(u + 1))
                                if u >= 2:
                                    wait_used(act, u - 2, 5)
                                split_act(act, hids[0][:, b], act_out[:, b], hid_high)
                        if ahead:
                            act.wait_ge(ahead_in.sem, ahead_in.count)

                    @block.vector
                    def _(dve):
                        dve.wait_ge(x_high.sem, x_high.at(1))
                        split_dve(dve, xs[1], xT[:], xs[0]).then_inc(x_ready.up(), 1)

                        def split_chunk(u, c):
                            dve.wait_ge(high.sem, high.at(number[u, c] + 1))
                            split_dve(dve, chunk(1, u, c), source(u, c), chunk(0, u, c)).then_inc(split.up(), 1)

                        for u in range(n_units + 1):
                            b = u % 2
                            if u < n_units:
                                for c in range(4):
                                    split_chunk(u, c)
                                gt = bank(2 * b).rearrange("p (f s) -> p f s", f=2)
                                up = bank(2 * b + 1).rearrange("p (f s) -> p f s", f=2)
                                dve.wait_ge(biased.sem, biased.at(2 * u + 2))
                                for lag, w in ((1, 1), (2, 0)):
                                    for f in range(2):
                                        ft = 2 * u + f
                                        x = conv[:, b, f, lag:SEQ]
                                        ins = dve.scalar_tensor_tensor(x, gt[:, f, 0:SEQ - lag], col("conv_w", (layer * 3 + w) * FT + ft), x, ALU.mult, ALU.add)
                                    if lag == 1:
                                        link(dve, "dve_step", ins)
                                ins.then_inc(conv_ready.up(), 1)
                            if u:
                                for c in (4, 5):
                                    split_chunk(u - 1, c)
                                unit_done(j0 + u - 1, split)
                            if u < n_units:
                                wait_used(dve, u, 3)
                                dve.wait_ge(act_ready.sem, act_ready.at(u + 1))
                                dve.tensor_tensor(act_out[:, b], act_out[:, b], up, ALU.mult).then_inc(hid_made.up(), 1)
                                dve.wait_ge(hid_high.sem, hid_high.at(u + 1))
                                split_dve(dve, hids[1][:, b], act_out[:, b], hids[0][:, b]).then_inc(hid_ready.up(), 1)
                        dve.wait_ge(used.sem, used.at(len(order)))
                        for t in range(T):
                            for c in range(2):
                                add_residual(dve, t, c, 1.0, bank(4 + 2 * t + c))
                    stream(block, n_units)
            open_part()
            open_part()

        def experts(layer, comb, xg, swT, row_src):
            j0 = next_unit(EU)
            steps = EU // EPG
            close_part()
            with ExitStack() as space:
                def parts_of(name, shape):
                    return [space.enter_context(nc.sbuf_tensor(f"expert_{name}_{x}{layer}", shape, F32R))[:] for x in "hl"]
                xs = space.enter_context(nc.sbuf_tensor(f"expert_x{layer}", [P, KD, 2, SLOTS_E], F32R))[:]
                ws, hids = parts_of("w", [P, CHUNKS_HELD, PART]), parts_of("hid", [P, 2, 2, P])
                block = space.enter_context(new_block())
                dn, summed, scaled, rows_in = sig("down_done"), sig("experts_summed"), sig("rows_scaled"), sig("rows_loaded")
                cleared = sig(f"zeros_made{layer}")
                turned, x_made, weights_out, weights_in, gu, act_ready, weighted, dense_hid = (sig(f"{x}{layer}") for x in (
                    "rows_turned", "input_made", "weight_rows_ready", "weight_rows_copied", "dense_gate_up", "dense_gate_active", "gate_weighted", "dense_hidden"))
                rowsE = span(4, 6).rearrange("p (e s) -> p e s", e=N_EXPERTS)
                hid = blk(3)[:, 0:1024].rearrange("p (b f s) -> p b f s", b=2, f=2)
                act_out = blk(3)[:, 1024:2048].rearrange("p (b f s) -> p b f s", b=2, f=2)
                chunk_high, chunk_split, chunk_used, x_high, x_split, gu_out, gu_turned = (sig(f"{x}{layer}") for x in (
                    "chunk_high", "chunk_split", "chunk_used", "expert_rows_high", "expert_rows_split", "gate_up_copied", "gate_up_turned"))
                silu_done, hid_made, hid_high, hid_ready, *copied = (sig(f"{x}{layer}") for x in (
                    "silu_done", "expert_hidden_made", "expert_hidden_high", "expert_hidden_split", "outputs_copied_act", "outputs_copied_dve"))
                y_now = rows[:, 0, :]
                sw_now = rows[:, 1, 0:SEQ]
                gu_halves = rows[:, 1, 256:768]
                act_sp = rows[:, 1, 768:896].rearrange("p (f s) -> p f s", f=2)
                fold = rows[:, 1, 896:960]

                QUARTERS = [(t, c) for t in range(T) for c in range(2)]

                def source(u, pos):
                    w = ring[:, (j0 + u) % SLOTS, :]
                    if pos >= 4:
                        return w[:, 2 * KD * 2 * P + (pos - 4) * D:2 * KD * 2 * P + (pos - 3) * D]
                    return w[:, 0:2 * KD * 2 * P].rearrange("p (g k n) -> p g k n", g=2, k=KD)[:, :, 2 * pos:2 * pos + 2, :]

                def before(i, u, pos):
                    return pos if start(i) and u == 0 else at(i, u) * 6 + (pos - 2)

                def chunk(part, i, u, pos):
                    return ws[part][:, (pos + (2 if start(i) and u == 0 else 0)) % CHUNKS_HELD, :]

                def own(u):
                    return slice(SLOTS_E * (u // 2), SLOTS_E * (u // 2 + 1))

                def turned_chunk(part, i, u, pos):
                    return chunk(part, i, u, pos).rearrange("p (k g n) -> p g k n", k=2, g=2)

                def runs(eng, body):
                    for u in range(EPG):
                        body(0, u, 1)
                    with eng.Fori(1, steps - 1) as i:
                        for u in range(EPG):
                            body(i, u, steps - 2)
                    for u in range(EPG):
                        body(steps - 1, u, 1)

                def start(i, n=0, u=0):
                    return isinstance(i, int) and i == 0 and (n == 0 or u < n)

                def at(i, u):
                    return i * EPG + u

                def previous(i, u):
                    return (i, u - 1) if u else (i - 1, EPG - 1)

                def either(eng, dense, sparse):
                    counts = {s: s.count for s in signals.values()}
                    full = eng.value_load(overflow[0:1, 0:1], min_val=0, max_val=1)
                    with eng.If(full == 1):
                        dense()
                    for s, n in counts.items():
                        s.count = n
                    with eng.Else():
                        sparse()

                @block.tensor
                def _(pe):
                    def dense():
                        pe.wait_ge(scaled.sem, scaled.at(1))
                        for t in range(T):
                            for f in range(2):
                                for k in range(4):
                                    mm = pe.transpose(bank(2 * t + f)[:, k * P:(k + 1) * P], h[:, t, (4 * f + k) * P:(4 * f + k + 1) * P], ident[:])
                        mm.then_inc(turned.up(), 1)
                        pe.wait_ge(x_made.sem, x_made.at(1))
                        for e in range(N_EXPERTS):
                            if e >= 8 and e % 2 == 0:
                                pe.wait_ge(weights_in.sem, weights_in.at(e // 2 - 3))
                            for t in range(T):
                                c = comb[:, t, e // 4, e % 4:e % 4 + 1].broadcast_to([P, P])
                                mm = pe.matmul(bank((e // 2) % 4)[:, ((e % 2) * T + t) * P:((e % 2) * T + t + 1) * P], c, ident[:], start=True, stop=True)
                            if e % 2:
                                mm.then_inc(weights_out.up(), 1)
                        pe.wait_ge(weights_in.sem, weights_in.at(PAIRS))

                        def down(i, u, r):
                            pe.wait_ge(dense_hid.sem, dense_hid.at(at(i, u) + 1))
                            w = ring[:, (j0 + u) % SLOTS, 2 * KD * 2 * P:UNIT].rearrange("p (f n) -> p f n", f=2)
                            for t in range(T):
                                for c in range(2):
                                    for f in range(2):
                                        mm = pe.matmul(bank(4 + 2 * t + c), hid[:, u % 2, f, t * P:(t + 1) * P], w[:, f, c * 512:(c + 1) * 512],
                                                       start=(start(i) and u == 0 and f == 0), stop=False, skip_group_check=True)
                            mm.then_inc(dn.up(1, r), 1)

                        def body(i, u, r):
                            s = (j0 + u) % SLOTS
                            pe.wait_ge(loaded[s].sem, i * 16 * (EPG // SLOTS) + 16 * ((j0 + u) // SLOTS + 1))
                            if not start(i, 2, u):
                                pe.wait_ge(dense_hid.sem, dense_hid.at(at(i, u) - 1))
                            w = ring[:, s, 0:2 * KD * 2 * P].rearrange("p (g k n) -> p g k n", g=2, k=KD)
                            for g in range(2):
                                for f in range(2):
                                    for k in range(KD):
                                        mm = pe.matmul(bank(2 * (u % 2) + g)[:, f * SEQ:(f + 1) * SEQ], w[:, g, k, f * P:(f + 1) * P], xT[:, k, :],
                                                       start=(k == 0), stop=(k == KD - 1))
                            mm.then_inc(gu.up(1, r), 1)
                            if u > 0:
                                down(i, u - 1, r)
                            elif not start(i):
                                down(i - 1, EPG - 1, r)
                        runs(pe, body)
                        down(steps - 1, EPG - 1, 1)
                        pe.matmul(bank(0)[:, 0:P], ident[:], ident[:], start=True, stop=True).then_inc(summed.up(), 1)

                    def sparse():
                        def gate_up(i, u, r):
                            if u % 2 == 0:
                                pe.wait_ge(x_split.sem, x_split.at(i * 2 + (u // 2 + 1)))
                            for pos in range(4):
                                pe.wait_ge(chunk_split.sem, chunk_split.at(before(i, u, pos) + 1))
                                for kk in range(2):
                                    k = 2 * pos + kk
                                    high, low = (chunk(part, i, u, pos)[:, kk * 512:(kk + 1) * 512] for part in range(2))
                                    pe.matmul(bank(0), xs[:, k].rearrange("p a s -> p (a s)"), high, start=(k == 0), stop=(k == KD - 1), skip_group_check=True)
                                    mm = pe.matmul(bank(0)[0:SLOTS_E, :], xs[:, k, 0, :], low, start=False, stop=(k == KD - 1), skip_group_check=True)
                                mm.then_inc(chunk_used.up(1, r), 1)

                        def turn(i, u, r):
                            pe.wait_ge(gu_out.sem, gu_out.at(at(i, u) + 1))
                            for c in range(4):
                                mm = pe.matmul(bank(1)[:, c * SLOTS_E:(c + 1) * SLOTS_E], gu_halves[:, c * P:(c + 1) * P], fold, start=True, stop=True, skip_group_check=True)
                                if c == 0 and not (start(i) and u == 0):
                                    mm.then_inc(dn.up(1, r), 1)
                            mm.then_inc(gu_turned.up(1, r), 1)

                        def down(i, u, wheres, r, last=False):
                            pe.wait_ge(hid_ready.sem, hid_ready.at(at(i, u) + 1))
                            if u == 0 and not start(i):
                                for c in range(2):
                                    pe.wait_ge(copied[c].sem, copied[c].at(i))
                            for f, where in enumerate(wheres):
                                pe.wait_ge(chunk_split.sem, chunk_split.at(before(*where) + 1))
                                for c in range(2):
                                    mm = three(pe, bank(2 + c), [x[:, u // 2, f, :] for x in hids], [chunk(part, *where)[:, c * 512:(c + 1) * 512] for part in range(2)],
                                               u == 0 and f == 0, u == EPG - 1 and f == 1)
                                if f == 1 and last:
                                    mm.then_inc(dn.up(), 1)
                                else:
                                    mm.then_inc(chunk_used.up(1, r), 1)

                        def scatter(i, parts):
                            for c in range(2):
                                pe.wait_ge(copied[c].sem, copied[c].at(i + 1))
                            for t, c in parts:
                                mm = pe.matmul(bank(4 + 2 * t + c), sw_now[:, t * P:(t + 1) * P], y_now[:, c * 512:(c + 1) * 512],
                                               start=False, stop=False, skip_group_check=True)
                            return mm

                        def body(i, u, r):
                            gate_up(i, u, r)
                            if u > 0 and not start(i):
                                scatter(i - 1, QUARTERS[u - 1:u] if u < EPG - 1 else QUARTERS[u - 1:])
                            if not (start(i) and u == 0):
                                down(*previous(i, u), [(i, u, 4), (i, u, 5)], r)
                            turn(i, u, r)
                        pe.wait_ge(scaled.sem, scaled.at(1))
                        for b in range(4, 8):
                            pe.matmul(bank(b), ident[:], y_now[:, 0:512], start=True, stop=False, skip_group_check=True)
                        runs(pe, body)
                        down(steps - 1, EPG - 1, [(steps, 0, 0), (steps, 0, 1)], 1, last=True)
                        scatter(steps - 1, QUARTERS).then_inc(summed.up(), 1)
                    either(pe, dense, sparse)

                @block.scalar
                def _(act):
                    def dense():
                        act.wait_ge(turned.sem, turned.at(1))
                        for t in range(T):
                            for f in range(2):
                                ins = act.copy(xT[:, 4 * f:4 * f + 4, t * P:(t + 1) * P], bank(2 * t + f).rearrange("p (k s) -> p k s", k=4))
                        ins.then_inc(x_made.up(), 1)
                        for n in range(PAIRS):
                            act.wait_ge(weights_out.sem, weights_out.at(n + 1))
                            act.copy(rowsE[:, 2 * n:2 * n + 2, :], bank(n % 4).rearrange("p (e s) -> p e s", e=2)).then_inc(weights_in.up(), 1)

                        def body(i, u, r):
                            b = u % 2
                            act.wait_ge(gu.sem, gu.at(at(i, u) + 1))
                            if not start(i, 2, u):
                                act.wait_ge(dense_hid.sem, dense_hid.at(at(i, u) - 1))
                            act.activation(act_out[:, b], bank(2 * b).rearrange("p (f s) -> p f s", f=2), ACT.Silu).then_inc(act_ready.up(1, r), 1)
                        runs(act, body)

                    def sparse():
                        def split_rows(n):
                            for ks, x in xg:
                                ins = act.copy(xs[:, ks[0]:ks[-1] + 1, 0, :], x[:, :, bass.ds(n * SLOTS_E, SLOTS_E)])
                            ins.then_inc(x_high.up(), 1)

                        def split(i, u, pos):
                            if not (start(i) and u == 0 and pos < CHUNKS_HELD):
                                act.wait_ge(chunk_used.sem, chunk_used.at(before(i, u, pos) - (CHUNKS_HELD - 1)))

                        def split_down(u, wheres):
                            for f, where in enumerate(wheres):
                                split(*where)
                                split_act(act, chunk(0, *where), source(u, 4 + f), chunk_high)

                        def silu(i, u, r):
                            act.wait_ge(gu_turned.sem, gu_turned.at(at(i, u) + 1))
                            act.activation(act_sp, bank(1)[:, 0:2 * SLOTS_E].rearrange("p (f s) -> p f s", f=2), ACT.Silu).then_inc(silu_done.up(1, r), 1)

                        def hidden(i, u, r):
                            act.wait_ge(hid_made.sem, hid_made.at(at(i, u) + 1))
                            split_act(act, hids[0][:, u // 2, :, own(u)], act_sp, hid_high)

                        def copy_out(i):
                            act.wait_ge(dn.sem, dn.at(at(i, EPG)))
                            act.copy(sw_now, swT[:, bass.ds(i * SEQ, SEQ)])
                            act.copy(y_now[:, 0:512], bank(2)).then_inc(copied[0].up(), 1)

                        def body(i, u, r):
                            n, s = at(i, u), (j0 + u) % SLOTS
                            later = not (start(i) and u == 0)
                            act.wait_ge(loaded[s].sem, i * 16 * (EPG // SLOTS) + 16 * ((j0 + u) // SLOTS + 1))
                            for pos in range(4):
                                if pos == 3:
                                    if u == 1 and not start(i):
                                        copy_out(i - 1)
                                    if later:
                                        silu(*previous(i, u), r)
                                split(i, u, pos)
                                split_act(act, turned_chunk(0, i, u, pos), source(u, pos), chunk_high)
                            if later:
                                hidden(*previous(i, u), r)
                                split_down((u - 1) % EPG, [(i, u, 4), (i, u, 5)])
                            act.wait_ge(chunk_used.sem, chunk_used.at(before(i, u, 3) + 1))
                            act.copy(gu_halves, bank(0)).then_inc(gu_out.up(1, r), 1)
                            if u % 2 and not (isinstance(i, int) and i == steps - 1 and u == EPG - 1):
                                split_rows(i * 2 + (u // 2 + 1))
                        act.wait_ge(scaled.sem, scaled.at(1))
                        split_rows(0)
                        runs(act, body)
                        silu(steps - 1, EPG - 1, 1)
                        hidden(steps - 1, EPG - 1, 1)
                        split_down(EPG - 1, [(steps, 0, 0), (steps, 0, 1)])
                        copy_out(steps - 1)
                    either(act, dense, sparse)
                    act.wait_ge(summed.sem, summed.at(1))
                    for n, r in enumerate(row_src):
                        act.dma_start(rows[:, n, :], r.rearrange("(o f) -> o f", o=1).broadcast_to([P, D])).then_inc(rows_in.up(16), 16)

                @block.vector
                def _(dve):
                    scale_rows(dve)
                    dve.memset(y_now[:, 0:512], 0.0).then_inc(cleared.up(), 1)
                    dve.wait_ge(cleared.sem, cleared.at(1))
                    for x in hids:
                        dve.tensor_copy(x.rearrange("p e f s -> p (e f s)"), y_now[:, 0:512])
                    dve.tensor_tensor(fold, ident[:, 0:SLOTS_E], ident[:, SLOTS_E:2 * SLOTS_E], ALU.add)
                    dve.tensor_copy(stat[:, 40:41], stat[:, 36:37]).then_inc(scaled.up(), 1)

                    def dense():
                        dve.wait_ge(weights_in.sem, weights_in.at(PAIRS))

                        def body(i, u, r):
                            b = u % 2
                            up = bank(2 * b + 1).rearrange("p (f s) -> p f s", f=2)
                            dve.wait_ge(act_ready.sem, act_ready.at(at(i, u) + 1))
                            if not start(i, 2, u):
                                dve.wait_ge(dn.sem, dn.at(at(i, u) - 1))
                            e = rowsE[:, bass.ds(i * 2 + u // 2, 1), :]
                            dve.tensor_tensor(act_out[:, b], act_out[:, b], e.broadcast_to([P, 2, SEQ]), ALU.mult).then_inc(weighted.up(1, r), 1)
                            dve.wait_ge(weighted.sem, weighted.at(at(i, u) + 1))
                            dve.tensor_tensor(hid[:, b], act_out[:, b], up, ALU.mult).then_inc(dense_hid.up(1, r), 1)
                        runs(dve, body)

                    def sparse():
                        def split_rows(n):
                            dve.wait_ge(x_high.sem, x_high.at(n + 1))
                            for ks, x in xg:
                                ks = slice(ks[0], ks[-1] + 1)
                                ins = split_dve(dve, xs[:, ks, 1, :], x[:, :, bass.ds(n * SLOTS_E, SLOTS_E)], xs[:, ks, 0, :])
                            ins.then_inc(x_split.up(), 1)

                        def split_down(u, wheres, r):
                            for f, where in enumerate(wheres):
                                dve.wait_ge(chunk_high.sem, chunk_high.at(before(*where) + 1))
                                split_dve(dve, chunk(1, *where), source(u, 4 + f), chunk(0, *where)).then_inc(chunk_split.up(1, r), 1)

                        def hidden(i, u, r):
                            dve.wait_ge(silu_done.sem, silu_done.at(at(i, u) + 1))
                            dve.tensor_tensor(act_sp, act_sp, bank(1)[:, 2 * SLOTS_E:4 * SLOTS_E].rearrange("p (f s) -> p f s", f=2), ALU.mult).then_inc(hid_made.up(1, r), 1)

                        def split_hidden(i, u, r):
                            dve.wait_ge(hid_high.sem, hid_high.at(at(i, u) + 1))
                            split_dve(dve, hids[1][:, u // 2, :, own(u)], act_sp, hids[0][:, u // 2, :, own(u)]).then_inc(hid_ready.up(1, r), 1)

                        def copy_out(i):
                            dve.wait_ge(dn.sem, dn.at(at(i, EPG)))
                            dve.tensor_copy(y_now[:, 512:1024], bank(3)).then_inc(copied[1].up(), 1)

                        def body(i, u, r):
                            later = not (start(i) and u == 0)
                            for pos in range(4):
                                if pos == 3:
                                    if u == 1 and not start(i):
                                        copy_out(i - 1)
                                    if later:
                                        hidden(*previous(i, u), r)
                                dve.wait_ge(chunk_high.sem, chunk_high.at(before(i, u, pos) + 1))
                                split_dve(dve, turned_chunk(1, i, u, pos), source(u, pos), turned_chunk(0, i, u, pos)).then_inc(chunk_split.up(1, r), 1)
                            if later:
                                split_hidden(*previous(i, u), r)
                                split_down((u - 1) % EPG, [(i, u, 4), (i, u, 5)], r)
                            if u % 2 and not (isinstance(i, int) and i == steps - 1 and u == EPG - 1):
                                split_rows(i * 2 + (u // 2 + 1))
                        split_rows(0)
                        runs(dve, body)
                        hidden(steps - 1, EPG - 1, 1)
                        split_hidden(steps - 1, EPG - 1, 1)
                        split_down(EPG - 1, [(steps, 0, 0), (steps, 0, 1)], 1)
                        copy_out(steps - 1)
                    either(dve, dense, sparse)
                    dve.wait_ge(summed.sem, summed.at(1))
                    for t in range(T):
                        for c in range(2):
                            add_residual(dve, t, c, ALPHA, bank(4 + 2 * t + c))

                for n in range(EU):
                    release[j0 + n] = dn.sem, dn.base + n + 1
                moe_i = moe_at.index(j0)
                first, last = pos["issued"], min(pos["issued"] + EU, len(loads))
                pos["issued"] = last

                @block.sync
                def _(sp):
                    with sp.Fori(0, steps - 1) as i:
                        for u in range(EPG):
                            sp.wait_ge(dn.sem, dn.at(i * EPG + (u + 1)))
                            src = moe[bass.ds(i * EPG + (moe_i * EU + EPG + u), 1), :, :].rearrange("a p n -> p (a n)")
                            sp.dma_start(ring[:, (first + u) % SLOTS, :], src).then_inc(loaded[(first + u) % SLOTS].up(16, steps - 1), 16)
                    for j in range(first + EU - EPG, last):
                        load(sp, j)
            open_part()

        def first_attention():
            norm("rms", col("norm_mix", 0, KD), z=tok(0), first=True)
            project(6, dest=lambda u, t: tok(u // 2)[:, t, (u % 2) * COLS:(u % 2 + 1) * COLS],
                    rotary=lambda u: (8, HD, 0, HD, cos0, sin0, blk(3)) if u < 4 else None)
            transpose_all([(tok(0), fm(3)), (tok(1), fm(4))])

            def hs(m):
                return slice(64 * (m % 2), 64 * (m % 2) + 64)
            attention(HEADS, lambda m, t: [fm(3)[hs(m), m // 2, t * P:(t + 1) * P]], lambda m: [fm(4)[hs(m), m // 2, :]],
                      lambda m, kt: tok(2)[:, kt, m * HD:(m + 1) * HD], HD, lambda m, t: tok(5)[:, t, m * HD:(m + 1) * HD],
                      HD ** -0.5, True, (blk(6), blk(7)))
            transpose_all([(tok(5), xT)])
            project(2, residual=1.0)

        def rwkv():
            BKs = span(3, 5).rearrange("p (m c w s) -> p m c w s", m=KD, c=NCH, w=2)
            UV = span(6, 8).rearrange("p (c g m v) -> p c g m v", c=NCH, g=2, m=KD)
            gT = fm(9)
            sgm, xx = fm(4), fm(0)
            mixes = [fm(1), fm(3)]
            kx, ax, rx = fm(8), fm(2), fm(5)
            pc = stat[:, 64:96].rearrange("p (m c) -> p m c", m=KD)
            norm("rms", col("norm_mix", KD, KD), z=tok(0))
            j0 = next_unit(7)
            spare = ring[:, (j0 + 6) % SLOTS, :]
            ARs = spare[:, 0:2 * BLK].rearrange("p (m c w s) -> p m c w s", m=KD, c=NCH, w=2)

            gm = cos0.rearrange("p t f -> p (t f)")
            lmask = sin0.rearrange("p t f -> p (t f)")[:, 0:CHUNK]
            masks_in = sig("masks_loaded")

            def by_chunk(x):
                return x.rearrange("p m (c s) -> p m c s", c=NCH)
            order = [0, 2, 3, 1, 4, 5]
            hw, ha, hg = rows[0:64, 0, 0:SEQ], rows[0:64, 0, 256:512], rows[:, 0, 512:768]
            with new_block() as block:
                mix_ready, mm, evac = sig("mix_ready"), sig("product_ready"), sig("act_evacuated")
                reads = [4, 8, 12, 13]

                @block.vector
                def _(dve):
                    link(dve, "dve_step", dve.tensor_tensor(xx[:, :, 1:SEQ], xT[:, :, 0:SEQ - 1], xT[:, :, 1:SEQ], ALU.subtract))
                    link(dve, "dve_step", dve.tensor_scalar(xx[:, :, 0:1], xT[:, :, 0:1], -1.0, None, ALU.mult))
                    for n, i in enumerate(order):
                        if n >= 2:
                            dve.wait_ge(mm.sem, mm.at(reads[n - 2]))
                        for k in range(KD):
                            ins = dve.scalar_tensor_tensor(mixes[n % 2][:, k, :], xx[:, k, :], col("mu", i * KD + k), xT[:, k, :], ALU.mult, ALU.add)
                        ins.then_inc(mix_ready.up(), 1)

                @block.tensor
                def _(pe):
                    n = 0
                    for i in range(2):
                        pe.wait_ge(mix_ready.sem, mix_ready.at(i + 1))
                        for u in range(2):
                            arrived(pe, j0 + 2 * i + u)
                            w = ring[:, (j0 + 2 * i + u) % SLOTS, 0:KD * COLS].rearrange("p (k n) -> p k n", k=KD)
                            project_fm(pe, w, mixes[i], n, mm, evac)
                            unit_done(j0 + 2 * i + u, mm)
                            n += 2
                    pe.wait_ge(mix_ready.sem, mix_ready.at(3))
                    for u in range(2):
                        arrived(pe, j0 + 4 + u)
                        w = ring[:, (j0 + 4 + u) % SLOTS, 0:KD * COLS].rearrange("p (k n) -> p k n", k=KD)
                        for t in range(T):
                            pe.wait_ge(evac.sem, evac.at(n - 3))
                            for k in range(KD):
                                last = pe.matmul(bank(n % 4), mixes[0][:, k, t * P:(t + 1) * P], w[:, k, :], start=(k == 0), stop=(k == KD - 1))
                            last.then_inc(mm.up(), 1)
                            n += 1
                        unit_done(j0 + 4 + u, mm)
                    arrived(pe, j0 + 6)
                    lora = ring[:, (j0 + 6) % SLOTS, :]
                    w1, a1 = (lora[:, a:a + 512].rearrange("p (k n) -> p k n", k=KD) for a in (0, 512))
                    g1 = lora[:, 1024:2048].rearrange("p (k n) -> p k n", k=KD)
                    w2, a2, g2 = lora[0:64, 2048:3072], lora[0:64, 3072:4096], lora[:, 4096:5120]
                    for i, (wi, rank, wo, hid) in enumerate([(w1, 64, w2, hw), (a1, 64, a2, ha), (g1, 128, g2, hg)]):
                        pe.wait_ge(mix_ready.sem, mix_ready.at(4 + i))
                        pe.wait_ge(evac.sem, evac.at(n - 3))
                        for k in range(KD):
                            last = pe.matmul(bank(n % 4)[0:rank, 0:SEQ], wi[:, k, :], mixes[(3 + i) % 2][:, k, :], start=(k == 0), stop=(k == KD - 1))
                        last.then_inc(mm.up(), 1)
                        n += 1
                        pe.wait_ge(evac.sem, evac.at(n))
                        for f in range(4):
                            pe.wait_ge(evac.sem, evac.at(n - 3))
                            for m in range(2):
                                c = (2 * f + m) * P
                                last = pe.matmul(bank(n % 4)[:, m * SEQ:(m + 1) * SEQ], wo[:, c:c + P], hid, start=True, stop=True)
                            last.then_inc(mm.up(), 1)
                            n += 1
                    unit_done(j0 + 6, mm)
                stream(block, 6)

                @block.scalar
                def _(act):
                    act.dma_start(gm, d["gmask"]).then_inc(masks_in.up(16), 16)
                    act.dma_start(lmask, d["lmask"]).then_inc(masks_in.up(16), 16)
                    n = 0
                    for dst in (rx, kx):
                        for f in range(4):
                            act.wait_ge(mm.sem, mm.at(n + 1))
                            act.copy(dst[:, 2 * f:2 * f + 2, :], bank(n % 4).rearrange("p (m s) -> p m s", m=2)).then_inc(evac.up(), 1)
                            n += 1
                    for u in range(2):
                        for t in range(T):
                            act.wait_ge(mm.sem, mm.at(n + 1))
                            for half in range(2):
                                o = UV[64:128, 2 * t + half, :, 4 * u:4 * u + 4, :].rearrange("p g m v -> p m g v")
                                ins = act.copy(o, bank(n % 4)[64 * half:64 * half + 64, :].rearrange("p (m g v) -> p m g v", m=4, g=2))
                            ins.then_inc(evac.up(), 1)
                            n += 1
                    for i, (hid, fn, rank, dst, fn2, bias) in enumerate([(hw, ACT.Tanh, 64, sgm, ACT.Sigmoid, "w0"), (ha, ACT.Copy, 64, ax, ACT.Sigmoid, "a0"),
                                                                         (hg, ACT.Sigmoid, 128, gT, ACT.Copy, None)]):
                        act.wait_ge(mm.sem, mm.at(n + 1))
                        act.activation(hid, bank(n % 4)[0:rank, 0:SEQ], fn).then_inc(evac.up(), 1)
                        n += 1
                        for f in range(4):
                            act.wait_ge(mm.sem, mm.at(n + 1))
                            for m in range(2):
                                k = 2 * f + m
                                src = bank(n % 4)[:, m * SEQ:(m + 1) * SEQ]
                                ins = act.activation(dst[:, k, :], src, fn2) if bias is None else act.activation(dst[:, k, :], src, fn2, bias=col(bias, k))
                            ins.then_inc(evac.up(), 1)
                            n += 1

            cum, kk, scratch = fm(0), fm(1), fm(3)
            spread = rows[0:HEADS, 0, :].rearrange("p (m f) -> p m f", m=KD)
            heads16 = rows[:, 1, 0:KD * HEADS].rearrange("p (m a) -> p m a", m=KD)
            reset = rows[:, 1, 256:512]
            pair = rows[:, 1, 512:514]
            with new_block() as block:
                c_in, step_a = sig("small_loaded"), sig("act_step")
                kk_raw, sq, ss_mm, nrm, inv_ready, wide_mm, wide_used = (sig(x) for x in ("kk_ready", "squares_ready", "scores_ready", "row_root", "inverse_ready", "product_ready", "dve_evacuated"))
                rk_ready, bonus_mm, cum_ready, diff_ready = sig("bonus_terms"), sig("transposed"), sig("cumsum_ready"), sig("cumsum_before")
                exp_ready, exp_used = sig("exps_ready"), sig("exps_used")
                root = mask.rearrange("p t s -> p (t s)")[0:HEADS, 0:SEQ]
                rin = mask.rearrange("p t s -> p (t s)")[0:HEADS, SEQ:2 * SEQ]

                @block.sync
                def _(sp):
                    sp.dma_start(spread, d["spread"]).then_inc(c_in.up(16), 16)
                    sp.dma_start(heads16, d["heads16"]).then_inc(c_in.up(16), 16)
                    sp.dma_start(reset, d["reset"]).then_inc(c_in.up(16), 16)
                    sp.dma_start(pair, d["pair"]).then_inc(c_in.up(16), 16)

                @block.vector
                def _(dve):
                    def step(ins):
                        link(dve, "dve_step", ins)
                    for m in range(KD):
                        dve.tensor_scalar(kk[:, m, :], kx[:, m, :], col("k_k", m), None, ALU.mult).then_inc(kk_raw.up(), 1)
                    dve.wait_ge(c_in.sem, c_in.at(64))
                    for m in range(KD):
                        ins = dve.tensor_tensor_scan(cum[:, m, :], reset, sgm[:, m, :], 0.0, ALU.mult, ALU.add)
                    ins.then_inc(cum_ready.up(), 1)
                    dve.wait_ge(sq.sem, sq.at(2))
                    dve.wait_ge(ss_mm.sem, ss_mm.at(1))
                    for m in range(KD):
                        ins = dve.tensor_scalar(scratch[:, m, :], ax[:, m, :], 1.0, col("k_a", m), ALU.subtract, ALU.mult)
                    step(ins)
                    step(dve.scalar_tensor_tensor(kx, scratch, 1.0, kx, ALU.add, ALU.mult))
                    for m in range(KD):
                        ins = dve.scalar_tensor_tensor(xT[:, m, :], rx[:, m, :], col("r_k", m), kx[:, m, :], ALU.mult, ALU.mult)
                    ins.then_inc(rk_ready.up(), 1)
                    dve.wait_ge(nrm.sem, nrm.at(1))
                    step(dve.tensor_scalar(root, root, 1e-12, None, ALU.max))
                    dve.reciprocal(rin, root).then_inc(inv_ready.up(), 1)
                    dve.tensor_tensor(sgm, cum, sgm, ALU.subtract).then_inc(diff_ready.up(), 1)
                    dve.wait_ge(exp_ready.sem, exp_ready.at(1))
                    dve.tensor_copy(pc, by_chunk(scratch)[:, :, :, CHUNK - 1])
                    dve.tensor_tensor(ARs[:, :, :, 1, :], by_chunk(rx), by_chunk(scratch), ALU.mult)
                    dve.wait_ge(exp_ready.sem, exp_ready.at(2))
                    dve.tensor_tensor(kx, kx, cum, ALU.mult)
                    dve.tensor_tensor(ax, ax, cum, ALU.mult)
                    for n in range(4):
                        dve.wait_ge(wide_mm.sem, wide_mm.at(n + 1))
                        x = kk[:, 2 * n:2 * n + 2, :]
                        ins = dve.tensor_tensor(x, x, bank(n + 1).rearrange("p (m s) -> p m s", m=2), ALU.mult)
                    step(ins)
                    dve.wait_ge(exp_ready.sem, exp_ready.at(3))
                    dve.scalar_tensor_tensor(ARs[:, :, :, 0, :], by_chunk(kk), -1.0, by_chunk(sgm), ALU.mult, ALU.mult).then_inc(exp_used.up(), 1)
                    dve.wait_ge(exp_used.sem, exp_used.at(1))
                    dve.tensor_tensor(BKs[:, :, :, 0, :], by_chunk(ax), by_chunk(kk), ALU.mult)
                    dve.wait_ge(bonus_mm.sem, bonus_mm.at(1))
                    dve.tensor_copy(bonus[64:128].rearrange("p c a -> p (c a)"), bank(5)[64:128, 0:NCH * HEADS])

                @block.scalar
                def _(act):
                    act.wait_ge(kk_raw.sem, kk_raw.at(KD))
                    act.activation(scratch, kk, ACT.Square).then_inc(sq.up(2), 2)
                    act.wait_ge(ss_mm.sem, ss_mm.at(1))
                    act.activation(root, bank(0)[0:HEADS, 0:SEQ], ACT.Sqrt).then_inc(nrm.up(), 1)
                    act.wait_ge(rk_ready.sem, rk_ready.at(1))
                    act.wait_ge(cum_ready.sem, cum_ready.at(1))
                    act.activation(scratch, cum, ACT.Exp, scale=DECAY).then_inc(exp_ready.up(), 1)
                    act.wait_ge(diff_ready.sem, diff_ready.at(1))
                    act.wait_ge(exp_ready.sem, exp_ready.at(1))
                    act.activation(cum, cum, ACT.Exp, scale=-DECAY).then_inc(exp_ready.up(), 1)
                    act.activation(sgm, sgm, ACT.Exp, scale=DECAY).then_inc(exp_ready.up(), 1)
                    act.wait_ge(exp_used.sem, exp_used.at(1))
                    act.copy(BKs[:, :, :, 1, :], by_chunk(kx))

                @block.tensor
                def _(pe):
                    pe.wait_ge(c_in.sem, c_in.at(64))
                    pe.wait_ge(sq.sem, sq.at(2))
                    for m in range(KD):
                        last = pe.matmul(bank(0)[0:HEADS, 0:SEQ], heads16[:, m, :], scratch[:, m, :], start=(m == 0), stop=(m == KD - 1))
                    last.then_inc(ss_mm.up(), 1)
                    pe.wait_ge(rk_ready.sem, rk_ready.at(1))
                    for c in range(NCH):
                        for m in range(KD):
                            last = pe.matmul(bank(5)[64:128, c * HEADS + 2 * m:c * HEADS + 2 * m + 2], xT[:, m, c * CHUNK:(c + 1) * CHUNK], pair, start=True, stop=True)
                    last.then_inc(bonus_mm.up(), 1)
                    pe.wait_ge(inv_ready.sem, inv_ready.at(1))
                    for m in range(KD):
                        last = pe.matmul(bank(1 + m // 2)[:, (m % 2) * SEQ:(m % 2 + 1) * SEQ], spread[:, m, :], rin, start=True, stop=True)
                        if m % 2:
                            last.then_inc(wide_mm.up(), 1)

            G = [blk(i).rearrange("p (g m s) -> p g m s", g=2, m=KD) for i in range(2)]
            BKt = blk(2)[:, 0:1024].rearrange("p (m s) -> p m s", m=KD)
            AT = blk(5)[:, 0:1024].rearrange("p (m s) -> p m s", m=KD)
            AN = spare[:, 4096:5120].rearrange("p (m s) -> p m s", m=KD)
            X = blk(5)[:, 1024:1536].rearrange("p (m s) -> p m s", m=KD)
            XF = blk(5)[:, 1536:2048].rearrange("p (m s) -> p m s", m=KD)
            R = spare[:, 5120:5632].rearrange("p (m v) -> p m v", m=KD)
            Y = blk(2)[64:128, 1024:2048]
            Z = blk(8)[64:128, 0:1024]
            W1 = blk(8)[64:128, 1024:2048]
            ST = mask.rearrange("p t s -> p (t s)").rearrange("p (m v) -> p m v", m=KD)
            POWERS = 5
            GROUP = KD // 2
            VY, AN_BANK, AT_BANK, X_BANK, STEP_BANK = 0, 2, 4, 6, 7

            def BK(m, c):
                return BKs[:, m, c, :, :].rearrange("p w s -> p (w s)")

            def AR(m, c):
                return ARs[:, m, c, :, :].rearrange("p w s -> p (w s)")

            def half(g):
                return slice(64 * g, 64 * g + 64)

            def pairs(q):
                return slice(GROUP * q, GROUP * (q + 1))

            def by_pair(x):
                return x.rearrange("p (m s) -> p m s", m=KD)

            with new_block() as block:
                c_in = sig("small_loaded")
                n = {x: sig(x) for x in ("bk_turned", "bk_copied", "g_ready", "g_masked", "m_ready", "an_begun", "at_begun", "x_begun",
                                         "values_done", "rhs_ready", "rhs_copied0", "rhs_copied1", "u_ready", "u_copied0", "u_copied1", "y_ready",
                                         "state_ready", "state_updated", "y_copied", "z_ready", "z_turned", "z_gated")}
                powers_ready, x_ready = ([sig(f"{x}_ready{q}") for q in range(2)] for x in ("powers", "x"))
                an_copied, at_copied, x_added = ([sig(x + str(q)) for q in range(2)] for x in ("an_copied", "at_copied", "x_added"))

                def wait(eng, name, count):
                    eng.wait_ge(n[name].sem, n[name].at(count))

                @block.sync
                def _(sp):
                    sp.dma_start(rows[:, 0, :], d["lnx_w"].rearrange("(o f) -> o f", o=1).broadcast_to([P, D])).then_inc(c_in.up(16), 16)
                    sp.dma_start(rows[:, 1, :], d["lnx_b"].rearrange("(o f) -> o f", o=1).broadcast_to([P, D])).then_inc(c_in.up(16), 16)

                @block.tensor
                def _(pe):
                    def products(c):
                        for g in range(2):
                            for m in range(KD):
                                last = pe.matmul(bank(AN_BANK + 2 * g + m // 4)[:, (m % 4) * P:(m % 4 + 1) * P], BK(m, c)[half(g)], AR(m, c)[half(g)], start=True, stop=True)
                        last.then_inc(n["g_ready"].up(), 1)
                        for q in range(2):
                            if c:
                                pe.wait_ge(x_added[q].sem, x_added[q].at(POWERS * c))
                        for g in range(2):
                            if g:
                                wait(pe, "m_ready", 2 * c + 1)
                            for m in range(KD):
                                last = pe.matmul(bank(X_BANK)[half(g), m * 64:(m + 1) * 64], ARs[half(g), m, c, 0, :], BKs[half(g), m, c, 0, :], start=True, stop=True)
                            last.then_inc(n["m_ready"].up(), 1)

                    def power(c, j):
                        for q in range(2):
                            if j == 0:
                                wait(pe, "at_begun", c + 1)
                                wait(pe, "an_begun", c + 1)
                            else:
                                pe.wait_ge(an_copied[q].sem, an_copied[q].at(POWERS * c + j))
                            if 0 < j < POWERS:
                                pe.wait_ge(at_copied[q].sem, at_copied[q].at((POWERS - 1) * c + j))
                            ms = range(GROUP * q, GROUP * (q + 1))
                            if j < POWERS - 1:
                                for m in ms:
                                    last = pe.matmul(bank(AT_BANK + q)[:, (m % GROUP) * P:(m % GROUP + 1) * P], AN[:, m, :], AT[:, m, :], start=True, stop=True)
                            if j:
                                if j == 1:
                                    wait(pe, "x_begun", c + 1)
                                else:
                                    pe.wait_ge(x_added[q].sem, x_added[q].at(POWERS * c + j - 1))
                                if q or j > 1:
                                    pe.wait_ge(x_added[1 - q].sem, x_added[1 - q].at(POWERS * c + j - 1 + q))
                                for m in ms:
                                    last = pe.matmul(bank(X_BANK)[:, m * 64:(m + 1) * 64], AN[:, m, :], X[:, m, :], start=True, stop=True)
                                last.then_inc(x_ready[q].up(), 1)
                            if j < POWERS:
                                for m in ms:
                                    last = pe.matmul(bank(AN_BANK + q)[:, (m % GROUP) * P:(m % GROUP + 1) * P], AT[:, m, :], AN[:, m, :], start=True, stop=True)
                                last.then_inc(powers_ready[q].up(), 1)

                    def values(c):
                        if c:
                            wait(pe, "y_copied", 2 * c)
                        for g in range(2):
                            for m in range(KD):
                                last = pe.matmul(bank(VY + g)[:, m * 64:(m + 1) * 64], G[c % 2][64:128, g, m, :], UV[64:128, c, g, m, :],
                                                 start=(m == 0), stop=False, skip_group_check=True)
                        last.then_inc((n["values_done"] if c else n["rhs_ready"]).up(), 1)

                    def z_turn(c):
                        wait(pe, "z_ready", c + 1)
                        for m in range(KD):
                            last = pe.transpose(bank(STEP_BANK)[:, m * CHUNK:(m + 1) * CHUNK], Z[:, m * P:(m + 1) * P], ident[64:128, 64:128])
                        last.then_inc(n["z_turned"].up(), 1)

                    products(0)
                    for j in range(POWERS):
                        power(0, j)
                    values(0)
                    power(0, POWERS)
                    for c in range(NCH):
                        ahead = c + 1 < NCH
                        for m in range(KD):
                            last = pe.transpose(bank(AN_BANK + m // 4)[:, (m % 4) * P:(m % 4 + 1) * P], BK(m, c), ident[:])
                            if m % 4 == 3:
                                last.then_inc(n["bk_turned"].up(), 1)
                        if c:
                            wait(pe, "state_updated", c)
                            wait(pe, "values_done", c)
                            for g in range(2):
                                for m in range(KD):
                                    last = pe.matmul(bank(VY + g)[:, m * 64:(m + 1) * 64], AR(m, c)[half(g)], ST[half(g), m, :], start=False, stop=False, skip_group_check=True)
                            last.then_inc(n["rhs_ready"].up(), 1)
                        if ahead:
                            wait(pe, "bk_copied", 2 * c + 2)
                            products(c + 1)
                        for g in range(2):
                            wait(pe, f"rhs_copied{g}", c + 1)
                            pe.wait_ge(x_added[g].sem, x_added[g].at(POWERS * (c + 1)))
                        if c >= 2:
                            wait(pe, "z_gated", c - 1)
                        for g in range(2):
                            if g:
                                wait(pe, "u_ready", 2 * c + 1)
                            for m in range(KD):
                                last = pe.matmul(bank(STEP_BANK)[half(g), m * 64:(m + 1) * 64], XF[half(g), m, :], R[half(g), m, :], start=True, stop=True)
                            last.then_inc(n["u_ready"].up(), 1)
                        if ahead:
                            power(c + 1, 0)
                        wait(pe, "u_copied0", c + 1)
                        wait(pe, "u_copied1", c + 1)
                        for g in range(2):
                            for m in range(KD):
                                last = pe.matmul(bank(VY + g)[64:128, m * 64:(m + 1) * 64], G[c % 2][0:64, g, m, 64:128], UV[0:64, c, g, m, :],
                                                 start=False, stop=(m == KD - 1), skip_group_check=True)
                        last.then_inc(n["y_ready"].up(), 1)
                        wait(pe, "bk_copied", 2 * c + 2)
                        for g in range(2):
                            for m in range(KD):
                                last = pe.matmul(bank(STEP_BANK)[half(g), m * 64:(m + 1) * 64], BKt[:, m, half(g)], UV[:, c, g, m, :], start=True, stop=True)
                        last.then_inc(n["state_ready"].up(), 1)
                        if ahead:
                            power(c + 1, 1)
                        if c:
                            wait(pe, "state_updated", c + 1)
                            z_turn(c - 1)
                        if ahead:
                            for j in range(2, POWERS):
                                power(c + 1, j)
                            values(c + 1)
                            power(c + 1, POWERS)
                    wait(pe, "z_gated", NCH - 1)
                    z_turn(NCH - 1)

                @block.scalar
                def _(act):
                    def begin_at(c):
                        wait(act, "g_masked", 4 * (c + 1))
                        for g in range(2):
                            ins = act.copy(AT[half(g), :, half(g)], G[c % 2][0:64, g, :, 0:64])
                        ins.then_inc(n["at_begun"].up(), 1)

                    def copy_at(c, j, q):
                        if c < NCH:
                            act.wait_ge(powers_ready[q].sem, powers_ready[q].at(POWERS * c + j + 1))
                            act.copy(AT[:, pairs(q), :], bank(AT_BANK + q).rearrange("p (m s) -> p m s", m=GROUP)).then_inc(at_copied[q].up(), 1)

                    begin_at(0)
                    for j in range(POWERS - 1):
                        copy_at(0, j, 0)
                        copy_at(0, j, 1)
                    for c in range(NCH):
                        for f in range(2):
                            wait(act, "bk_turned", 2 * c + f + 1)
                            act.copy(BKt[:, 4 * f:4 * f + 4, :], bank(AN_BANK + f).rearrange("p (m s) -> p m s", m=4)).then_inc(n["bk_copied"].up(), 1)
                        wait(act, "rhs_ready", c + 1)
                        act.copy(R[half(0)], by_pair(bank(VY)[0:64, :])).then_inc(n["rhs_copied0"].up(), 1)
                        if c + 1 < NCH:
                            begin_at(c + 1)
                        wait(act, "u_ready", 2 * c + 1)
                        act.copy(UV[0:64, c, 0, :, :], by_pair(bank(STEP_BANK)[half(0), :])).then_inc(n["u_copied0"].up(), 1)
                        copy_at(c + 1, 0, 0)
                        copy_at(c + 1, 0, 1)
                        wait(act, "y_ready", c + 1)
                        if c:
                            wait(act, "z_ready", c)
                        for g in range(2):
                            act.copy(Y.rearrange("p (m g v) -> p m g v", m=KD, g=2)[:, :, g, :], by_pair(bank(VY + g)[64:128, :])).then_inc(n["y_copied"].up(), 1)
                        copy_at(c + 1, 1, 0)
                        copy_at(c + 1, 1, 1)
                        copy_at(c + 1, 2, 0)
                        act.wait_ge(sig("centred").sem, sig("centred").at(c + 1))
                        act.activation(W1, Y, ACT.Square).then_inc(sig("squares_ready").up(), 1)
                        copy_at(c + 1, 2, 1)
                        copy_at(c + 1, 3, 0)
                        act.wait_ge(sig("mean_square").sem, sig("mean_square").at(c + 1))
                        act.activation(stat[64:128, 32:48], stat[64:128, 16:32], ACT.Sqrt).then_inc(sig("row_root").up(), 1)
                        copy_at(c + 1, 3, 1)

                @block.vector
                def _(dve):
                    def step(ins):
                        link(dve, "dve_step", ins)

                    def by_head(s):
                        return s.rearrange("p (a o) -> p a o", o=1).broadcast_to([64, HEADS, HD])

                    def rows3(x):
                        return x.rearrange("p (a v) -> p a v", a=HEADS)

                    sm = stat[64:128, 0:16]
                    wide_g = gm.rearrange("p (o s) -> p o s", o=1).broadcast_to([P, 4, P])
                    wide_l = lmask.rearrange("p (o s) -> p o s", o=1).broadcast_to([P, KD, CHUNK])
                    wide_i = ident[0:64, 0:64].rearrange("p (o s) -> p o s", o=1).broadcast_to([64, KD, 64])

                    def begin(c):
                        wait(dve, "g_ready", c + 1)
                        for b in range(4):
                            dve.tensor_tensor(G[c % 2][:, b // 2, 4 * (b % 2):4 * (b % 2) + 4, :], bank(AN_BANK + b).rearrange("p (m s) -> p m s", m=4), wide_g, ALU.mult).then_inc(n["g_masked"].up(), 1)
                        for g in range(2):
                            wait(dve, "m_ready", 2 * c + g + 1)
                            ins = dve.tensor_tensor(AN[half(g), :, half(g)], by_pair(bank(X_BANK)[half(g), :]), wide_l[half(g)], ALU.mult)
                        ins.then_inc(n["an_begun"].up(), 1)
                        wait(dve, "g_masked", 4 * (c + 1))
                        for g in range(2):
                            ins = dve.tensor_tensor(X[half(g)], G[c % 2][0:64, g, :, 0:64], wide_i, ALU.add)
                        ins.then_inc(n["x_begun"].up(), 1)

                    def copy_power(c, j, q):
                        if c == NCH:
                            return
                        if j:
                            dve.wait_ge(x_ready[q].sem, x_ready[q].at(POWERS * c + j))
                            dve.tensor_tensor((XF if j == POWERS else X)[:, pairs(q), :], X[:, pairs(q), :], by_pair(bank(X_BANK))[:, pairs(q), :], ALU.add).then_inc(x_added[q].up(), 1)
                        if j < POWERS:
                            dve.wait_ge(powers_ready[q].sem, powers_ready[q].at(POWERS * c + j + 1))
                            dve.tensor_copy(AN[:, pairs(q), :], bank(AN_BANK + q).rearrange("p (m s) -> p m s", m=GROUP)).then_inc(an_copied[q].up(), 1)

                    def gate(c):
                        wait(dve, "z_turned", c + 1)
                        dve.tensor_tensor(xT[:, :, c * CHUNK:(c + 1) * CHUNK], by_pair(bank(STEP_BANK)), gT[:, :, c * CHUNK:(c + 1) * CHUNK], ALU.mult).then_inc(n["z_gated"].up(), 1)

                    dve.memset(AT, 0.0)
                    step(dve.memset(AN, 0.0))
                    dve.wait_ge(masks_in.sem, masks_in.count)
                    begin(0)
                    for j in range(POWERS + 1):
                        copy_power(0, j, 0)
                        copy_power(0, j, 1)
                    dve.wait_ge(c_in.sem, c_in.at(32))
                    for c in range(NCH):
                        wait(dve, "rhs_ready", c + 1)
                        dve.tensor_copy(R[half(1)], by_pair(bank(VY + 1)[0:64, :])).then_inc(n["rhs_copied1"].up(), 1)
                        if c + 1 < NCH:
                            begin(c + 1)
                        wait(dve, "u_ready", 2 * c + 2)
                        dve.tensor_copy(UV[0:64, c, 1, :, :], by_pair(bank(STEP_BANK)[half(1), :])).then_inc(n["u_copied1"].up(), 1)
                        copy_power(c + 1, 0, 0)
                        copy_power(c + 1, 0, 1)
                        wait(dve, "state_ready", c + 1)
                        new = by_pair(bank(STEP_BANK))
                        decay = pc[:, :, c:c + 1].broadcast_to([P, KD, HD])
                        if c:
                            step(dve.tensor_tensor(ST, ST, new, ALU.add))
                        dve.tensor_tensor(ST, ST if c else new, decay, ALU.mult).then_inc(n["state_updated"].up(), 1)
                        copy_power(c + 1, 1, 0)
                        wait(dve, "y_copied", 2 * c + 2)
                        step(dve.tensor_reduce(sm, rows3(Y), AX, ALU.add))
                        copy_power(c + 1, 1, 1)
                        step(dve.tensor_scalar(sm, sm, 1.0 / HD, None, ALU.mult))
                        dve.tensor_tensor(rows3(Y), rows3(Y), by_head(sm), ALU.subtract).then_inc(sig("centred").up(), 1)
                        copy_power(c + 1, 2, 0)
                        if c:
                            gate(c - 1)
                        copy_power(c + 1, 2, 1)
                        dve.wait_ge(sig("squares_ready").sem, sig("squares_ready").at(c + 1))
                        step(dve.tensor_reduce(sm, rows3(W1), AX, ALU.add))
                        copy_power(c + 1, 3, 0)
                        dve.tensor_scalar(stat[64:128, 16:32], sm, 1.0 / HD, LNX_EPS, ALU.mult, ALU.add).then_inc(sig("mean_square").up(), 1)
                        for g in range(2):
                            w = bonus[64:128, c, g:HEADS:2].rearrange("p (m o) -> p m o", o=1).broadcast_to([64, KD, HD])
                            ins = dve.tensor_tensor(W1.rearrange("p (m g v) -> p m g v", m=KD, g=2)[:, :, g, :], UV[64:128, c, g, :, :], w, ALU.mult)
                        step(ins)
                        copy_power(c + 1, 3, 1)
                        step(dve.tensor_tensor(W1, W1, rows[64:128, 1, :], ALU.add))
                        copy_power(c + 1, 4, 0)
                        dve.wait_ge(sig("row_root").sem, sig("row_root").at(c + 1))
                        step(dve.reciprocal(stat[64:128, 48:64], stat[64:128, 32:48]))
                        step(dve.tensor_tensor(rows3(Y), rows3(Y), by_head(stat[64:128, 48:64]), ALU.mult))
                        copy_power(c + 1, 4, 1)
                        step(dve.tensor_tensor(Y, Y, rows[64:128, 0, :], ALU.mult))
                        copy_power(c + 1, 5, 0)
                        copy_power(c + 1, 5, 1)
                        dve.tensor_tensor(Z, Y, W1, ALU.add).then_inc(n["z_ready"].up(), 1)
                    gate(NCH - 1)
            project(2, residual=1.0, loads_due=3)

        memK, memV = fm(0), tok(1)

        def ln_cols(i):
            return col("ln_g", i * KD, KD), col("ln_b", i * KD, KD)

        def memory_kv():
            transpose_all([(tok(1), fm(3))])
            project_features(fm(3), memK, act_aside=tables_act, dve_aside=tables_dve)
            project(2, dest=lambda u, t: memV[:, t, u * COLS:(u + 1) * COLS], src=fm(3))

        def differential():
            project(6, dest=lambda u, t: tok(2 + u // 2)[:, t, (u % 2) * COLS:(u % 2 + 1) * COLS],
                    rotary=lambda u: (8, HD, 0, DIFF_ROPE, cosd, sind, blk(5)) if u < 4 else None)
            transpose_all([(tok(2), fm(6)), (tok(3), fm(7))])

            def hs(m):
                return slice(64 * (m % 2), 64 * (m % 2) + 64)
            o = tok(5)
            attention(16, lambda m, t: [fm(6)[hs(m), m // 2, t * P:(t + 1) * P]], lambda m: [fm(7)[hs(m), m // 2, :]],
                      lambda m, kt: tok(4)[:, kt, (m // 2) * P:(m // 2 + 1) * P], P, lambda m, t: o[:, t, (m // 2) * P:(m // 2 + 1) * P],
                      HD ** -0.5, True, (blk(8), blk(9)), diff=True)
            with new_block() as block:
                sq, ms, root = sig("squares_ready"), sig("mean_square"), sig("row_root")
                o3 = blk(5).rearrange("p (a f) -> p a f", f=P)

                @block.scalar
                def _(act):
                    act.activation(blk(2), blk(5), ACT.Square).then_inc(sq.up(), 1)
                    act.wait_ge(ms.sem, ms.at(1))
                    act.activation(stat[:, 16:32], stat[:, 0:16], ACT.Sqrt).then_inc(root.up(), 1)

                @block.vector
                def _(dve):
                    dve.wait_ge(sq.sem, sq.at(1))
                    link(dve, "dve_step", dve.tensor_reduce(stat[:, 0:16], blk(2).rearrange("p (a f) -> p a f", f=P), AX, ALU.add))
                    dve.tensor_scalar(stat[:, 0:16], stat[:, 0:16], 1.0 / P, LN_EPS, ALU.mult, ALU.add).then_inc(ms.up(), 1)
                    link(dve, "dve_step", dve.tensor_scalar(stat[:, 48:49], col("subln", 0), 1.0 - LAMBDA_INIT, None, ALU.mult))
                    dve.wait_ge(root.sem, root.at(1))
                    link(dve, "dve_step", dve.reciprocal(stat[:, 32:48], stat[:, 16:32]))
                    link(dve, "dve_step", dve.tensor_tensor(o3, o3, stat[:, 32:48].rearrange("p (a o) -> p a o", o=1).broadcast_to([P, 16, P]), ALU.mult))
            transpose_all([(o, xT)], scale=stat[:, 48:49])
            project(2, residual=ALPHA, row_src=(d["ln_g"][0], d["ln_b"][0]))
            norm("ln", *ln_cols(0))

        def cross_attention(layer):
            project_features(xT, fm(2))
            o = tok(3)
            attention(4, lambda m, t: [fm(2)[:, 2 * m + i, t * P:(t + 1) * P] for i in range(2)], lambda m: [memK[:, 2 * m + i, :] for i in range(2)],
                      lambda m, kt: memV[:, kt, m * 256:(m + 1) * 256], 256, lambda m, t: o[:, t, m * 256:(m + 1) * 256],
                      256 ** -0.5, False, (blk(4), blk(5)))
            transpose_all([(o, xT)])
            project(2, residual=ALPHA, row_src=(d["ln_g"][3 * layer + 1], d["ln_b"][3 * layer + 1]))
            norm("ln", *ln_cols(3 * layer + 1))

        def mixture(layer, gain, shift, store=None):
            w = blk(6)
            lg, key = w[:, 0:40].rearrange("p (t n) -> p t n", t=T), w[:, 40:48].rearrange("p (t n) -> p t n", t=T)
            gsel, es = w[:, 48:56].rearrange("p (t n) -> p t n", t=T), w[:, 56:64].rearrange("p (t n) -> p t n", t=T)
            eg = w[:, 64:96].rearrange("p (t e g) -> p t e g", t=T, e=4)
            oh1, oh2 = w[:, 96:104].rearrange("p (t n) -> p t n", t=T), w[:, 104:112].rearrange("p (t n) -> p t n", t=T)
            es2, gexp = w[:, 112:120].rearrange("p (t n) -> p t n", t=T), w[:, 120:128].rearrange("p (t n) -> p t n", t=T)
            gmx, kmx, m1, m2 = w[:, 128:130], w[:, 130:132], w[:, 132:134], w[:, 134:136]
            gsum, dm, de, den = w[:, 136:138], w[:, 138:140], w[:, 140:142], w[:, 142:144]
            w1, w2, tmp = w[:, 144:146], w[:, 146:148], w[:, 148:156].rearrange("p (t n) -> p t n", t=T)
            comb = stat[:, 64:96].rearrange("p (t g e) -> p t g e", t=T, g=4)
            bias, rank = w[:, 192:212], w[:, 212:216]
            sel, place = w[:, 224:256].rearrange("p (t g e) -> p t g e", t=T, g=4), w[:, 256:288]
            tri, ones, slot_no = w[:, 512:512 + P], w[:, 640:640 + P], w[:, 768:768 + SLOTS_E]
            put, put_w = blk(7), blk(8)
            half = PAIRS * SLOTS_E
            xg = [(range(0, 2), blk(2).rearrange("p (k n) -> p k n", k=2)), (range(2, KD), span(3, 6).rearrange("p (k n) -> p k n", k=KD - 2))]
            swT = xT[:].rearrange("p k s -> p (k s)")
            with new_block() as block:
                got, mm, e_in, e_out = sig("small_loaded"), sig("product_ready"), sig("max_ready"), sig("exps_ready")
                chosen, placed, tp, ev = sig("experts_chosen"), sig("tokens_placed"), sig("transposed"), [sig("act_evacuated"), sig("dve_evacuated")]

                def copy_out(copy, scaled_copy, eng, e):
                    for n in range(e, 2 * KD, 2):
                        eng.wait_ge(mm.sem, mm.at(n + 3))
                        ks, x = xg[0 if n // 2 in xg[0][0] else 1]
                        scaled_copy(x[:, n // 2 - ks[0], e * half:(e + 1) * half], bank(2 + n % 4), n // 2).then_inc(ev[e].up(), 1)
                    for n in range(e, PAIRS // 2, 2):
                        eng.wait_ge(tp.sem, tp.at(n + 1))
                        copy(swT[:, n * 2 * SEQ:(n + 1) * 2 * SEQ], bank(2 + n))

                @block.sync
                def _(sp):
                    sp.dma_start(bias, d["route_b"][layer].rearrange("(o f) -> o f", o=1).broadcast_to([P, ROUTE])).then_inc(got.up(16), 16)
                    sp.dma_start(w[:, 512:512 + 2 * P + SLOTS_E], d["slots"]).then_inc(got.up(16), 16)
                    sp.dma_start(rank, d["rank"].rearrange("(o f) -> o f", o=1).broadcast_to([P, 4])).then_inc(got.up(16), 16)

                @block.tensor
                def _(pe):
                    for t in range(T):
                        for k in range(KD):
                            last = pe.matmul(bank(0)[:, t * ROUTE:(t + 1) * ROUTE], xT[:, k, t * P:(t + 1) * P], col("route", (layer * KD + k) * ROUTE, ROUTE),
                                             start=(k == 0), stop=(k == KD - 1))
                    last.then_inc(mm.up(), 1)
                    pe.wait_ge(got.sem, got.at(48))
                    pe.wait_ge(chosen.sem, chosen.at(1))
                    s0, s1 = [sel[:, t].rearrange("p g e -> p (g e)") for t in range(T)]
                    n = N_EXPERTS
                    pe.matmul(bank(1)[:, 0:n], tri, s0, start=True, stop=True)
                    for o, a in ((n, tri), (2 * n, ones)):
                        pe.matmul(bank(1)[:, o:o + n], a, s1, start=True, stop=False)
                        last = pe.matmul(bank(1)[:, o:o + n], ones, s0, start=False, stop=True)
                    last.then_inc(mm.up(), 1)
                    pe.wait_ge(placed.sem, placed.at(1))
                    for n in range(2 * KD):
                        if n >= 4:
                            pe.wait_ge(ev[n % 2].sem, ev[n % 2].at(n // 2 - 1))
                        k, c = n // 2, n % 2
                        for t in range(T):
                            last = pe.matmul(bank(2 + n % 4), h[:, t, k * P:(k + 1) * P], put[:, t * D + c * half:t * D + (c + 1) * half], start=(t == 0), stop=(t == T - 1))
                        last.then_inc(mm.up(), 1)
                    pe.wait_ge(placed.sem, placed.at(2))
                    for n in range(PAIRS // 2):
                        pe.wait_ge(ev[n % 2].sem, ev[n % 2].at(KD - 1 + n // 2))
                        for q in range(2):
                            for t in range(T):
                                last = pe.transpose(bank(2 + n)[:, (q * T + t) * P:(q * T + t + 1) * P], put_w[:, t * D + (2 * n + q) * P:t * D + (2 * n + q + 1) * P], ident[:])
                        last.then_inc(tp.up(), 1)

                @block.scalar
                def _(act):
                    act.wait_ge(e_in.sem, e_in.at(1))
                    act.activation(gexp, gexp, ACT.Exp).then_inc(e_out.up(), 1)
                    act.wait_ge(e_in.sem, e_in.at(2))
                    act.activation(de, dm, ACT.Exp).then_inc(e_out.up(), 1)
                    copy_out(act.copy, lambda o, i, k: act.activation(o, i, ACT.Identity, bias=shift[:, k:k + 1], scale=gain[:, k:k + 1]), act, 0)

                @block.vector
                def _(dve):
                    def step(ins):
                        link(dve, "dve_step", ins)

                    def w4(x):
                        return x.rearrange("p (t o) -> p t o", o=1).broadcast_to([P, T, 4])

                    wr = rank.rearrange("p (o n) -> p o n", o=1).broadcast_to([P, T, 4])

                    def first_max(x, m, onehot):
                        step(dve.tensor_reduce(m, x, AX, ALU.max))
                        step(dve.tensor_tensor(key, x, w4(m), ALU.is_equal))
                        step(dve.tensor_tensor(key, key, wr, ALU.mult))
                        step(dve.tensor_reduce(kmx, key, AX, ALU.max))
                        step(dve.tensor_tensor(onehot, key, w4(kmx), ALU.is_equal))

                    dve.wait_ge(mm.sem, mm.at(1))
                    dve.wait_ge(got.sem, got.at(48))
                    step(dve.tensor_tensor(lg, bank(0)[:, 0:T * ROUTE].rearrange("p (t n) -> p t n", t=T), bias.rearrange("p (o n) -> p o n", o=1).broadcast_to([P, T, ROUTE]), ALU.add))
                    first_max(lg[:, :, 0:4], gmx, gsel)
                    dve.tensor_tensor(gexp, lg[:, :, 0:4], w4(gmx), ALU.subtract).then_inc(e_in.up(), 1)
                    for t in range(T):
                        el = lg[:, t, 4:ROUTE].rearrange("p (g e) -> p e g", g=4)
                        ins = dve.tensor_tensor(eg[:, t], el, gsel[:, t:t + 1, :].broadcast_to([P, 4, 4]), ALU.mult)
                    step(ins)
                    step(dve.tensor_reduce(es, eg, AX, ALU.add))
                    first_max(es, m1, oh1)
                    step(dve.scalar_tensor_tensor(es2, oh1, MASKED, es, ALU.mult, ALU.add))
                    first_max(es2, m2, oh2)
                    dve.tensor_tensor(dm, m2, m1, ALU.subtract).then_inc(e_in.up(), 1)
                    step(dve.tensor_tensor(tmp, oh1, oh2, ALU.add))
                    for t in range(T):
                        g = gsel[:, t, :].rearrange("p (g o) -> p g o", o=1).broadcast_to([P, 4, 4])
                        ins = dve.tensor_tensor(sel[:, t], tmp[:, t:t + 1, :].broadcast_to([P, 4, 4]), g, ALU.mult)
                    ins.then_inc(chosen.up(), 1)
                    dve.wait_ge(e_out.sem, e_out.at(2))
                    step(dve.tensor_reduce(gsum, gexp, AX, ALU.add))
                    step(dve.tensor_scalar(den, de, 1.0, None, ALU.add))
                    step(dve.tensor_tensor(den, den, gsum, ALU.mult))
                    step(dve.reciprocal(w1, den))
                    step(dve.tensor_tensor(w2, w1, de, ALU.mult))
                    step(dve.tensor_tensor(oh1, oh1, w4(w1), ALU.mult))
                    step(dve.tensor_tensor(oh2, oh2, w4(w2), ALU.mult))
                    step(dve.tensor_tensor(tmp, oh1, oh2, ALU.add))
                    for t in range(T):
                        g = gsel[:, t, :].rearrange("p (g o) -> p g o", o=1).broadcast_to([P, 4, 4])
                        ins = dve.tensor_tensor(comb[:, t], tmp[:, t:t + 1, :].broadcast_to([P, 4, 4]), g, ALU.mult)
                    step(ins)
                    dve.wait_ge(mm.sem, mm.at(2))
                    step(dve.scalar_tensor_tensor(place, bank(1)[:, 0:T * N_EXPERTS], 1.0, w[:, 224:256], ALU.add, ALU.mult))
                    put3, put_w3 = [x.rearrange("p (a s) -> p a s", s=SLOTS_E) for x in (put, put_w)]

                    def by_expert(x):
                        return x.rearrange("p (a o) -> p a o", o=1).broadcast_to([P, T * N_EXPERTS, SLOTS_E])
                    ins = dve.tensor_tensor(put3, by_expert(place), slot_no.rearrange("p (o s) -> p o s", o=1).broadcast_to([P, T * N_EXPERTS, SLOTS_E]), ALU.is_equal)
                    ins.then_inc(placed.up(), 1)
                    dve.wait_ge(placed.sem, placed.at(1))
                    dve.tensor_tensor(put_w3, put3, by_expert(stat[:, 64:96]), ALU.mult).then_inc(placed.up(), 1)
                    step(dve.tensor_reduce(stat[:, 0:1], bank(1)[:, T * N_EXPERTS:(T + 1) * N_EXPERTS], AX, ALU.max))
                    dve.tensor_scalar(overflow[:], stat[:, 0:1], float(SLOTS_E), None, ALU.is_gt)
                    copy_out(dve.tensor_copy, lambda o, i, k: dve.tensor_scalar(o, i, gain[:, k:k + 1], shift[:, k:k + 1], ALU.mult, ALU.add), dve, 1)
            experts(layer, comb, xg, swT, (d["ln_g"][3 * layer + 2], d["ln_b"][3 * layer + 2]))
            norm("ln", *ln_cols(3 * layer + 2), store=store)

        def sparse_mla():
            cin = blk(2)[:, 0:T * 640].rearrange("p (t f) -> p t f", t=T)
            kpad = blk(3)[:, 1024:2048].rearrange("p (t a f) -> p t a f", t=T, a=4)
            cT = blk(4)[:, 0:1024].rearrange("p (k s) -> p k s", k=4)
            kiT = blk(4)[:, 1024:1280]
            q_tok, qi_tok, v_tok = tok(5), tok(6), tok(7)
            qT, kT, qiT = fm(8), fm(9), xT
            j0 = next_unit(1)
            with new_block() as block:
                mm, ev, dv = sig("product_ready"), sig("act_evacuated"), sig("dve_evacuated")
                sq, ms, root, ready, tp = sig("row_stats"), sig("mean_square"), sig("row_root"), sig("normed"), sig("transposed")
                ss = stat[:, 0:4].rearrange("p (t a) -> p t a", t=T)
                halves = (0, B_IN // 2, B_IN)

                @block.tensor
                def _(pe):
                    arrived(pe, j0)
                    w = ring[:, j0 % SLOTS, 0:KD * B_IN].rearrange("p (k n) -> p k n", k=KD)
                    for t in range(T):
                        for c in range(2):
                            for k in range(KD):
                                last = pe.matmul(bank(2 * t + c)[:, 0:B_IN // 2], xT[:, k, t * P:(t + 1) * P], w[:, k, halves[c]:halves[c + 1]], start=(k == 0), stop=(k == KD - 1))
                            last.then_inc(mm.up(), 1)
                    unit_done(j0, mm)
                    for t in range(T):
                        pe.wait_ge(ready.sem, ready.at(t + 1))
                        for k in range(4):
                            last = pe.transpose(bank(4 + t)[:, k * P:(k + 1) * P], cin[:, t, k * P:(k + 1) * P], ident[:])
                        last.then_inc(tp.up(), 1)
                    pe.wait_ge(ready.sem, ready.at(T + 1))
                    for a in range(2):
                        for t in range(T):
                            last = pe.transpose(bank(6)[:, (a * T + t) * P:(a * T + t + 1) * P], kpad[:, t, a, :], ident[:])
                    last.then_inc(tp.up(), 1)

                @block.scalar
                def _(act):
                    for t in range(T):
                        for c in range(2):
                            act.wait_ge(mm.sem, mm.at(2 * t + c + 1))
                            act.copy(cin[:, t, halves[c]:halves[c + 1]], bank(2 * t + c)[:, 0:B_IN // 2]).then_inc(ev.up(), 1)
                    act.wait_ge(ev.sem, ev.at(4))
                    for t in range(T):
                        for a in range(2):
                            act.activation(blk(5)[:, (2 * t + a) * 256:(2 * t + a + 1) * 256], cin[:, t, a * 256:(a + 1) * 256], ACT.Square, accum_out=ss[:, t, a:a + 1]).then_inc(sq.up(), 1)
                    act.wait_ge(ms.sem, ms.at(1))
                    act.activation(stat[:, 8:12], stat[:, 4:8], ACT.Sqrt).then_inc(root.up(), 1)
                    act.wait_ge(tp.sem, tp.at(T + 1))
                    for hd in range(KD):
                        act.copy(kT[96:128, hd, :], bank(6)[96:128, 0:SEQ])
                    act.copy(kiT, bank(6)[:, SEQ:2 * SEQ])

                @block.vector
                def _(dve):
                    def step(ins):
                        link(dve, "dve_step", ins)
                    step(dve.memset(kpad, 0.0))
                    dve.wait_ge(sq.sem, sq.at(4))
                    dve.tensor_scalar(stat[:, 4:8], stat[:, 0:4], 1.0 / Q_RANK, LN_EPS, ALU.mult, ALU.add).then_inc(ms.up(), 1)
                    dve.wait_ge(root.sem, root.at(1))
                    step(dve.reciprocal(stat[:, 12:16], stat[:, 8:12]))
                    for t in range(T):
                        for a in range(2):
                            x = cin[:, t, a * 256:(a + 1) * 256]
                            ins = dve.tensor_scalar(x, x, stat[:, 12 + 2 * t + a:13 + 2 * t + a], None, ALU.mult)
                        ins.then_inc(ready.up(), 1)
                    tmp = blk(5)[:, 1024:1536]
                    r0 = Q_RANK + KV_RANK
                    for t in range(T):
                        step(rope(dve, cin[:, t, r0:r0 + 32], 1, 32, 0, MLA_ROPE, cosr[:, t, :], sinr[:, t, :], tmp))
                        step(rope(dve, cin[:, t, r0 + 32:r0 + 96], 1, 64, 0, DIFF_ROPE, cosd[:, t, :], sind[:, t, :], tmp))
                        dve.tensor_copy(kpad[:, t, 0, 96:128], cin[:, t, r0:r0 + 32])
                        for a in range(2):
                            ins = dve.tensor_copy(kpad[:, t, 1, a * 64:(a + 1) * 64], cin[:, t, r0 + 32:r0 + 96])
                        step(ins)
                        x = cin[:, t, r0 + 96:r0 + 112]
                        step(dve.tensor_scalar(x, x, (IDX_HEADS * IDX_DIM) ** -0.5, None, ALU.mult))
                    dve.tensor_scalar(kpad[:, 0, 2, 0:1], kpad[:, 0, 2, 0:1], 1.0, None, ALU.mult).then_inc(ready.up(), 1)
                    for t in range(T):
                        dve.wait_ge(tp.sem, tp.at(t + 1))
                        for a, g in enumerate(("q_norm", "kv_norm")):
                            g3 = col(g, 0, 2).rearrange("p (k o) -> p k o", o=1).broadcast_to([P, 2, P])
                            dve.tensor_tensor(cT[:, 2 * a:2 * a + 2, t * P:(t + 1) * P], bank(4 + t)[:, a * 256:(a + 1) * 256].rearrange("p (k s) -> p k s", k=2), g3, ALU.mult)
                stream(block, 1)
            j0 = next_unit(2)
            with new_block() as block:
                mm, ev = sig("product_ready"), sig("act_evacuated")

                @block.tensor
                def _(pe):
                    n = 0
                    arrived(pe, j0)
                    w = ring[:, j0 % SLOTS, 0:4096].rearrange("p (a k n) -> p a k n", a=2, k=2)
                    for a in range(2):
                        for c in range(2):
                            for t in range(T):
                                if n >= 8:
                                    pe.wait_ge(ev.sem, ev.at(n - 7))
                                for k in range(2):
                                    last = pe.matmul(bank(n % 8), cT[:, k, t * P:(t + 1) * P], w[:, a, k, c * 512:(c + 1) * 512], start=(k == 0), stop=(k == 1))
                                last.then_inc(mm.up(), 1)
                                n += 1
                    unit_done(j0, mm)
                    arrived(pe, j0 + 1)
                    wk = ring[:, (j0 + 1) % SLOTS, 0:1536].rearrange("p (k n) -> p k n", k=2)
                    wv = ring[:, (j0 + 1) % SLOTS, 1536:3584].rearrange("p (k n) -> p k n", k=2)
                    for hd in range(KD):
                        if hd % 2 == 0:
                            pe.wait_ge(ev.sem, ev.at(n - 7))
                        for k in range(2):
                            last = pe.matmul(bank(n % 8)[0:MLA_NOPE, (hd % 2) * SEQ:(hd % 2 + 1) * SEQ], wk[:, k, hd * MLA_NOPE:(hd + 1) * MLA_NOPE], cT[:, 2 + k, :], start=(k == 0), stop=(k == 1))
                        if hd % 2:
                            last.then_inc(mm.up(), 1)
                            n += 1
                    for c in range(2):
                        for t in range(T):
                            pe.wait_ge(ev.sem, ev.at(n - 7))
                            for k in range(2):
                                last = pe.matmul(bank(n % 8), cT[:, 2 + k, t * P:(t + 1) * P], wv[:, k, c * 512:(c + 1) * 512], start=(k == 0), stop=(k == 1))
                            last.then_inc(mm.up(), 1)
                            n += 1
                    unit_done(j0 + 1, mm)
                stream(block, 2)

                @block.scalar
                def _(act):
                    n = 0
                    for a in (q_tok, qi_tok):
                        for c in range(2):
                            for t in range(T):
                                act.wait_ge(mm.sem, mm.at(n + 1))
                                act.copy(a[:, t, c * 512:(c + 1) * 512], bank(n % 8)).then_inc(ev.up(), 1)
                                n += 1
                    for hd in range(0, KD, 2):
                        act.wait_ge(mm.sem, mm.at(n + 1))
                        act.copy(kT[0:96, hd:hd + 2, :], bank(n % 8)[0:96, :].rearrange("p (a s) -> p a s", a=2)).then_inc(ev.up(), 1)
                        n += 1
                    for c in range(2):
                        for t in range(T):
                            act.wait_ge(mm.sem, mm.at(n + 1))
                            act.copy(v_tok[:, t, c * 512:(c + 1) * 512], bank(n % 8)).then_inc(ev.up(), 1)
                            n += 1

                @block.vector
                def _(dve):
                    scale_rows(dve)
                    tmp = blk(4)[:, 1280:2048]
                    for t in range(T):
                        dve.wait_ge(ev.sem, ev.at(4))
                        link(dve, "dve_step", rope(dve, q_tok[:, t, :], 8, P, MLA_NOPE, MLA_ROPE, cosr[:, t, :], sinr[:, t, :], tmp))
                    for t in range(T):
                        dve.wait_ge(ev.sem, ev.at(8))
                        link(dve, "dve_step", rope(dve, qi_tok[:, t, :], 16, IDX_DIM, 0, DIFF_ROPE, cosd[:, t, :], sind[:, t, :], tmp))
            transpose_all([(q_tok, qT), (qi_tok, qiT)])
            score, left = blk(5)[:, 0:512], blk(5)[:, 512:1024]
            relus = blk(6).rearrange("p (b s) -> p b s", b=4)
            top8 = stat[:, 0:16].rearrange("p (t n) -> p t n", t=T)
            with new_block() as block:
                mm, ev, summed = sig("product_ready"), sig("act_evacuated"), [sig("early_scores_summed"), sig("late_scores_summed")]
                found = [sig("early_keys_found"), sig("late_keys_found")]

                SUM = ((0, P), (P, P + SEQ))

                @block.tensor
                def _(pe):
                    for i in range(IDX_HEADS):
                        hs = slice(64 * (i % 2), 64 * (i % 2) + 64)
                        if i >= 4:
                            pe.wait_ge(ev.sem, ev.at(i - 3))
                        for t, (lo, hi) in enumerate(SUM):
                            last = pe.matmul(bank(i % 4)[:, lo:hi], qiT[hs, i // 2, t * P:(t + 1) * P], kiT[hs, 0:hi - lo], start=True, stop=True)
                        last.then_inc(mm.up(), 1)

                @block.scalar
                def _(act):
                    for i in range(IDX_HEADS):
                        act.wait_ge(mm.sem, mm.at(i + 1))
                        if i >= 4:
                            for t in range(T):
                                act.wait_ge(summed[t].sem, summed[t].at(i - 3))
                        act.activation(relus[:, i % 4, 0:P + SEQ], bank(i % 4)[:, 0:P + SEQ], ACT.Relu).then_inc(ev.up(), 1)

                @block.vector
                def _(dve):
                    w0 = Q_RANK + KV_RANK + MLA_ROPE + IDX_DIM
                    for i in range(IDX_HEADS):
                        dve.wait_ge(ev.sem, ev.at(i + 1))
                        for t, (lo, hi) in enumerate(SUM):
                            wi = cin[:, t, w0 + i:w0 + i + 1]
                            if i == 0:
                                dve.tensor_scalar(score[:, lo:hi], relus[:, 0, lo:hi], wi, None, ALU.mult).then_inc(summed[t].up(), 1)
                            else:
                                dve.wait_ge(summed[t].sem, summed[t].at(i))
                                dve.scalar_tensor_tensor(score[:, lo:hi], relus[:, i % 4, lo:hi], wi, score[:, lo:hi], ALU.mult, ALU.add).then_inc(summed[t].up(), 1)
                    for t, (lo, hi) in enumerate(SUM):
                        dve.wait_ge(summed[t].sem, summed[t].at(IDX_HEADS))
                        ins = dve.tensor_tensor(left[:, lo:hi], score[:, lo:hi], mask[:, t, 0:hi - lo], ALU.add)
                    link(dve, "dve_step", ins)
                    for _ in range(TOPK // 8):
                        for t, (lo, hi) in enumerate(SUM):
                            dve.max(top8[:, t, :], left[:, lo:hi]).then_inc(found[t].up(), 1)
                        for t, (lo, hi) in enumerate(SUM):
                            dve.wait_ge(found[t].sem, found[t].count)
                            dve.match_replace(left[:, lo:hi], top8[:, t, :], left[:, lo:hi], TAKEN).then_inc(found[t].up(), 1)
                        for t in range(T):
                            dve.wait_ge(found[t].sem, found[t].count)
                    for t, (lo, hi) in enumerate(SUM):
                        dve.tensor_scalar(mask[:, t, 0:hi - lo], left[:, lo:hi], TAKEN / 2, MASKED, ALU.is_gt, ALU.mult)
            attention(KD, lambda m, t: [qT[:, m, t * P:(t + 1) * P]], lambda m: [kT[:, m, :]], lambda m, kt: v_tok[:, kt, m * P:(m + 1) * P], P,
                      lambda m, t: tok(6)[:, t, m * P:(m + 1) * P], (MLA_ROPE + MLA_NOPE) ** -0.5, True, (blk(2), blk(3)))
            transpose_all([(tok(6), xT)])
            project(2, residual=ALPHA, row_src=(d["ln_g"][3], d["ln_b"][3]))
            norm("ln", *ln_cols(3))

        first_attention()
        norm("rms", col("norm_ffn", 0, KD), z=tok(0))
        ffn_stage(FU, 0)
        rwkv()
        norm("rms", col("norm_ffn", KD, KD), z=tok(0))
        ffn_stage(FU, 1, row_src=(d["norm_final"],), ahead=[
            (tok(1), d["mem"].rearrange("(t p) f -> p t f", p=P)), (mask[:], d["chunk_mask"]), (cols[:, 0:LN_COLS], d["ln_cols"]), (posn[:], d["pos"]),
            (inv, d["inv"].rearrange("(o f) -> o f", o=1).broadcast_to([P, 24])),
            (lam.rearrange("p a f -> p (a f)"), d["lam"].rearrange("(o f) -> o f", o=1).broadcast_to([P, 4 * HD]))])
        norm("rms_rows", col("norm_final", 0, KD))
        memory_kv()
        differential()
        cross_attention(0)
        mixture(0, *ln_cols(1))
        sparse_mla()
        cross_attention(1)
        mixture(1, *ln_cols(4), store=out)


def _units(w, width):
    k, n = w.shape
    return w.reshape(k // P, P, n // width, width).transpose(2, 1, 0, 3).reshape(n // width, P, k // P * width)


def _ffn_units(gate, up, down):
    n = gate.shape[1] // (2 * P)
    dn = down.reshape(n, 2, P, D).transpose(0, 2, 1, 3).reshape(n, P, 2 * D)
    return np.concatenate([_units(gate, 2 * P), _units(up, 2 * P), dn], axis=2)


def _features(v):
    return v.reshape(-1, P).T


def _rows(w):
    return w.reshape(-1, P, w.shape[-1]).transpose(1, 0, 2).reshape(P, -1)


def _constants():
    f = np.float32
    pos = np.arange(SEQ, dtype=f)
    e0 = np.arange(0, HD, 2, dtype=f) / f(HD)
    inv0 = f(1) / (10000.0 ** e0.astype(np.float64)).astype(f)
    ang = (pos[:, None] * inv0[None, :]).astype(np.float64)
    c, s = np.cos(ang).astype(f), np.sin(ang).astype(f)

    def by_token(a):
        return np.ascontiguousarray(a.reshape(T, P, -1).transpose(1, 0, 2))

    def inv(rot):
        e = np.arange(0, rot, 2, dtype=f) / f(rot)
        return (500000.0 ** (-e.astype(np.float64))).astype(f)
    i = np.arange(SEQ)
    head = np.arange(D) // HD
    onehot = (head[:, None] == np.arange(HEADS)[None, :]).astype(f)
    s_, t_ = np.arange(CHUNK)[:, None], np.arange(CHUNK)[None, :]
    before, upto = (s_ < t_).astype(f), (s_ <= t_).astype(f)
    return {
        "ident": np.eye(P, dtype=f),
        "causal": by_token(np.where(i[None, :] <= i[:, None], 0, MASKED).astype(f)),
        "chunk_mask": by_token(np.where(i[None, :] // CHUNK <= i[:, None] // CHUNK, 0, MASKED).astype(f)),
        "cos0": by_token(np.concatenate([c, c], 1)), "sin0": by_token(np.concatenate([-s, s], 1)),
        "inv": np.concatenate([inv(DIFF_ROPE), inv(MLA_ROPE)]),
        "spread": np.ascontiguousarray(onehot.T.reshape(HEADS, KD, P)), "heads16": np.ascontiguousarray(onehot.reshape(KD, P, HEADS).transpose(1, 0, 2)),
        "pair": np.ascontiguousarray(onehot[0:P, 0:2]), "reset": np.tile((np.arange(SEQ) % CHUNK != 0).astype(f), (P, 1)),
        "gmask": np.tile(np.concatenate([before, upto], 1), (2, 1)), "lmask": np.tile(before.T, (2, 1)),
        "rank": np.array([4, 3, 2, 1], f),
        "slots": np.concatenate([np.triu(np.ones((P, P), f), 1), np.ones((P, P), f), np.tile(np.arange(1, SLOTS_E + 1, dtype=f), (P, 1))], 1),
    }


def _pack(a):
    cols = np.concatenate([_features(a["norm_mix"]), _features(a["norm_ffn"]), _features(a["rwkv_mu"]), _features(a["rwkv_w0"]), _features(a["rwkv_a0"]),
                           _features(a["rwkv_k_k"]), _features(a["rwkv_k_a"]), _features(a["rwkv_r_k"].reshape(-1)), _features(a["ffn_conv_w"]),
                           _features(a["ffn_conv_b"]), _features(a["a_subln_g_2"]), _features(a["norm_final"]), _features(a["b_q_norm_g_2"]), _features(a["b_kv_norm_g_2"]),
                           *[_rows(np.concatenate([a["moe_w_group_2"][i], a["moe_w_expert_2"][i]], 1)) for i in range(2)]], axis=1)
    rkv = a["rwkv_w_rkv"][0]
    w_proj = np.concatenate([_units(w, COLS) for w in (
        a["attn_w_qkv"][0], a["attn_w_o"][0], rkv[0], rkv[1], rkv[2], a["rwkv_w_o"][0], a["mem_w_kv_2"], a["a_w_in_2"][0], a["a_w_out_2"][0],
        a["xa_w_q_2"][0], a["xa_w_out_2"][0], a["b_w_out_2"][0], a["xa_w_q_2"][1], a["xa_w_out_2"][1])])
    z = np.zeros((P - 64, D), np.float32)
    lora = np.concatenate([_rows(a["rwkv_w1"][0]), _rows(a["rwkv_a1"][0]), _rows(a["rwkv_g1"][0]), np.concatenate([a["rwkv_w2"][0], z]),
                           np.concatenate([a["rwkv_a2"][0], z]), a["rwkv_g2"][0]], axis=1)
    uq = a["b_w_uq_2"][0].reshape(Q_RANK, KD, P)
    uq = np.concatenate([uq[:, :, MLA_ROPE:], uq[:, :, :MLA_ROPE]], 2).reshape(Q_RANK, D)
    uk = a["b_w_uk_2"][0].transpose(1, 0, 2).reshape(KV_RANK, -1)
    uv = a["b_w_uv_2"][0].transpose(1, 0, 2).reshape(KV_RANK, -1)

    moe = np.concatenate([_ffn_units(a["moe_w_gate_2"][l, e], a["moe_w_up_2"][l, e], a["moe_w_down_2"][l, e]) for l in range(2) for e in range(N_EXPERTS)])
    arrays = {
        "x": a["x"][0], "mem": a["mem_2"][0], "pos": a["positions_2"].reshape(T, P).T, "cols": cols, "w_proj": w_proj, "w_lora": lora,
        "w_ffn": np.concatenate([_ffn_units(a["ffn_w_gate"][i], a["ffn_w_up"][i], a["ffn_w_down"][i]) for i in range(2)]), "w_moe": moe,
        "w_b_in": _rows(a["b_w_in_2"][0]), "w_uq": np.concatenate([_rows(uq), _rows(a["b_w_qidx_2"][0])], 1), "w_ukv": np.concatenate([_rows(uk), _rows(uv)], 1),
        "lam": a["a_lambda_2"][0].reshape(-1), "ln_g": a["ln_g_2"].reshape(6, D), "ln_b": a["ln_b_2"].reshape(6, D), "ln_cols": np.concatenate([_features(a["ln_g_2"]), _features(a["ln_b_2"])], 1), "norm_final": a["norm_final"],
        "lnx_w": a["rwkv_lnx_w"][0], "lnx_b": a["rwkv_lnx_b"][0],
        "route_b": np.concatenate([a["moe_b_group_2"], a["moe_b_expert_2"]], 1),
    }
    return {k: np.ascontiguousarray(v) for k, v in arrays.items()} | _constants()


def kernel(**inputs):
    import concourse.bacc as bacc
    from concourse.bass_utils import run_bass_kernel_spmd as run

    arrays = _pack({k: np.asarray(v) for k, v in inputs.items()})
    nc = bacc.Bacc("TRN2", target_bir_lowering=False, num_devices=1)
    d = {n: nc.dram_tensor(f"in_{n}", v.shape, mybir.dt.from_np(v.dtype), kind="ExternalInput").ap() for n, v in arrays.items()}
    out = nc.dram_tensor("out_0", (SEQ, D), F32, kind="ExternalOutput").ap()
    build_program(nc, d, out)
    r = run(nc, [{f"in_{n}": v for n, v in arrays.items()}], core_ids=[0])
    return r.results[0]["out_0"].reshape(1, SEQ, D)
```
